# Optimizing a Trainium2 kernel written in Bass

```python
import math
import jax, jax.numpy as jnp
from jax import lax
import numpy as np

D_MODEL = 1024
BATCH = 1
SEQ = 512
DEPTH = 1
DEC_BATCH = 8
DEC_SEQ = 1
PAST_LEN = 1024
PAGE_SIZE = 128

N_HEADS = 8
HEAD_DIM = 64
N_KV_HEADS = 2
ATT_WIDTH = N_HEADS * HEAD_DIM
IDX_HEADS = 8
IDX_DIM = 64
TOPK_MAX = 256
Q_BLOCK = 128
N_BUCKETS = 32
MAX_EXACT = N_BUCKETS // 2
MAX_DISTANCE = 128
HG_HEADS = 4
HG_DK = 128
HG_DV = 128
HG_KEY_WIDTH = HG_HEADS * HG_DK
HG_VAL_WIDTH = HG_HEADS * HG_DV
HG_CHUNK = 64
PEER_HEADS = 8
PEER_NKEYS = 128
PEER_EXPERTS = PEER_NKEYS * PEER_NKEYS
PEER_DQ = 256
PEER_TOPK = 16
PEER_BLOCK = 256
PLE_DIM = 256
EPS = 1e-6

IN_SPLITS = (ATT_WIDTH, N_KV_HEADS * HEAD_DIM, N_KV_HEADS * HEAD_DIM,
             IDX_HEADS * IDX_DIM, IDX_DIM, IDX_HEADS,
             HG_KEY_WIDTH, HG_KEY_WIDTH, HG_VAL_WIDTH, HG_VAL_WIDTH,
             D_MODEL, D_MODEL)
IN_WIDTH = sum(IN_SPLITS)

kernel_name = 'dsa_hgrn2_peer_hybrid_step'

def rmsnorm(x, g):
    xf = x.astype(jnp.float32)
    y = xf * lax.rsqrt(jnp.mean(xf * xf, axis=-1, keepdims=True) + EPS)
    return (y * g.astype(jnp.float32)).astype(x.dtype)

def rel_bucket(dist):
    n = jnp.maximum(dist, 0)
    nf = jnp.maximum(n, 1).astype(jnp.float32)
    large = MAX_EXACT + (jnp.log(nf / MAX_EXACT) / math.log(MAX_DISTANCE / MAX_EXACT)
                         * (N_BUCKETS - MAX_EXACT)).astype(jnp.int32)
    large = jnp.minimum(large, N_BUCKETS - 1)
    return jnp.where(n < MAX_EXACT, n, large)

rows_gather = jax.vmap(lambda a, i: a[i])

def index_topk(qi, wi, ki, qpos, topk):
    s = jnp.einsum('bqhd,bld->bqhl', qi.astype(jnp.float32), ki.astype(jnp.float32)) * IDX_DIM ** -0.5
    score = jnp.einsum('bqh,bqhl->bql', wi.astype(jnp.float32), jax.nn.relu(s))
    causal = jnp.arange(ki.shape[1], dtype=jnp.int32)[None, :] <= qpos[:, None]
    score = jnp.where(causal[None], score, -jnp.inf)
    _, idx = lax.top_k(score, topk)
    valid = idx <= qpos[None, :, None]
    return idx, valid

def sparse_attend(q, kg, vg, idx, valid, qpos, rel_bias):
    B, Q = q.shape[:2]
    G = N_HEADS // N_KV_HEADS
    qg = q.reshape(B, Q, N_KV_HEADS, G, HEAD_DIM).astype(jnp.float32)
    logits = jnp.einsum('bqcgd,bqncd->bqcgn', qg, kg.astype(jnp.float32)) * HEAD_DIM ** -0.5
    bucket = rel_bucket(qpos[None, :, None] - idx)
    bias = rel_bias.astype(jnp.float32)[bucket]
    bias = bias.reshape(B, Q, -1, N_KV_HEADS, G).transpose(0, 1, 3, 4, 2)
    logits = jnp.where(valid[:, :, None, None, :], logits + bias, -jnp.inf)
    p = jax.nn.softmax(logits, axis=-1)
    o = jnp.einsum('bqcgn,bqncd->bqcgd', p, vg.astype(jnp.float32))
    return o.reshape(B, Q, ATT_WIDTH).astype(q.dtype)

def attn_prompt(q, k, v, qi, ki, wi, rel_bias):
    B, T = q.shape[:2]
    topk = min(TOPK_MAX, T // 4)
    nb = T // Q_BLOCK

    def blk(a):
        return a.reshape((B, nb, Q_BLOCK) + a.shape[2:]).swapaxes(0, 1)

    qpos = jnp.arange(T, dtype=jnp.int32).reshape(nb, Q_BLOCK)

    def one(args):
        qb, qib, wib, pos = args
        idx, valid = index_topk(qib, wib, ki, pos, topk)
        kg = rows_gather(k, idx)
        vg = rows_gather(v, idx)
        return sparse_attend(qb, kg, vg, idx, valid, pos, rel_bias)

    out = lax.map(one, (blk(q), blk(qi), blk(wi), qpos))
    return out.swapaxes(0, 1).reshape(B, T, ATT_WIDTH)

def attn_sample(q, k_new, v_new, qi, ki_new, wi, cache_k, cache_v, cache_kidx, page_table, rel_bias):
    DB, T = q.shape[:2]
    past = page_table.shape[1] * PAGE_SIZE
    topk = min(TOPK_MAX, (past + T) // 4)
    ki_past = cache_kidx[page_table].reshape(DB, past, IDX_DIM)
    ki_all = jnp.concatenate([ki_past.astype(ki_new.dtype), ki_new], axis=1)
    qpos = past + jnp.arange(T, dtype=jnp.int32)
    idx, valid = index_topk(qi, wi, ki_all, qpos, topk)
    is_past = (idx < past)[..., None, None]
    pidx = jnp.minimum(idx, past - 1)
    phys = rows_gather(page_table, pidx // PAGE_SIZE)
    off = pidx % PAGE_SIZE
    nidx = jnp.clip(idx - past, 0, T - 1)
    kg = jnp.where(is_past, cache_k[phys, off].astype(k_new.dtype), rows_gather(k_new, nidx))
    vg = jnp.where(is_past, cache_v[phys, off].astype(v_new.dtype), rows_gather(v_new, nidx))
    return sparse_attend(q, kg, vg, idx, valid, qpos, rel_bias)

def hgrn2_scan(q, k, v, logf, S0, chunk):
    B, T, H, DK = q.shape
    DV = v.shape[-1]
    n = T // chunk

    def blk(a):
        return a.reshape((B, n, chunk) + a.shape[2:]).swapaxes(0, 1)

    tri = jnp.tril(jnp.ones((chunk, chunk), dtype=bool))

    def step(S, args):
        qc, kc, vc, lf = args
        b = jnp.cumsum(lf, axis=1)
        rel = b[:, :, None] - b[:, None, :]
        decay = jnp.exp(jnp.where(tri[None, :, :, None, None], rel, -jnp.inf))
        A = jnp.einsum('bthd,btshd,bshd->bhts', qc, decay, kc)
        o = (jnp.einsum('bhts,bshv->bthv', A, vc)
             + jnp.einsum('bthd,bhdv->bthv', qc * jnp.exp(b), S))
        bl = b[:, -1]
        S = (jnp.exp(bl)[..., None] * S
             + jnp.einsum('bshd,bshv->bhdv', kc * jnp.exp(bl[:, None] - b), vc))
        return S, o

    S, o = lax.scan(step, S0, (blk(q), blk(k), blk(v), blk(logf)))
    return o.swapaxes(0, 1).reshape(B, T, H, DV), S

def hgrn2_branch(hq, hf, hi, hg, lb, g_hgrn, S0):
    B, T = hq.shape[:2]
    f32 = jnp.float32
    lbh = lb.reshape(HG_HEADS, HG_DK)
    q = hq.reshape(B, T, HG_HEADS, HG_DK).astype(f32)
    f = lbh + (1.0 - lbh) * jax.nn.sigmoid(hf.reshape(B, T, HG_HEADS, HG_DK).astype(f32))
    v = hi.reshape(B, T, HG_HEADS, HG_DV).astype(f32)
    chunk = math.gcd(T, HG_CHUNK)
    o, S = hgrn2_scan(q, 1.0 - f, v, jnp.log(f), S0, chunk)
    o = rmsnorm(o, g_hgrn).reshape(B, T, HG_VAL_WIDTH)
    return (o * jax.nn.silu(hg.astype(f32))).astype(hq.dtype), S

def peer(x, wq, subkeys, u, v):
    N = x.shape[0]
    pad = (-N) % PEER_BLOCK
    xp = jnp.pad(x, ((0, pad), (0, 0))).reshape(-1, PEER_BLOCK, D_MODEL)
    f32 = jnp.float32

    def one(xb):
        qh = (xb @ wq).reshape(PEER_BLOCK, PEER_HEADS, 2, PEER_DQ // 2).astype(f32)
        s1 = jnp.einsum('nhd,kd->nhk', qh[:, :, 0], subkeys[0].astype(f32))
        s2 = jnp.einsum('nhd,kd->nhk', qh[:, :, 1], subkeys[1].astype(f32))
        v1, i1 = lax.top_k(s1, PEER_TOPK)
        v2, i2 = lax.top_k(s2, PEER_TOPK)
        cand = (v1[..., :, None] + v2[..., None, :]).reshape(PEER_BLOCK, PEER_HEADS, PEER_TOPK * PEER_TOPK)
        sc, ci = lax.top_k(cand, PEER_TOPK)
        e = (jnp.take_along_axis(i1, ci // PEER_TOPK, axis=-1) * PEER_NKEYS
             + jnp.take_along_axis(i2, ci % PEER_TOPK, axis=-1))
        g = jax.nn.softmax(sc, axis=-1)
        ue = u[e]
        ve = v[e]
        a = jax.nn.gelu(jnp.einsum('nd,nhkd->nhk', xb, ue, preferred_element_type=f32), approximate=False)
        return jnp.einsum('nhk,nhkd->nd', (g * a).astype(x.dtype), ve).astype(x.dtype)

    return lax.map(one, xp).reshape(-1, D_MODEL)[:N]

def decoder_layer(x, p, S0, attn_fn, lb, g_mix, w_in, w_branch_a, w_branch_b, w_out, g_hgrn,
                  g_ffn, peer_wq, peer_subkeys, peer_u, peer_v, g_ple, w_ple_gate, w_ple_proj):
    B, T, _ = x.shape
    h = rmsnorm(x, g_mix)
    offs = np.cumsum(IN_SPLITS)[:-1].tolist()
    aq, ak, av, iq, ik, iw, hq, hf, hi, hg, za, zb = jnp.split(h @ w_in, offs, axis=-1)
    q = aq.reshape(B, T, N_HEADS, HEAD_DIM)
    k = ak.reshape(B, T, N_KV_HEADS, HEAD_DIM)
    v = av.reshape(B, T, N_KV_HEADS, HEAD_DIM)
    qi = iq.reshape(B, T, IDX_HEADS, IDX_DIM)
    wi = iw * IDX_HEADS ** -0.5
    att = attn_fn(q, k, v, qi, ik, wi)
    hgo, S = hgrn2_branch(hq, hf, hi, hg, lb, g_hgrn, S0)
    mix = jax.nn.sigmoid(za) * (att @ w_branch_a) + jax.nn.sigmoid(zb) * (hgo @ w_branch_b)
    x = x + mix @ w_out
    x = x + peer(rmsnorm(x, g_ffn).reshape(B * T, D_MODEL), peer_wq, peer_subkeys, peer_u, peer_v).reshape(B, T, D_MODEL)
    x = x + jax.nn.sigmoid(rmsnorm(x, g_ple) @ w_ple_gate) * (p @ w_ple_proj)
    return x, k, v, ik, S

def setup_inputs(seed: int = 0) -> dict:
    key = jax.random.key(seed)
    ks = jax.random.split(key, 32)
    f32 = jnp.float32
    n_pages = PAST_LEN // PAGE_SIZE
    n_used = DEC_BATCH * n_pages
    n_phys = n_used + max(1, n_used // 4)

    def nrm(k, shape, scale=1.0):
        return jax.random.normal(k, shape, f32) * scale

    def gain(k, shape):
        return 1.0 + 0.1 * jax.random.normal(k, shape, f32)

    page_table = jax.random.permutation(ks[0], n_phys)[:n_used].reshape(DEC_BATCH, n_pages).astype(jnp.int32)
    return {
        'x_prompt': nrm(ks[1], (BATCH, SEQ, D_MODEL)),
        'x_sample': nrm(ks[2], (DEC_BATCH, DEC_SEQ, D_MODEL)),
        'cache_k': nrm(ks[3], (DEPTH, n_phys, PAGE_SIZE, N_KV_HEADS, HEAD_DIM)),
        'cache_v': nrm(ks[4], (DEPTH, n_phys, PAGE_SIZE, N_KV_HEADS, HEAD_DIM)),
        'cache_kidx': nrm(ks[5], (DEPTH, n_phys, PAGE_SIZE, IDX_DIM)),
        'state_hgrn': nrm(ks[6], (DEPTH, DEC_BATCH, HG_HEADS, HG_DK, HG_DV), 0.5),
        'page_table': page_table,
        'p_prompt': nrm(ks[7], (DEPTH, BATCH, SEQ, PLE_DIM)),
        'p_sample': nrm(ks[8], (DEPTH, DEC_BATCH, DEC_SEQ, PLE_DIM)),
        'g_mix': gain(ks[9], (DEPTH, D_MODEL)),
        'w_in': nrm(ks[10], (DEPTH, D_MODEL, IN_WIDTH), D_MODEL ** -0.5),
        'w_branch_a': nrm(ks[11], (DEPTH, ATT_WIDTH, D_MODEL), ATT_WIDTH ** -0.5),
        'w_branch_b': nrm(ks[12], (DEPTH, HG_VAL_WIDTH, D_MODEL), HG_VAL_WIDTH ** -0.5),
        'w_out': nrm(ks[13], (DEPTH, D_MODEL, D_MODEL), D_MODEL ** -0.5),
        'g_hgrn': gain(ks[14], (DEPTH, HG_DV)),
        'lb_logits': nrm(ks[15], (DEPTH + 1, HG_KEY_WIDTH), 0.5),
        'rel_bias': nrm(ks[16], (N_BUCKETS, N_HEADS), 0.5),
        'g_ffn': gain(ks[17], (DEPTH, D_MODEL)),
        'peer_wq': nrm(ks[18], (DEPTH, D_MODEL, PEER_HEADS * PEER_DQ), D_MODEL ** -0.5),
        'peer_subkeys': nrm(ks[19], (DEPTH, 2, PEER_NKEYS, PEER_DQ // 2), (PEER_DQ // 2) ** -0.5),
        'peer_u': nrm(ks[20], (DEPTH, PEER_EXPERTS, D_MODEL), D_MODEL ** -0.5),
        'peer_v': nrm(ks[21], (DEPTH, PEER_EXPERTS, D_MODEL), PEER_HEADS ** -0.5),
        'g_ple': gain(ks[22], (DEPTH, D_MODEL)),
        'w_ple_gate': nrm(ks[23], (DEPTH, D_MODEL, D_MODEL), D_MODEL ** -0.5),
        'w_ple_proj': nrm(ks[24], (DEPTH, PLE_DIM, D_MODEL), PLE_DIM ** -0.5),
        'g_final': gain(ks[25], (D_MODEL,)),
    }

def reference(x_prompt, x_sample, cache_k, cache_v, cache_kidx, state_hgrn, page_table, p_prompt, p_sample,
              g_mix, w_in, w_branch_a, w_branch_b, w_out, g_hgrn, lb_logits, rel_bias, g_ffn,
              peer_wq, peer_subkeys, peer_u, peer_v, g_ple, w_ple_gate, w_ple_proj, g_final):
    lb_all = jnp.cumsum(jax.nn.softmax(lb_logits.astype(jnp.float32), axis=0), axis=0)
    xp, xs = x_prompt, x_sample
    kp_l, vp_l, kip_l, sp_l = [], [], [], []
    ks_l, vs_l, kis_l, ss_l = [], [], [], []
    for i in range(DEPTH):
        lw = (g_mix[i], w_in[i], w_branch_a[i], w_branch_b[i], w_out[i], g_hgrn[i], g_ffn[i],
              peer_wq[i], peer_subkeys[i], peer_u[i], peer_v[i], g_ple[i], w_ple_gate[i], w_ple_proj[i])
        attn_p = lambda q, k, v, qi, ki, wi: attn_prompt(q, k, v, qi, ki, wi, rel_bias)
        attn_s = lambda q, k, v, qi, ki, wi: attn_sample(q, k, v, qi, ki, wi, cache_k[i], cache_v[i],
                                                         cache_kidx[i], page_table, rel_bias)
        S0p = jnp.zeros((xp.shape[0], HG_HEADS, HG_DK, HG_DV), jnp.float32)
        xp, kp, vp, kip, Sp = decoder_layer(xp, p_prompt[i], S0p, attn_p, lb_all[i], *lw)
        xs, kss, vss, kis, Ss = decoder_layer(xs, p_sample[i], state_hgrn[i].astype(jnp.float32), attn_s, lb_all[i], *lw)
        kp_l.append(kp); vp_l.append(vp); kip_l.append(kip); sp_l.append(Sp.astype(state_hgrn.dtype))
        ks_l.append(kss); vs_l.append(vss); kis_l.append(kis); ss_l.append(Ss.astype(state_hgrn.dtype))
    y_prompt = rmsnorm(xp, g_final)
    y_sample = rmsnorm(xs, g_final)
    return (y_prompt, y_sample, jnp.stack(kp_l), jnp.stack(vp_l), jnp.stack(kip_l), jnp.stack(sp_l),
            jnp.stack(ks_l), jnp.stack(vs_l), jnp.stack(kis_l), jnp.stack(ss_l))


_drawn_inputs = setup_inputs


def setup_inputs(seed=0):
    import zlib

    import numpy as np

    out = dict(_drawn_inputs(seed))
    spreads = {}
    factors = {'g_ple': 3.216}
    for name, (base, spread) in spreads.items():
        noise = np.random.default_rng([zlib.crc32(name.encode()), seed]).standard_normal(out[name].shape)
        drawn = base * np.exp(spread * noise) if base else spread * noise
        out[name] = __import__('jax').numpy.asarray(drawn.astype(out[name].dtype))
    for name, factor in factors.items():
        out[name] = (out[name] * factor).astype(out[name].dtype)
    return out
```

```python
from contextlib import ExitStack
import math

import numpy as np
import concourse.bass as bass
from concourse import mybir

F32 = mybir.dt.float32
U32 = mybir.dt.uint32
I32 = mybir.dt.int32
ALU = mybir.AluOpType
ACT = mybir.ActivationFunctionType
X = mybir.AxisListType.X

P = 128
D = 1024
DC = D // P
TP = 512
NT = TP // P
TS = 8
N = TP + TS
HALF = N // 2
HD = 64
NH = 8
NQ = NH * HD // P
HG = 4
CH = 32
NCH = TP // CH
PAST = 1024
PG = 128
NPG = PAST // PG
L = PAST + 1
TOPP = min(256, TP // 4)
TOPS = min(256, L // 4)
SK = TP + P
REV = PAST + P
NB = 32
PH = 8
PK = 16
SLOT = PH * PK
E1 = 128
SENT = -3.0e38
LOW = -1.0e38
OFF = -1.0e30
EPS = 1e-6
AQ, AK, IQ, HQ, HGT, HF, ZA, ZB, MT = 0, 4, 5, 9, 13, 17, 21, 29, 37
TB = 130
NBLK = N // TB


def halves(ap):
    return ap.rearrange("p (j n) -> p j n", j=2)


class Alloc:

    def __init__(self, nc, ctx):
        self.nc, self.ctx = nc, ctx

    def sb(self, name, shape, dt=F32):
        return self.ctx.enter_context(self.nc.sbuf_tensor(name, shape, dt))

    def ps(self, name, shape):
        return self.ctx.enter_context(self.nc.psum_tensor(name, shape, F32))

    def sem(self, name):
        return self.nc.alloc_semaphore(name)


class Chain:

    def __init__(self, eng, sem):
        self.eng, self.sem, self.n = eng, sem, 0

    def __call__(self, ins):
        self.n += 1
        ins.then_inc(self.sem, 1)
        self.eng.wait_ge(self.sem, self.n)


def rms_block(nc, turn, sems, src, dst, gain, ones, eps):
    s_sq, s_ms, s_rt, s_rs, s_h = sems
    with ExitStack() as ctx:
        a = Alloc(nc, ctx)
        sq = a.sb(f"rms{turn}_sq", [P, DC, N])
        rt = a.sb(f"rms{turn}_rt", [P, N])
        rs = a.sb(f"rms{turn}_rs", [P, N])
        pm = a.ps(f"rms{turn}_pm", [P, 2, 512])
        block = ctx.enter_context(nc.Block())

        @block.scalar
        def _(act):
            for c in range(DC):
                nc.scalar.activation(sq[:, c, :], src[:, c, :], ACT.Square).then_inc(s_sq, 1)
            act.wait_ge(s_ms, turn + 1)
            nc.scalar.activation(halves(rt[:, :]), pm[:, :, 0:HALF], ACT.Sqrt, scale=1.0 / D,
                                 bias=eps[:, 0:1]).then_inc(s_rt, 1)

        @block.tensor
        def _(pe):
            for c in range(DC):
                pe.wait_ge(s_sq, turn * DC + c + 1)
                for j in range(2):
                    last = nc.tensor.matmul(pm[:, j, 0:HALF], ones[:, :], sq[:, c, j * HALF:(j + 1) * HALF],
                                            start=(c == 0), stop=(c == DC - 1))
            last.then_inc(s_ms, 1)

        @block.vector
        def _(dve):
            dve.wait_ge(s_rt, turn + 1)
            nc.vector.reciprocal(rs[:, :], rt[:, :]).then_inc(s_rs, 1)
            dve.wait_ge(s_rs, turn + 1)
            for c in range(DC):
                nc.vector.scalar_tensor_tensor(out=dst[:, c, :], in0=src[:, c, :], scalar=gain[:, c:c + 1],
                                               in1=rs[:, :], op0=ALU.mult, op1=ALU.mult).then_inc(s_h, 1)
            dve.wait_ge(s_h, (turn + 1) * DC)


def constants(nc, a, I, c):
    s_c, s_c2, s_d = a.sem("const_made"), a.sem("bias_row_set"), a.sem("const_loaded")
    with nc.Block() as block:
        @block.gpsimd
        def _(pool):
            link = Chain(pool, s_c)
            link(nc.gpsimd.memset(c.ones[:, :], 1.0))
            link(nc.gpsimd.memset(c.eps[:, :], EPS))
            link(nc.gpsimd.memset(c.ident[:, :], 0.0))
            link(nc.gpsimd.affine_select(out=c.ident[:, :], in_=c.ident[:, :], compare_op=ALU.not_equal,
                                         fill=1.0, base=0, pattern=[[-1, P]], channel_multiplier=1))
            link(nc.gpsimd.memset(c.causal[:, :], 0.0))
            link(nc.gpsimd.affine_select(out=c.causal[:, :], in_=c.causal[:, :], compare_op=ALU.is_ge,
                                         fill=LOW, base=0, pattern=[[-1, P]], channel_multiplier=1))
            link(nc.gpsimd.memset(c.tri[:, :], 1.0))
            link(nc.gpsimd.affine_select(out=c.tri[:, :], in_=c.tri[:, :], compare_op=ALU.is_ge,
                                         fill=0.0, base=0, pattern=[[1, P]], channel_multiplier=-1))
            for k in range(P // CH):
                v = c.tri[:, k * CH:(k + 1) * CH]
                link(nc.gpsimd.affine_select(out=v, in_=v, compare_op=ALU.is_ge, fill=0.0, base=-k * CH,
                                             pattern=[[0, CH]], channel_multiplier=1))
            link(nc.gpsimd.memset(c.reset[:, :], 1.0))
            link(nc.gpsimd.memset(c.reset[:, :].rearrange("p (c k) -> p c k", k=CH)[:, :, 0:1], 0.0))
            for t in (c.sel_b, c.sel_h):
                link(nc.gpsimd.memset(t[:, :, :], 0.0))
            link(nc.gpsimd.affine_select(out=c.sel_b[:, :, :], in_=c.sel_b[:, :, :], compare_op=ALU.not_equal,
                                         fill=1.0, base=0, pattern=[[-1, 8], [0, 8]], channel_multiplier=1))
            link(nc.gpsimd.affine_select(out=c.sel_h[:, :, :], in_=c.sel_h[:, :, :], compare_op=ALU.not_equal,
                                         fill=1.0, base=0, pattern=[[0, 8], [-1, 8]], channel_multiplier=1))
            link(nc.gpsimd.memset(c.pick[:, :, :], 0.0))
            link(nc.gpsimd.affine_select(out=c.pick[:, :, :], in_=c.pick[:, :, :], compare_op=ALU.not_equal,
                                         fill=1.0, base=0, pattern=[[-1, 8], [0, P]], channel_multiplier=1))
            link(nc.gpsimd.memset(c.selT[:, :], 1.0))
            link(nc.gpsimd.affine_select(out=c.selT[:, :], in_=c.selT[:, :], compare_op=ALU.is_ge, fill=0.0,
                                         base=0, pattern=[[-NH, TS]], channel_multiplier=1))
            link(nc.gpsimd.affine_select(out=c.selT[:, :], in_=c.selT[:, :], compare_op=ALU.is_ge, fill=0.0,
                                         base=NH - 1, pattern=[[NH, TS]], channel_multiplier=-1))
            link(nc.gpsimd.iota(c.iota[:, :], pattern=[[1, P]], base=0, channel_multiplier=0,
                                allow_small_or_imprecise_dtypes=True))

        @block.sync
        def _(sp):
            sp.dma_start(c.x[:, :, :], I["xT"]).then_inc(s_d, 16)
            for k in ("g_mix", "g_ffn", "g_ple", "g_final", "g_hgrn", "lbl", "pages"):
                sp.dma_start(c.small[k][:, :, :] if k == "lbl" else c.small[k][:, :], I[k]).then_inc(s_d, 16)
            sp.dma_start(c.rb[0:NB, :], I["rel_bias"]).then_inc(s_d, 16)
            sp.wait_ge(s_d, 144)

        @block.vector
        def _(dve):
            nc.vector.memset(c.rb[NB:NB + 1, :], OFF).then_inc(s_c2, 1)
            dve.wait_ge(s_c2, 1)


def project(nc, I, O, c, h, proj, ikT, vtok, hitok, iwtok):
    RING = 4
    with ExitStack() as ctx:
        a = Alloc(nc, ctx)
        ring = a.sb("w_ring", [P, RING, DC, P])
        wtok = a.sb("w_tok", [P, DC, 648])
        wik = a.sb("w_ik", [P, DC, HD])
        pp = a.ps("proj_ps", [P, 2, 2, 512])
        pt = a.ps("tok_ps", [P, 2, 2, 512])
        s_w = [a.sem(f"w_loaded{r}") for r in range(RING)]
        s_wt, s_wi = a.sem("wtok_loaded"), a.sem("wik_loaded")
        s_pt, s_ct = a.sem("tok_product"), a.sem("tok_copied")
        s_pp, s_cp = a.sem("tile_product"), a.sem("tile_copied")
        s_ik, s_ikc, s_o = a.sem("ik_product"), a.sem("ik_copied"), a.sem("kv_stored")
        block = ctx.enter_context(nc.Block())
        TT = NT + 1

        @block.sync
        def _(sp):
            sp.dma_start(wtok[:, :, :], I["w_tok"]).then_inc(s_wt, 16)
            for r in range(RING):
                sp.dma_start(ring[:, r], I["w_t"][r]).then_inc(s_w[r], 16)
            sp.dma_start(wik[:, :, :], I["w_ik"]).then_inc(s_wi, 16)
            with sp.Fori(1, MT // RING) as i:
                for r in range(RING):
                    sp.wait_ge(s_pp, (i - 1) * RING + r + 1)
                    sp.dma_start(ring[:, r], I["w_t"][i * RING + r]).then_inc(s_w[r], 16)
            sp.wait_ge(s_pp, MT - RING)
            sp.dma_start(ring[:, 0], I["w_t"][MT - 1]).then_inc(s_w[0], 16)
            sp.wait_ge(s_ct, 2 * TT)
            sp.dma_start(O["v_p"].rearrange("(t p) n -> p t n", p=P), vtok[:, 0:NT, :]).then_inc(s_o, 16)
            sp.dma_start(O["v_s"], vtok[0:TS, NT, :]).then_inc(s_o, 16)
            sp.wait_ge(s_cp, MT)
            sp.dma_start(O["kT"], proj[:, AK, :]).then_inc(s_o, 16)
            sp.wait_ge(s_ikc, 2)
            sp.dma_start(O["ikT"], ikT[0:HD, :]).then_inc(s_o, 16)
            sp.wait_ge(s_o, 64)

        @block.tensor
        def _(pe):
            pe.wait_ge(s_wt, 16)
            for t in range(TT):
                m = P if t < NT else TS
                if t >= 2:
                    pe.wait_ge(s_ct, 2 * (t - 1))
                for c0, c1, j in ((0, 324, 0), (324, 648, 1)):
                    for k in range(DC):
                        last = nc.tensor.matmul(pt[0:m, t % 2, j, 0:324], h[:, k, t * P:t * P + m],
                                                wtok[:, k, c0:c1], start=(k == 0), stop=(k == DC - 1))
                last.then_inc(s_pt, 1)

            def tile(r, done, base):
                pe.wait_ge(s_w[r], done)
                pe.wait_ge(s_cp, base)
                for j in range(2):
                    for k in range(DC):
                        last = nc.tensor.matmul(pp[:, r % 2, j, 0:HALF], ring[:, r, k, :],
                                                h[:, k, j * HALF:(j + 1) * HALF],
                                                start=(k == 0), stop=(k == DC - 1))
                last.then_inc(s_pp, 1)

            for r in range(RING):
                tile(r, 16, max(0, r - 1))
            with pe.Fori(1, MT // RING) as i:
                for r in range(RING):
                    tile(r, i * 16 + 16, i * RING + r - 1)
            tile(0, 16 * (MT // RING + 1), MT - 2)
            pe.wait_ge(s_wi, 16)
            pe.wait_ge(s_cp, MT - 1)
            for j in range(2):
                for k in range(DC):
                    last = nc.tensor.matmul(pp[0:HD, 1, j, 0:HALF], wik[:, k, :], h[:, k, j * HALF:(j + 1) * HALF],
                                            start=(k == 0), stop=(k == DC - 1))
            last.then_inc(s_ik, 1)

        @block.vector
        def _(dve):
            for t in range(TT):
                m = P if t < NT else TS
                dve.wait_ge(s_pt, t + 1)
                nc.vector.tensor_copy(vtok[0:m, t, :], pt[0:m, t % 2, 0, 0:P])
                nc.vector.tensor_copy(hitok[0:m, t, 0:196], pt[0:m, t % 2, 0, P:324]).then_inc(s_ct, 1)
                nc.vector.tensor_copy(hitok[0:m, t, 196:512], pt[0:m, t % 2, 1, 0:316])
                nc.vector.tensor_scalar(iwtok[0:m, t, :], pt[0:m, t % 2, 1, 316:324], NH ** -0.5, None,
                                        ALU.mult).then_inc(s_ct, 1)
            dve.wait_ge(s_ik, 1)
            nc.vector.tensor_copy(halves(ikT[0:HD, :]), pp[0:HD, 1, :, 0:HALF]).then_inc(s_ikc, 1)
            nc.vector.tensor_copy(halves(ikT[HD:P, :]), pp[0:HD, 1, :, 0:HALF]).then_inc(s_ikc, 1)

        @block.scalar
        def _(act):
            def evacuate(m, r, func):
                act.wait_ge(s_pp, m + 1)
                nc.scalar.activation(halves(proj[:, m, :]), pp[:, r, :, 0:HALF], func).then_inc(s_cp, 1)

            with act.Fori(0, (HF - 1) // 2) as i:
                for r in range(2):
                    evacuate(i * 2 + r, r, ACT.Identity)
            evacuate(HF - 1, 0, ACT.Identity)
            with act.Fori(0, (MT - HF) // 2) as i:
                for r in range(2):
                    evacuate(i * 2 + HF + r, (HF + r) % 2, ACT.Sigmoid)


def index_prompt(nc, c, proj, ikT, iwtok, maskp):
    with ExitStack() as ctx:
        a = Alloc(nc, ctx)
        ps = a.ps("ix_ps", [P, 4, 512])
        rl = a.sb("ix_relu", [P, 4, TP])
        sc = a.sb("ix_score", [P, 2, TP])
        wk = a.sb("ix_work", [P, TP])
        m8 = a.sb("ix_max8", [P, 8])
        s_ps, s_rl, s_ac, s_v = (a.sem("ix_" + x) for x in ("product", "relu", "accumulated", "chain"))
        block = ctx.enter_context(nc.Block())

        @block.tensor
        def _(pe):
            n = 0
            for t in range(1, NT):
                S = (t + 1) * P
                for h in range(NH):
                    r = HD * (h % 2)
                    if n >= 4:
                        pe.wait_ge(s_rl, n - 3)
                    nc.tensor.matmul(ps[:, n % 4, 0:S], proj[r:r + HD, IQ + h // 2, t * P:(t + 1) * P],
                                     ikT[r:r + HD, 0:S], start=True, stop=True).then_inc(s_ps, 1)
                    n += 1

        @block.scalar
        def _(act):
            n = 0
            for t in range(1, NT):
                S = (t + 1) * P
                for h in range(NH):
                    act.wait_ge(s_ps, n + 1)
                    if n >= 4:
                        act.wait_ge(s_ac, n - 3)
                    nc.scalar.activation(rl[:, n % 4, 0:S], ps[:, n % 4, 0:S], ACT.Relu,
                                         scale=HD ** -0.5).then_inc(s_rl, 1)
                    n += 1

        @block.vector
        def _(dve):
            link = Chain(dve, s_v)
            nc.vector.memset(maskp[:, 0, :], 0.0)
            n = 0
            for t in range(1, NT):
                S = (t + 1) * P
                for h in range(NH):
                    dve.wait_ge(s_rl, n + 1)
                    if h == 0:
                        ins = nc.vector.tensor_scalar(sc[:, 0, 0:S], rl[:, n % 4, 0:S], iwtok[:, t, 0:1], None,
                                                      ALU.mult)
                    else:
                        ins = nc.vector.scalar_tensor_tensor(out=sc[:, h % 2, 0:S], in0=rl[:, n % 4, 0:S],
                                                             scalar=iwtok[:, t, h:h + 1],
                                                             in1=sc[:, (h - 1) % 2, 0:S],
                                                             op0=ALU.mult, op1=ALU.add)
                    n += 1
                    ins.then_inc(s_ac, 1)
                    dve.wait_ge(s_ac, n)
                f = sc[:, 1, :]
                link(nc.vector.tensor_tensor(f[:, t * P:S], f[:, t * P:S], c.causal[:, :], ALU.add))
                for k in range(TOPP // 8):
                    src = f if k == 0 else wk
                    link(nc.vector.max(m8[:, :], src[:, 0:S]))
                    link(nc.vector.match_replace(wk[:, 0:S], m8[:, :], src[:, 0:S], SENT))
                link(nc.vector.tensor_scalar(maskp[:, t, 0:S], wk[:, 0:S], SENT, OFF, ALU.not_equal, ALU.mult))


def bias_table(nc, c, onehot, rev, scratch, toep):
    with ExitStack() as ctx:
        a = Alloc(nc, ctx)
        pb = a.ps("bias_ps", [P, 3, 512])
        oh = a.sb("bias_onehot", [NB + 1, REV])
        s_h = a.sem("bias_onehot_loaded")
        s_p, s_c, s_o, s_i = (a.sem("bias_" + x) for x in ("product", "copied", "stored", "loaded"))
        block = ctx.enter_context(nc.Block())
        W = REV // 3

        @block.tensor
        def _(pe):
            pe.wait_ge(s_h, 16)
            for j in range(3):
                last = nc.tensor.matmul(pb[0:NH, j, 0:W], c.rb[:, :], oh[:, j * W:(j + 1) * W],
                                        start=True, stop=True)
            last.then_inc(s_p, 1)

        @block.vector
        def _(dve):
            dve.wait_ge(s_p, 1)
            nc.vector.tensor_copy(rev[:, :].rearrange("h (j w) -> h j w", j=3), pb[0:NH, :, 0:W]).then_inc(s_c, 1)

        @block.sync
        def _(sp):
            sp.dma_start(oh[:, :], onehot).then_inc(s_h, 16)
            sp.wait_ge(s_c, 1)
            sp.dma_start(scratch[:, :, 0:SK - 1],
                         rev[:, REV - SK + 1:REV].unsqueeze(1).to_broadcast([NH, P, SK - 1])).then_inc(s_o, 16)
            sp.wait_ge(s_o, 16)
            src = bass.AP(tensor=scratch.tensor, offset=P - 1, ap=[[SK - 1, P], [P * SK, NH], [1, TP]])
            sp.dma_start(toep[:, :, :], src).then_inc(s_i, 16)
            sp.wait_ge(s_i, 16)


def attend_prompt(nc, c, proj, vtok, maskp, toep, attT):
    with ExitStack() as ctx:
        a = Alloc(nc, ctx)
        pl = a.ps("at_logit_ps", [P, 2, 512])
        px = a.ps("at_turn_ps", [P, 2, 512])
        po = a.ps("at_out_ps", [P, 2, 512])
        pa = a.ps("at_att_ps", [P, 1, 512])
        lg = a.sb("at_logit", [P, 2, TP])
        lm = a.sb("at_masked", [P, 2, TP])
        pr = a.sb("at_prob", [P, 2, TP])
        pT = a.sb("at_probT", [P, 2, TP])
        mx = a.sb("at_max", [P, NT, NH])
        nm = a.sb("at_negmax", [P, NT, NH])
        sm = a.sb("at_sum", [P, NT, NH])
        rc = a.sb("at_recip", [P, NT, NH])
        at = a.sb("at_att", [P, 2, 512])
        s_l, s_b, s_m, s_n, s_e, s_x, s_c, s_o, s_r, s_a, s_t, s_f = (a.sem("at_" + x) for x in (
            "product", "biased", "masked", "negmax_made", "exp", "turned", "turn_copied", "pv", "recip_made",
            "normalised", "att_turned", "att_copied"))
        block = ctx.enter_context(nc.Block())
        work = [(t, m, g) for t in range(NT) for m in range(4) for g in range(2)]

        @block.tensor
        def _(pe):
            def logits(n):
                t, m, g = work[n]
                S = (t + 1) * P
                if n >= 2:
                    pe.wait_ge(s_b, n - 1)
                nc.tensor.matmul(pl[:, n % 2, 0:S], proj[HD * g:HD * g + HD, AQ + m, t * P:S],
                                 proj[HD * g:HD * g + HD, AK, 0:S], start=True, stop=True).then_inc(s_l, 1)

            def turn(n):
                t, m, g = work[n]
                pe.wait_ge(s_e, n + 1)
                if n >= 2:
                    pe.wait_ge(s_c, n - 1)
                for k in range(t + 1):
                    last = nc.tensor.transpose(px[:, n % 2, k * P:(k + 1) * P], pr[:, n % 2, k * P:(k + 1) * P],
                                               c.ident[:, :])
                last.then_inc(s_x, 1)

            def pv(n):
                t, m, g = work[n]
                pe.wait_ge(s_c, n + 1)
                if n % 8 == 0 and t >= 2:
                    pe.wait_ge(s_a, t - 1)
                o = (2 * m + g) * HD
                for k in range(t + 1):
                    last = nc.tensor.matmul(po[:, t % 2, o:o + HD], pT[:, n % 2, k * P:(k + 1) * P],
                                            vtok[:, k, g * HD:g * HD + HD], start=(k == 0), stop=(k == t))
                last.then_inc(s_o, 1)

            def att(t):
                pe.wait_ge(s_a, t + 1)
                if t >= 1:
                    pe.wait_ge(s_f, t)
                for m in range(4):
                    last = nc.tensor.transpose(pa[:, 0, m * P:(m + 1) * P], at[:, t % 2, m * P:(m + 1) * P],
                                               c.ident[:, :])
                last.then_inc(s_t, 1)

            logits(0)
            for n in range(len(work)):
                if n + 1 < len(work):
                    logits(n + 1)
                turn(n)
                pv(n)
                if n % 8 == 7:
                    att(n // 8)

        @block.vector
        def _(dve):
            def score(n):
                t, m, g = work[n]
                S = (t + 1) * P
                h = m + 4 * g
                u = TP - S
                dve.wait_ge(s_l, n + 1)
                nc.vector.scalar_tensor_tensor(out=lg[:, n % 2, 0:S], in0=pl[:, n % 2, 0:S], scalar=HD ** -0.5,
                                               in1=toep[:, h, u:TP], op0=ALU.mult, op1=ALU.add).then_inc(s_b, 1)
                dve.wait_ge(s_b, n + 1)
                if n >= 2:
                    dve.wait_ge(s_e, n - 1)
                nc.vector.tensor_tensor_reduce(out=lm[:, n % 2, 0:S], in0=lg[:, n % 2, 0:S],
                                               in1=maskp[:, t, 0:S], scale=1.0, scalar=-3.0e38, op0=ALU.add,
                                               op1=ALU.max, accum_out=mx[:, t, h:h + 1]).then_inc(s_m, 1)
                dve.wait_ge(s_m, n + 1)
                nc.vector.tensor_scalar(nm[:, t, h:h + 1], mx[:, t, h:h + 1], -1.0, None, ALU.mult).then_inc(s_n, 1)

            def turned(n):
                t, m, g = work[n]
                S = (t + 1) * P
                dve.wait_ge(s_x, n + 1)
                if n >= 2:
                    dve.wait_ge(s_o, n - 1)
                nc.vector.tensor_copy(pT[:, n % 2, 0:S], px[:, n % 2, 0:S]).then_inc(s_c, 1)

            score(0)
            for n in range(len(work)):
                if n + 1 < len(work):
                    score(n + 1)
                turned(n)
                if n % 8 == 7:
                    t = n // 8
                    dve.wait_ge(s_e, n + 1)
                    nc.vector.reciprocal(rc[:, t, :], sm[:, t, :]).then_inc(s_r, 1)
                    dve.wait_ge(s_r, t + 1)
                    dve.wait_ge(s_o, n + 1)
                    if t >= 2:
                        dve.wait_ge(s_t, t - 1)
                    r = rc[:, t, :].rearrange("p (g m) -> p m g", g=2).unsqueeze(3).to_broadcast([P, 4, 2, HD])
                    nc.vector.tensor_tensor(at[:, t % 2, :].rearrange("p (m g d) -> p m g d", m=4, g=2),
                                            po[:, t % 2, :].rearrange("p (m g d) -> p m g d", m=4, g=2),
                                            r, ALU.mult).then_inc(s_a, 1)
                    dve.wait_ge(s_t, t + 1)
                    nc.vector.tensor_copy(attT[:, :, t * P:(t + 1) * P],
                                          pa[:, 0, :].rearrange("p (m n) -> p m n", m=4)).then_inc(s_f, 1)

        @block.scalar
        def _(act):
            for n, (t, m, g) in enumerate(work):
                S = (t + 1) * P
                h = m + 4 * g
                act.wait_ge(s_n, n + 1)
                if n >= 2:
                    act.wait_ge(s_x, n - 1)
                nc.scalar.activation(pr[:, n % 2, 0:S], lm[:, n % 2, 0:S], ACT.Exp, bias=nm[:, t, h:h + 1],
                                     accum_out=sm[:, t, h:h + 1]).then_inc(s_e, 1)


def sample_attention(nc, I, c, proj, ikT, vtok, iwtok, rev, attT):
    R = TS * NH
    with ExitStack() as ctx:
        a = Alloc(nc, ctx)
        kx = a.sb("sa_kidx", [HD, 2, NPG, PG])
        kc = a.sb("sa_k", [P, 2, NPG, PG])
        vc = a.sb("sa_v", [P, 4, NPG, P])
        qi = a.sb("sa_iq", [HD, TS, TS, NH])
        qa = a.sb("sa_q", [P, TS, TS, NH])
        wx = a.sb("sa_iw", [TS, TS, NH])
        wb = a.sb("sa_iwT", [R, TS])
        rl = a.sb("sa_relu", [R, L])
        wk = a.sb("sa_work", [TS, L])
        m8 = a.sb("sa_max8", [TS, 8])
        mk = a.sb("sa_mask", [TS, L])
        mx = a.sb("sa_max", [R, 4])
        pr = a.sb("sa_prob", [R, L])
        pT = a.sb("sa_probT", [P, NPG, R])
        pn = a.sb("sa_new", [R, TS])
        pnT = a.sb("sa_newT", [TS, R])
        pS = a.ps("sa_ps", [P, 3, 512])
        pC = a.ps("sa_score_ps", [P, 3, 512])
        pX = a.ps("sa_turn_ps", [P, 1, 512])
        pO = a.ps("sa_out_ps", [P, 1, 512])
        s_xl, s_kl = [a.sem(f"sa_kidx_loaded{i}") for i in range(2)], [a.sem(f"sa_k_loaded{i}") for i in range(2)]
        s_vl = [a.sem(f"sa_v_loaded{i}") for i in range(4)]
        s_z, s_g, s_q = a.sem("sa_zeroed"), a.sem("sa_iwmask"), a.sem("sa_qblocks")
        s_px, s_pk, s_v, s_wT, s_e = (a.sem("sa_" + x) for x in ("ixprod", "kprod", "dve_chain", "iwturned", "exp"))
        s_sc, s_rl, s_cp, s_mk, s_tn, s_tc, s_ov = (a.sem("sa_" + x) for x in (
            "scores", "relued", "iwT_copied", "mask_made", "turned", "turn_copied", "out"))
        s_nm = a.sem("sa_negmax")
        block = ctx.enter_context(nc.Block())
        pSf = pS[:, :, :].rearrange("p a b -> p (a b)")
        pCf = pC[:, :, :].rearrange("p a b -> p (a b)")
        pieces = ((0, 512), (512, 1024), (1024, L))

        def load(eng, src, dst, b, s):
            for g in range(NPG):
                page = eng.value_load(c.small["pages"][0:1, b * NPG + g:b * NPG + g + 1], min_val=0, max_val=79)
                eng.dma_start(dst[:, g, :], src[bass.ds(page, 1), :, :].rearrange("a p n -> p (a n)")).then_inc(s, 16)

        @block.sync
        def _(sp):
            for b in range(TS):
                if b >= 2:
                    sp.wait_ge(s_px, b - 1)
                load(sp, I["kidxT"], kx[:, b % 2], b, s_xl[b % 2])
            for b in range(TS):
                if b >= 4:
                    sp.wait_ge(s_ov, b - 3)
                load(sp, I["vC"], vc[:, b % 4], b, s_vl[b % 4])

        @block.gpsimd
        def _(pool):
            nc.gpsimd.memset(qi[:, :, :, :], 0.0).then_inc(s_z, 1)
            nc.gpsimd.memset(qa[:, :, :, :], 0.0).then_inc(s_z, 1)
            nc.gpsimd.tensor_tensor(wx[:, :, :], c.sel_b[:, :, :],
                                    iwtok[0:TS, NT, :].unsqueeze(1).to_broadcast([TS, TS, NH]), ALU.mult).then_inc(s_g, 1)

        @block.scalar
        def _(act):
            for b in range(TS):
                if b >= 2:
                    act.wait_ge(s_pk, b - 1)
                load(act, I["kT"], kc[:, b % 2], b, s_kl[b % 2])
                if b == 1:
                    act.wait_ge(s_px, TS)
                    nc.scalar.activation(rl[:, :], pSf[0:R, 0:L], ACT.Relu, scale=HD ** -0.5).then_inc(s_rl, 1)
            act.wait_ge(s_nm, 1)
            nc.scalar.activation(pr[:, :], pSf[0:R, 0:L], ACT.Exp, bias=mx[:, 1:2],
                                 accum_out=mx[:, 2:3]).then_inc(s_e, 1)

        @block.vector
        def _(dve):
            link = Chain(dve, s_v)
            dve.wait_ge(s_z, 2)
            for h in range(NH):
                r = HD * (h % 2)
                d = qi[:, :, :, :].rearrange("p a b h -> p (a b h)")[:, h:h + 72 * 7 + 1:72]
                nc.vector.tensor_copy(d, proj[r:r + HD, IQ + h // 2, TP:N]).then_inc(s_q, 1)
            for m in range(4):
                for g in range(2):
                    h = m + 4 * g
                    d = qa[:, :, :, :].rearrange("p a b h -> p (a b h)")[HD * g:HD * g + HD, h:h + 72 * 7 + 1:72]
                    nc.vector.tensor_scalar(d, proj[HD * g:HD * g + HD, AQ + m, TP:N], HD ** -0.5, None,
                                            ALU.mult).then_inc(s_q, 1)
            dve.wait_ge(s_wT, 1)
            nc.vector.tensor_copy(wb[:, :], pX[0:R, 0, 0:TS]).then_inc(s_cp, 1)
            dve.wait_ge(s_sc, 1)
            for k in range(TOPS // 8):
                src = pCf[0:TS, 0:L] if k == 0 else wk[:, :]
                link(nc.vector.max(m8[:, :], src))
                link(nc.vector.match_replace(wk[:, :], m8[:, :], src, SENT))
            nc.vector.tensor_scalar(mk[:, :], wk[:, :], SENT, OFF, ALU.not_equal, ALU.mult).then_inc(s_mk, 1)
            dve.wait_ge(s_pk, TS + 1)
            link(nc.vector.tensor_reduce(mx[:, 0:1], pSf[0:R, 0:L], X, ALU.max))
            nc.vector.tensor_scalar(mx[:, 1:2], mx[:, 0:1], -1.0, None, ALU.mult).then_inc(s_nm, 1)
            dve.wait_ge(s_e, 1)
            link(nc.vector.reciprocal(mx[:, 3:4], mx[:, 2:3]))
            link(nc.vector.tensor_scalar(pr[:, :], pr[:, :], mx[:, 3:4], None, ALU.mult))
            link(nc.vector.tensor_scalar(pn[:, :], c.selT[:, :], pr[:, PAST:L], None, ALU.mult))
            dve.wait_ge(s_tn, 1)
            nc.vector.tensor_copy(pT[:, :, :], pX[:, 0, :].rearrange("p (g r) -> p g r", r=R)).then_inc(s_tc, 1)
            dve.wait_ge(s_tn, 2)
            nc.vector.tensor_copy(pnT[:, :], pC[0:TS, 0, 0:R]).then_inc(s_tc, 1)
            dve.wait_ge(s_ov, TS)
            for m in range(4):
                for g in range(2):
                    h = m + 4 * g
                    src = pO[HD * g:HD * g + HD, 0, 0:R].rearrange("p (b h) -> p b h", h=NH)[:, :, h]
                    nc.vector.tensor_copy(attT[HD * g:HD * g + HD, m, TP:N], src).then_inc(s_tc, 1)

        @block.tensor
        def _(pe):
            pe.wait_ge(s_g, 1)
            nc.tensor.transpose(pX[0:R, 0, 0:TS], wx[:, :, :].rearrange("p a b -> p (a b)"),
                                c.ident[0:TS, 0:TS]).then_inc(s_wT, 1)
            pe.wait_ge(s_q, 16)
            for b in range(TS):
                pe.wait_ge(s_xl[b % 2], 16 * NPG * (b // 2 + 1))
                q = qi[:, b, :, :].rearrange("p b h -> p (b h)")
                for s0, s1 in pieces:
                    k = (kx[:, b % 2].rearrange("p g n -> p (g n)")[:, s0:s1] if s0 < PAST
                         else ikT[0:HD, TP + b:TP + b + 1])
                    last = nc.tensor.matmul(pSf[0:R, s0:s1], q, k, start=(b == 0), stop=(b == TS - 1))
                last.then_inc(s_px, 1)
            pe.wait_ge(s_rl, 1)
            pe.wait_ge(s_cp, 1)
            for s0, s1 in pieces:
                last = nc.tensor.matmul(pCf[0:TS, s0:s1], wb[:, :], rl[:, s0:s1], start=True, stop=True)
            last.then_inc(s_sc, 1)
            for b in range(TS):
                pe.wait_ge(s_kl[b % 2], 16 * NPG * (b // 2 + 1))
                q = qa[:, b, :, :].rearrange("p b h -> p (b h)")
                for s0, s1 in pieces:
                    k = (kc[:, b % 2].rearrange("p g n -> p (g n)")[:, s0:s1] if s0 < PAST
                         else proj[:, AK, TP + b:TP + b + 1])
                    last = nc.tensor.matmul(pSf[0:R, s0:s1], q, k, start=(b == 0), stop=False)
                last.then_inc(s_pk, 1)
            pe.wait_ge(s_mk, 1)
            for s0, s1 in pieces:
                nc.tensor.matmul(pSf[0:R, s0:s1], c.sel_h[:, :, :].rearrange("p a b -> p (a b)"), rev[:, s0:s1],
                                 start=False, stop=False)
                last = nc.tensor.matmul(pSf[0:R, s0:s1], c.sel_b[:, :, :].rearrange("p a b -> p (a b)"), mk[:, s0:s1],
                                        start=False, stop=True)
            last.then_inc(s_pk, 1)
            pe.wait_ge(s_v, 2 * (TOPS // 8) + 4)
            for g in range(NPG):
                last = nc.tensor.transpose(pX[:, 0, g * R:(g + 1) * R], pr[:, g * PG:(g + 1) * PG], c.ident[0:R, 0:R])
            last.then_inc(s_tn, 1)
            nc.tensor.transpose(pC[0:TS, 0, 0:R], pn[:, :], c.ident[0:R, 0:R]).then_inc(s_tn, 1)
            pe.wait_ge(s_tc, 2)
            nc.tensor.matmul(pO[:, 0, 0:R], vtok[0:TS, NT, :], pnT[:, :], start=True, stop=False,
                             skip_group_check=True)
            for b in range(TS):
                pe.wait_ge(s_vl[b % 4], 16 * NPG * (b // 4 + 1))
                for g in range(NPG):
                    last = nc.tensor.matmul(pO[:, 0, b * NH:(b + 1) * NH], vc[:, b % 4, g, :],
                                            pT[:, g, b * NH:(b + 1) * NH], start=False,
                                            stop=(b == TS - 1 and g == NPG - 1), skip_group_check=True)
                last.then_inc(s_ov, 1)


def hgrn(nc, I, O, c, proj, hitok, hgoT):
    M = CH // 2 - 1
    RS = 2 * (P // CH) + 1
    with ExitStack() as ctx:
        a = Alloc(nc, ctx)
        lb = a.sb("hg_lb", [P, 8, HG])
        kk = a.sb("hg_k", [P, HG, N])
        ff = proj[:, HF:HF + HG, :]
        q1, k1 = proj[:, AQ:AQ + HG, 0:TP], proj[:, IQ:IQ + HG, 0:TP]
        bb = a.sb("hg_b", [P, HG, TP])
        k2T = bb[:, :, :].rearrange("p h (t n) -> p h t n", t=NT)
        dd = a.sb("hg_d", [P, HG, N])
        q2 = a.sb("hg_q2", [P, HG, TP])
        el = a.sb("hg_decay", [P, HG, NCH])
        be = a.sb("hg_b_end", [P, HG, NCH])
        AT = a.sb("hg_scores", [P, 2, HG, P])
        st = a.sb("hg_state", [P, RS, HG, P])
        oT = hgoT
        ss = a.sb("hg_sample_state", [P, TS, HG, P])
        kv = a.sb("hg_sample_kv", [P, 2, HG, P])
        epsc = a.sb("hg_eps", [P, 1])
        pA = a.ps("hg_ps_a", [P, 2, 512])
        pB = a.ps("hg_ps_b", [P, 2, 512])
        pO = a.ps("hg_ps_o", [P, 4, 512])
        s_v, s_a, s_d, s_o = a.sem("hg_dve_chain"), a.sem("hg_act"), a.sem("hg_loaded"), a.sem("hg_stored")
        s_lb, s_f, s_b, s_d1, s_d2, s_w = (a.sem("hg_" + x) for x in (
            "lbdiff", "f_made", "b_made", "mid_diff", "end_diff", "weighted"))
        s_x, s_xc, s_s, s_sc, s_u, s_st, s_oo, s_oc = (a.sem("hg_" + x) for x in (
            "turned", "turn_copied", "scores_made", "scores_masked", "kv_made", "state", "out_made", "out_copied"))
        s_vc, s_n = a.sem("hg_v_used"), a.sem("hg_norm_chain")
        s_vb, s_ss, s_so, s_sq, s_ms, s_rt, s_e = (a.sem("hg_" + x) for x in (
            "v_spread", "sample_state_made", "sample_out", "squared", "mean", "root", "exps"))

        def chunks(t, h):
            return t[:, h, 0:TP].rearrange("p (c k) -> p c k", k=CH)

        with nc.Block() as block:
            @block.sync
            def _(sp):
                sp.dma_start(ss[:, :, :, :], I["state"]).then_inc(s_d, 16)

            @block.scalar
            def _(act):
                act.wait_ge(s_lb, 1)
                nc.scalar.activation(lb[:, 3:5, :], lb[:, 1:3, :], ACT.Exp).then_inc(s_a, 1)
                act.wait_ge(s_f, HG)
                for h in range(HG):
                    nc.scalar.activation(dd[:, h, 0:TP], ff[:, h, 0:TP], ACT.Ln).then_inc(s_a, 1)
                for h in range(HG):
                    act.wait_ge(s_d1, h + 1)
                    nc.scalar.activation(q1[:, h, :], dd[:, h, 0:TP], ACT.Exp).then_inc(s_e, 1)
                    nc.scalar.activation(k1[:, h, :], dd[:, h, 0:TP], ACT.Exp, scale=-1.0).then_inc(s_e, 1)
                    nc.scalar.activation(q2[:, h, :], bb[:, h, :], ACT.Exp).then_inc(s_e, 1)
                    nc.scalar.activation(el[:, h, :], chunks(bb, h)[:, :, CH - 1], ACT.Exp).then_inc(s_e, 1)
                for h in range(HG):
                    act.wait_ge(s_d2, h + 1)
                    nc.scalar.activation(dd[:, h, 0:TP], bb[:, h, :], ACT.Exp, scale=-1.0).then_inc(s_e, 1)

            @block.vector
            def _(dve):
                link = Chain(dve, s_v)
                l = c.small["lbl"]
                link(nc.vector.tensor_tensor(lb[:, 0, :], l[:, 0, :], l[:, 1, :], ALU.max))
                link(nc.vector.tensor_tensor(lb[:, 1, :], l[:, 0, :], lb[:, 0, :], ALU.subtract))
                nc.vector.tensor_tensor(lb[:, 2, :], l[:, 1, :], lb[:, 0, :], ALU.subtract).then_inc(s_lb, 1)
                dve.wait_ge(s_a, 1)
                link(nc.vector.tensor_tensor(lb[:, 5, :], lb[:, 3, :], lb[:, 4, :], ALU.add))
                link(nc.vector.reciprocal(lb[:, 6, :], lb[:, 5, :]))
                link(nc.vector.tensor_tensor(lb[:, 7, :], lb[:, 3, :], lb[:, 6, :], ALU.mult))
                link(nc.vector.tensor_scalar(lb[:, 0, :], lb[:, 7, :], -1.0, 1.0, ALU.mult, ALU.add))
                for h in range(HG):
                    nc.vector.tensor_scalar(ff[:, h, :], proj[:, HF + h, :], lb[:, 0, h:h + 1], lb[:, 7, h:h + 1],
                                            ALU.mult, ALU.add).then_inc(s_f, 1)
                dve.wait_ge(s_f, HG)
                for h in range(HG):
                    nc.vector.tensor_scalar(kk[:, h, :], ff[:, h, :], -1.0, 1.0, ALU.mult, ALU.add).then_inc(s_f, 1)
                for h in range(HG):
                    dve.wait_ge(s_a, 2 + h)
                    nc.vector.tensor_tensor_scan(bb[:, h, :], c.reset[:, :], dd[:, h, 0:TP], 0.0, ALU.mult,
                                                 ALU.add).then_inc(s_b, 1)
                for h in range(HG):
                    dve.wait_ge(s_b, h + 1)
                    b = chunks(bb, h)
                    nc.vector.tensor_tensor(chunks(dd, h), b, b[:, :, M:M + 1].to_broadcast([P, NCH, CH]),
                                            ALU.subtract).then_inc(s_d1, 1)
                dve.wait_ge(s_f, 2 * HG)
                for h in range(HG):
                    dve.wait_ge(s_e, 4 * h + 4)
                    b = chunks(bb, h)
                    link(nc.vector.tensor_copy(be[:, h, :], b[:, :, CH - 1]))
                    nc.vector.tensor_tensor(b, b, be[:, h, :].unsqueeze(2).to_broadcast([P, NCH, CH]),
                                            ALU.subtract).then_inc(s_d2, 1)
                    nc.vector.tensor_tensor(q1[:, h, :], q1[:, h, :], proj[:, HQ + h, 0:TP], ALU.mult).then_inc(s_w, 1)
                    nc.vector.tensor_tensor(k1[:, h, :], k1[:, h, :], kk[:, h, 0:TP], ALU.mult).then_inc(s_w, 1)
                    nc.vector.tensor_tensor(q2[:, h, :], q2[:, h, :], proj[:, HQ + h, 0:TP], ALU.mult).then_inc(s_w, 1)
                for h in range(HG):
                    dve.wait_ge(s_e, 4 * HG + h + 1)
                    nc.vector.tensor_tensor(dd[:, h, 0:TP], dd[:, h, 0:TP], kk[:, h, 0:TP], ALU.mult).then_inc(s_w, 1)
                dve.wait_ge(s_w, 4 * HG)

        s_m = a.sem("hg_zero_state")
        with nc.Block() as block:
            @block.tensor
            def _(pe):
                for h in range(HG):
                    if h >= 2:
                        pe.wait_ge(s_xc, h - 1)
                    for t in range(NT):
                        last = nc.tensor.transpose(pA[:, h % 2, t * P:(t + 1) * P], dd[:, h, t * P:(t + 1) * P],
                                                   c.ident[:, :])
                    last.then_inc(s_x, 1)
                pe.wait_ge(s_xc, HG)

                def kv_of(n):
                    t, r = n * CH // P, n * CH % P
                    if n >= 2:
                        pe.wait_ge(s_st, (n - 1) * HG)
                    for h in range(HG):
                        last = nc.tensor.matmul(pB[:, n % 2, h * P:(h + 1) * P], k2T[r:r + CH, h, t, :],
                                                hitok[r:r + CH, t, h * P:(h + 1) * P], start=True, stop=True)
                    last.then_inc(s_u, 1)

                def scores(t):
                    if t >= 2:
                        pe.wait_ge(s_sc, t - 1)
                    for h in range(HG):
                        last = nc.tensor.matmul(pA[:, t % 2, h * P:(h + 1) * P], k1[:, h, t * P:(t + 1) * P],
                                                q1[:, h, t * P:(t + 1) * P], start=True, stop=True)
                    last.then_inc(s_s, 1)

                def out(t):
                    pe.wait_ge(s_sc, t + 1)
                    pe.wait_ge(s_st, (4 * t + 3) * HG)
                    if t >= 2:
                        pe.wait_ge(s_oc, t - 1)
                    for h in range(HG):
                        o = pO[:, t % 2, h * P:(h + 1) * P]
                        nc.tensor.matmul(o, hitok[:, t, h * P:(h + 1) * P], AT[:, t % 2, h, :],
                                         start=True, stop=False, skip_group_check=True)
                        for j in range(P // CH):
                            n = t * (P // CH) + j
                            last = nc.tensor.matmul(o[:, j * CH:(j + 1) * CH], st[:, n % RS, h, :],
                                                    q2[:, h, n * CH:(n + 1) * CH], start=False,
                                                    stop=(j == P // CH - 1), skip_group_check=True)
                    last.then_inc(s_oo, 1)

                for t in range(NT):
                    scores(t)
                    for j in range(P // CH):
                        kv_of(t * (P // CH) + j)
                    out(t)
                for b in range(TS):
                    if b >= 2:
                        pe.wait_ge(s_vc, b - 1)
                    nc.tensor.matmul(pO[:, 2 + b % 2, :], c.pick[:, b, :], hitok[0:TS, NT, :],
                                     start=True, stop=True).then_inc(s_vb, 1)
                pe.wait_ge(s_ss, TS)
                pe.wait_ge(s_st, NCH * HG)
                for b in range(TS):
                    for h in range(HG):
                        last = nc.tensor.matmul(pB[:, 0, h * TS + b:h * TS + b + 1], ss[:, b, h, :],
                                                proj[:, HQ + h, TP + b:TP + b + 1], start=True, stop=True)
                last.then_inc(s_so, 1)

            @block.vector
            def _(dve):
                nc.vector.memset(st[:, 0, :, :], 0.0).then_inc(s_m, 1)
                nc.vector.memset(epsc[:, :], EPS).then_inc(s_m, 1)
                for h in range(HG):
                    dve.wait_ge(s_x, h + 1)
                    nc.vector.tensor_copy(k2T[:, h, :, :], pA[:, h % 2, :].rearrange("p (t n) -> p t n", t=NT)
                                          ).then_inc(s_xc, 1)
                dve.wait_ge(s_m, 2)
                for t in range(NT):
                    dve.wait_ge(s_s, t + 1)
                    if t >= 2:
                        dve.wait_ge(s_oo, t - 1)
                    for h in range(HG):
                        ins = nc.vector.scalar_tensor_tensor(out=AT[:, t % 2, h, :], in0=pA[:, t % 2, h * P:(h + 1) * P],
                                                             scalar=3.0e38, in1=c.tri[:, :], op0=ALU.min, op1=ALU.mult)
                    ins.then_inc(s_sc, 1)
                    for j in range(P // CH):
                        n = t * (P // CH) + j
                        dve.wait_ge(s_u, n + 1)
                        if n >= 1:
                            dve.wait_ge(s_st, n * HG)
                        for h in range(HG):
                            nc.vector.scalar_tensor_tensor(out=st[:, (n + 1) % RS, h, :], in0=st[:, n % RS, h, :],
                                                           scalar=el[:, h, n:n + 1], in1=pB[:, n % 2, h * P:(h + 1) * P],
                                                           op0=ALU.mult, op1=ALU.add).then_inc(s_st, 1)
                    dve.wait_ge(s_oo, t + 1)
                    nc.vector.tensor_copy(oT[:, :, t * P:(t + 1) * P], pO[:, t % 2, :].rearrange("p (h n) -> p h n", h=HG)
                                          ).then_inc(s_oc, 1)
                dve.wait_ge(s_d, 16)
                for b in range(TS):
                    dve.wait_ge(s_vb, b + 1)
                    if b >= 2:
                        dve.wait_ge(s_ss, b - 1)
                    for h in range(HG):
                        ins = nc.vector.tensor_scalar(kv[:, b % 2, h, :], pO[:, 2 + b % 2, h * P:(h + 1) * P],
                                                      kk[:, h, TP + b:TP + b + 1], None, ALU.mult)
                    ins.then_inc(s_vc, 1)
                    dve.wait_ge(s_vc, b + 1)
                    for h in range(HG):
                        ins = nc.vector.scalar_tensor_tensor(out=ss[:, b, h, :], in0=ss[:, b, h, :],
                                                             scalar=ff[:, h, TP + b:TP + b + 1], in1=kv[:, b % 2, h, :],
                                                             op0=ALU.mult, op1=ALU.add)
                    ins.then_inc(s_ss, 1)
                dve.wait_ge(s_so, 1)
                nc.vector.tensor_copy(oT[:, :, TP:N], pB[:, 0, 0:HG * TS].rearrange("p (h b) -> p h b", h=HG)
                                      ).then_inc(s_oc, 1)
                dve.wait_ge(s_oc, NT + 1)

            @block.sync
            def _(sp):
                sp.wait_ge(s_st, NCH * HG)
                sp.dma_start(O["hg_p"], st[:, NCH % RS, :, :]).then_inc(s_o, 16)
                sp.wait_ge(s_ss, TS)
                sp.dma_start(O["hg_s"], ss[:, :, :, :]).then_inc(s_o, 16)
                sp.wait_ge(s_o, 32)

        sq, rt, sg = kk, ff, dd
        with nc.Block() as block:
            @block.scalar
            def _(act):
                for h in range(HG):
                    nc.scalar.activation(sq[:, h, :], oT[:, h, :], ACT.Square).then_inc(s_sq, 1)
                for h in range(HG):
                    act.wait_ge(s_ms, h + 1)
                    nc.scalar.activation(halves(rt[:, h, :]), pO[:, 2 * (h % 2):2 * (h % 2) + 2, 0:HALF], ACT.Sqrt,
                                         scale=1.0 / P, bias=epsc[:, 0:1]).then_inc(s_rt, 1)
                for h in range(HG):
                    nc.scalar.activation(sg[:, h, :], proj[:, HGT + h, :], ACT.Sigmoid).then_inc(s_rt, 1)

            @block.tensor
            def _(pe):
                for h in range(HG):
                    pe.wait_ge(s_sq, h + 1)
                    if h >= 2:
                        pe.wait_ge(s_rt, h - 1)
                    for j in range(2):
                        last = nc.tensor.matmul(pO[:, 2 * (h % 2) + j, 0:HALF], c.ones[:, :],
                                                sq[:, h, j * HALF:(j + 1) * HALF], start=True, stop=True)
                    last.then_inc(s_ms, 1)

            @block.vector
            def _(dve):
                link = Chain(dve, s_n)
                for h in range(HG):
                    dve.wait_ge(s_rt, h + 1)
                    link(nc.vector.reciprocal(rt[:, h, :], rt[:, h, :]))
                    link(nc.vector.scalar_tensor_tensor(out=oT[:, h, :], in0=oT[:, h, :],
                                                        scalar=c.small["g_hgrn"][:, 0:1], in1=rt[:, h, :],
                                                        op0=ALU.mult, op1=ALU.mult))
                    link(nc.vector.tensor_tensor(oT[:, h, :], oT[:, h, :], proj[:, HGT + h, :], ALU.mult))
                for h in range(HG):
                    dve.wait_ge(s_rt, HG + h + 1)
                    link(nc.vector.tensor_tensor(hgoT[:, h, :], oT[:, h, :], sg[:, h, :], ALU.mult))


def merge(nc, I, c, proj, attT, hgoT, x):
    RING = 4
    with ExitStack() as ctx:
        a = Alloc(nc, ctx)
        ring = a.sb("mg_ring", [P, RING, DC, P])
        mix = a.sb("mg_mix", [P, DC, N])
        ta = a.sb("mg_a", [P, 2, N])
        tb = a.sb("mg_b", [P, 2, N])
        pa = a.ps("mg_ps_a", [P, 2, 2, 512])
        pb = a.ps("mg_ps_b", [P, 2, 2, 512])
        s_w = [a.sem(f"mg_loaded{r}") for r in range(RING)]
        s_p, s_g, s_m, s_o, s_x = (a.sem("mg_" + k) for k in ("products", "gated", "mixed", "out_product", "added"))
        block = ctx.enter_context(nc.Block())

        @block.sync
        def _(sp):
            for n in range(2 * DC):
                if n >= RING:
                    k = n - RING
                    sp.wait_ge(s_p if k < DC else s_o, k % DC + 1)
                src = I["w_ab"][n] if n < DC else I["w_out"][n - DC]
                sp.dma_start(ring[:, n % RING], src).then_inc(s_w[n % RING], 16)

        @block.tensor
        def _(pe):
            for n in range(2 * DC):
                pe.wait_ge(s_w[n % RING], 16 * (n // RING + 1))
                m = n % DC
                if n < DC:
                    if n >= 2:
                        pe.wait_ge(s_g, 2 * (n - 1))
                    for ps, src, k0 in ((pa, attT, 0), (pb, hgoT, 4)):
                        for j in range(2):
                            for k in range(4):
                                last = nc.tensor.matmul(ps[:, n % 2, j, 0:HALF], ring[:, n % RING, k0 + k, :],
                                                        src[:, k, j * HALF:(j + 1) * HALF],
                                                        start=(k == 0), stop=(k == 3))
                    last.then_inc(s_p, 1)
                else:
                    if m == 0:
                        pe.wait_ge(s_m, DC)
                    if m >= 2:
                        pe.wait_ge(s_x, m - 1)
                    for j in range(2):
                        for k in range(DC):
                            last = nc.tensor.matmul(pa[:, n % 2, j, 0:HALF], ring[:, n % RING, k, :],
                                                    mix[:, k, j * HALF:(j + 1) * HALF],
                                                    start=(k == 0), stop=(k == DC - 1))
                    last.then_inc(s_o, 1)

        @block.vector
        def _(dve):
            for m in range(DC):
                dve.wait_ge(s_p, m + 1)
                if m >= 2:
                    dve.wait_ge(s_m, m - 1)
                nc.vector.tensor_tensor(halves(ta[:, m % 2, :]), pa[:, m % 2, :, 0:HALF], halves(proj[:, ZA + m, :]),
                                        ALU.mult).then_inc(s_g, 1)
                nc.vector.tensor_tensor(halves(tb[:, m % 2, :]), pb[:, m % 2, :, 0:HALF], halves(proj[:, ZB + m, :]),
                                        ALU.mult).then_inc(s_g, 1)
                dve.wait_ge(s_g, 2 * m + 2)
                nc.vector.tensor_tensor(mix[:, m, :], ta[:, m % 2, :], tb[:, m % 2, :], ALU.add).then_inc(s_m, 1)
            for m in range(DC):
                dve.wait_ge(s_o, m + 1)
                nc.vector.tensor_tensor(halves(x[:, m, :]), pa[:, m % 2, :, 0:HALF], halves(x[:, m, :]),
                                        ALU.add).then_inc(s_x, 1)
            dve.wait_ge(s_x, DC)


def route(nc, I, c, xn, i1T, i2T, gT):
    RING = 4
    NG = 2 * PH
    TT = NT + 1
    with ExitStack() as ctx:
        a = Alloc(nc, ctx)
        ring = a.sb("rt_ring", [P, RING, DC, P])
        sk = a.sb("rt_keys", [P, 2, P])
        q = a.sb("rt_q", [P, NG, N])
        pq = a.ps("rt_ps_q", [P, 2, 2, 512])
        s_w = [a.sem(f"rt_loaded{r}") for r in range(RING)]
        s_k, s_p, s_c = a.sem("rt_keys_loaded"), a.sem("rt_product"), a.sem("rt_copied")
        with nc.Block() as block:
            @block.sync
            def _(sp):
                sp.dma_start(sk[:, :, :], I["subkeys"]).then_inc(s_k, 16)
                for n in range(NG):
                    if n >= RING:
                        sp.wait_ge(s_p, n - RING + 1)
                    sp.dma_start(ring[:, n % RING], I["w_q"][n]).then_inc(s_w[n % RING], 16)

            @block.tensor
            def _(pe):
                pe.wait_ge(s_k, 16)
                for n in range(NG):
                    pe.wait_ge(s_w[n % RING], 16 * (n // RING + 1))
                    if n >= 2:
                        pe.wait_ge(s_c, n - 1)
                    for j in range(2):
                        for k in range(DC):
                            last = nc.tensor.matmul(pq[:, n % 2, j, 0:HALF], ring[:, n % RING, k, :],
                                                    xn[:, k, j * HALF:(j + 1) * HALF],
                                                    start=(k == 0), stop=(k == DC - 1))
                    last.then_inc(s_p, 1)

            @block.scalar
            def _(act):
                for n in range(NG):
                    act.wait_ge(s_p, n + 1)
                    nc.scalar.activation(halves(q[:, n, :]), pq[:, n % 2, :, 0:HALF], ACT.Identity).then_inc(s_c, 1)
                act.wait_ge(s_c, NG)

        S = a.sb("rt_scores", [P, 2, NG, P])
        wk = a.sb("rt_work", [P, 2, P])
        v = a.sb("rt_top", [P, NG, PK])
        ix = a.sb("rt_index", [P, NG, PK], U32)
        ixf = a.sb("rt_index_f", [P, NG, PK])
        cd = a.sb("rt_sums", [P, PH, PK, PK])
        cw = a.sb("rt_sums_work", [P, PK * PK])
        sv = a.sb("rt_sum_top", [P, PH, PK])
        ci = a.sb("rt_sum_index", [P, PH, PK], U32)
        cb = a.sb("rt_sum_parts", [P, 2, PH, PK], U32)
        cf = a.sb("rt_sum_parts_f", [P, 2, PH, PK])
        oh = a.sb("rt_onehot", [P, PH * PK, PK])
        se = a.sb("rt_slots", [P, 3, PH, PK])
        ex = a.sb("rt_exp", [P, PH, PK])
        sm = a.sb("rt_sum", [P, 2, PH])
        ps = a.ps("rt_ps_s", [P, 4, 512])
        px = pq[:, 0, :, :]
        s_v, s_s, s_sc, s_e, s_ex, s_t, s_x = (a.sem("rt_" + k) for k in (
            "chain", "scores_made", "scores_copied", "shifted", "exp", "slots_made", "turned"))
        with nc.Block() as block:
            @block.tensor
            def _(pe):
                def scores(t):
                    m = P if t < NT else TS
                    if t >= 1:
                        pe.wait_ge(s_sc, t)
                    for g in range(NG):
                        last = nc.tensor.matmul(ps[0:m, g // 4, (g % 4) * P:(g % 4 + 1) * P], q[:, g, t * P:t * P + m],
                                                sk[:, g % 2, :], start=True, stop=True)
                    last.then_inc(s_s, 1)

                def turn(t):
                    m = P if t < NT else TS
                    pe.wait_ge(s_t, t + 1)
                    for j in range(3):
                        last = nc.tensor.transpose(px[:, 0, j * P:j * P + m],
                                                   se[0:m, j].rearrange("p h k -> p (h k)"), c.ident[0:m, 0:m])
                    last.then_inc(s_x, 1)

                scores(0)
                for t in range(TT):
                    if t + 1 < TT:
                        scores(t + 1)
                    turn(t)

            @block.scalar
            def _(act):
                for t in range(TT):
                    m = P if t < NT else TS
                    act.wait_ge(s_s, t + 1)
                    if t >= 2:
                        act.wait_ge(s_t, t - 1)
                    nc.scalar.copy(S[0:m, t % 2].rearrange("p g k -> p (g k)"),
                                   ps[0:m, :, :].rearrange("p a b -> p (a b)")).then_inc(s_sc, 1)
                    act.wait_ge(s_e, t + 1)
                    nc.scalar.activation(ex[0:m, :, :], se[0:m, 2], ACT.Exp).then_inc(s_ex, 1)

            @block.vector
            def _(dve):
                link = Chain(dve, s_v)
                for t in range(TT):
                    m = P if t < NT else TS
                    dve.wait_ge(s_sc, t + 1)
                    for g in range(NG):
                        s = S[0:m, t % 2, g, :]
                        w = wk[0:m, g % 2, :]
                        link(nc.vector.max(v[0:m, g, 0:8], s))
                        link(nc.vector.max_index(ix[0:m, g, 0:8], v[0:m, g, 0:8], s))
                        link(nc.vector.match_replace(w, v[0:m, g, 0:8], s, SENT))
                        link(nc.vector.max(v[0:m, g, 8:16], w))
                        link(nc.vector.max_index(ix[0:m, g, 8:16], v[0:m, g, 8:16], w))
                    vv = v[0:m].rearrange("p (h a) k -> p h a k", a=2)
                    link(nc.vector.tensor_tensor(cd[0:m], vv[:, :, 0, :].unsqueeze(3).to_broadcast([m, PH, PK, PK]),
                                                 vv[:, :, 1, :].unsqueeze(2).to_broadcast([m, PH, PK, PK]), ALU.add))
                    for h in range(PH):
                        s = cd[0:m, h].rearrange("p a b -> p (a b)")
                        w = cw[0:m, :]
                        link(nc.vector.max(sv[0:m, h, 0:8], s))
                        link(nc.vector.max_index(ci[0:m, h, 0:8], sv[0:m, h, 0:8], s))
                        link(nc.vector.match_replace(w, sv[0:m, h, 0:8], s, SENT))
                        link(nc.vector.max(sv[0:m, h, 8:16], w))
                        link(nc.vector.max_index(ci[0:m, h, 8:16], sv[0:m, h, 8:16], w))
                    if t >= 1:
                        dve.wait_ge(s_x, t)
                    nc.vector.tensor_tensor(se[0:m, 2], sv[0:m], sv[0:m, :, 0:1].to_broadcast([m, PH, PK]),
                                            ALU.subtract).then_inc(s_e, 1)
                    link(nc.vector.tensor_scalar(cb[0:m, 0], ci[0:m], 4, None, ALU.logical_shift_right))
                    link(nc.vector.tensor_scalar(cb[0:m, 1], ci[0:m], PK - 1, None, ALU.bitwise_and))
                    link(nc.vector.tensor_copy(cf[0:m], cb[0:m]))
                    link(nc.vector.tensor_copy(ixf[0:m], ix[0:m]))
                    iv = ixf[0:m].rearrange("p (h a) k -> p h a k", a=2)
                    o3 = oh[0:m]
                    o4 = oh[0:m].rearrange("p (h s) k -> p h s k", h=PH)
                    for j in range(2):
                        part = cf[0:m, j].rearrange("p h k -> p (h k)").unsqueeze(2).to_broadcast([m, SLOT, PK])
                        link(nc.vector.tensor_tensor(o3, part, c.iota[0:m, 0:PK].unsqueeze(1).to_broadcast(
                            [m, SLOT, PK]), ALU.is_equal))
                        link(nc.vector.tensor_tensor(o4, o4, iv[:, :, j, :].unsqueeze(2).to_broadcast(
                            [m, PH, PK, PK]), ALU.mult))
                        link(nc.vector.tensor_reduce(se[0:m, j].rearrange("p h k -> p (h k)"), o3, X, ALU.add))
                    dve.wait_ge(s_ex, t + 1)
                    link(nc.vector.tensor_reduce(sm[0:m, 0, :], ex[0:m], X, ALU.add))
                    link(nc.vector.reciprocal(sm[0:m, 1, :], sm[0:m, 0, :]))
                    nc.vector.tensor_tensor(se[0:m, 2], ex[0:m], sm[0:m, 1, :].unsqueeze(2).to_broadcast(
                        [m, PH, PK]), ALU.mult).then_inc(s_t, 1)
                    dve.wait_ge(s_x, t + 1)
                    for j, dst in enumerate((i1T, i2T, gT)):
                        link(nc.vector.tensor_copy(dst[:, t * P:t * P + m], px[:, 0, j * P:j * P + m]))


def routing_weights(nc, c, i1T, i2T, gT, W):
    G = 2
    with ExitStack() as ctx:
        a = Alloc(nc, ctx)
        B = a.sb("rw_b", [P, G, P])
        A = a.sb("rw_a", [P, G, P])
        out = a.sb("rw_out", [P, P, TB])
        ps = a.ps("rw_ps", [P, 2, 512])
        s_b, s_p, s_c, s_o = (a.sem("rw_" + k) for k in ("rows_made", "product", "copied", "stored"))
        block = ctx.enter_context(nc.Block())

        @block.vector
        def _(dve):
            def rows(n, g):
                nc.vector.tensor_scalar(B[:, g, :], c.iota[:, :], i2T[:, n], None, ALU.is_equal)
                nc.vector.tensor_scalar(A[:, g, :], c.iota[:, :], i1T[:, n], gT[:, n], ALU.is_equal,
                                        ALU.mult).then_inc(s_b, 1)

            for g in range(G):
                rows(slice(g, g + 1), g)
            with dve.Fori(1, N // G) as i:
                dve.wait_ge(s_p, i * G)
                for g in range(G):
                    rows(bass.ds(i * G + g, 1), g)

        @block.tensor
        def _(pe):
            def product(made, g):
                pe.wait_ge(s_b, made)
                nc.tensor.matmul(ps[:, g, 0:P], B[:, g, :], A[:, g, :], start=True, stop=True).then_inc(s_p, 1)

            for g in range(G):
                product(g + 1, g)
            with pe.Fori(1, N // G) as i:
                pe.wait_ge(s_c, i * G)
                for g in range(G):
                    product(i * G + (g + 1), g)

        @block.scalar
        def _(act):
            for b in range(NBLK):
                if b >= 1:
                    act.wait_ge(s_o, 16 * b)
                with act.Fori(0, TB // G) as i:
                    for g in range(G):
                        act.wait_ge(s_p, i * G + (b * TB + g + 1))
                        nc.scalar.copy(out[:, :, bass.ds(i * G + g, 1)], ps[:, g, 0:P].unsqueeze(2)).then_inc(s_c, 1)

        @block.sync
        def _(sp):
            for b in range(NBLK):
                sp.wait_ge(s_c, (b + 1) * TB)
                sp.dma_start(W[:, :, b * TB:(b + 1) * TB].rearrange("i p n -> p i n"), out[:, :, :]).then_inc(s_o, 16)
            sp.wait_ge(s_o, 16 * NBLK)


def experts(nc, I, xn, W, x):
    E = 8
    NG = E1 // E
    UR, VR = 4, 8
    with ExitStack() as ctx:
        a = Alloc(nc, ctx)
        u = a.sb("ex_u", [P, UR, DC, P])
        v = a.sb("ex_v", [P, E, D])
        w = a.sb("ex_w", [P, UR, N])
        ge = a.sb("ex_gelu", [P, 2, N])
        H = a.sb("ex_h", [P, 2, E, N])
        pu = a.ps("ex_ps_u", [P, 2, 2, 512])
        pv = a.ps("ex_ps_v", [P, 2, 2, 512])
        s_u = [a.sem(f"ex_u_loaded{r}") for r in range(UR)]
        s_w = [a.sem(f"ex_w_loaded{r}") for r in range(UR)]
        s_v = a.sem("ex_v_loaded")
        s_pu, s_ge, s_h, s_pv, s_ac = (a.sem("ex_" + k) for k in (
            "u_product", "gelu", "hidden", "v_product", "added"))
        block = ctx.enter_context(nc.Block())

        def sum_at(base, k):
            return k if isinstance(base, int) and base == 0 else base + k

        @block.sync
        def _(sp):
            def loads(i0, e, first):
                r = e % UR
                if not first:
                    sp.wait_ge(s_pu, i0 + (e - UR + 1))
                sp.dma_start(u[:, r], I["uT"][i0 + e]).then_inc(s_u[r], 16)

            for e in range(UR):
                loads(0, e, True)
            for e in range(UR, E):
                loads(0, e, False)
            with sp.Fori(1, NG) as g:
                for e in range(E):
                    loads(g * E, e, False)

        @block.gpsimd
        def _(pool):
            def loads(i0, e, first):
                r = e % UR
                if not first:
                    pool.wait_ge(s_h, i0 + (e - UR + 1))
                pool.dma_start(w[:, r, :], W[i0 + e, :, :] if isinstance(i0, int) else
                               W[bass.ds(i0 + e, 1), :, :].rearrange("a p n -> p (a n)")).then_inc(s_w[r], 16)

            for e in range(UR):
                loads(0, e, True)
            for e in range(UR, E):
                loads(0, e, False)
            with pool.Fori(1, NG) as g:
                for e in range(E):
                    loads(g * E, e, False)

        @block.scalar
        def _(act):
            vsrc = I["v"].rearrange("(g e p) d -> g p e d", p=P, e=E)
            act.dma_start(v[:, :, :], vsrc[0]).then_inc(s_v, 16)

            def gelus(i0, e, free):
                act.wait_ge(s_pu, i0 + e + 1)
                if free is not None:
                    act.wait_ge(s_h, free)
                nc.scalar.activation(halves(ge[:, e % 2, :]), pu[:, e % 2, :, 0:HALF], ACT.Gelu).then_inc(s_ge, 1)

            for e in range(E):
                gelus(0, e, e - 1 if e >= 2 else None)
            with act.Fori(1, NG) as g:
                for e in range(E):
                    gelus(g * E, e, g * E + (e - 1))
                act.wait_ge(s_pv, g * DC)
                act.dma_start(v[:, :, :], vsrc[bass.ds(g, 1)].rearrange("g p e d -> p (g e) d")).then_inc(s_v, 16)

        @block.vector
        def _(dve):
            def hide(i0, e, b, free):
                dve.wait_ge(s_ge, i0 + e + 1)
                dve.wait_ge(s_w[e % UR], (i0 // UR if isinstance(i0, int) else i0 // UR) * 16 + (e // UR + 1) * 16)
                if free is not None:
                    dve.wait_ge(s_pv, free)
                nc.vector.tensor_tensor(H[:, b, e, :], ge[:, e % 2, :], w[:, e % UR, :], ALU.mult).then_inc(s_h, 1)

            def add(n0, m):
                dve.wait_ge(s_pv, n0 + m + 1)
                if not isinstance(n0, int) or n0:
                    dve.wait_ge(s_ac, n0 + (m + 1 - DC))
                nc.vector.tensor_tensor(halves(x[:, m, :]), pv[:, m % 2, :, 0:HALF], halves(x[:, m, :]),
                                        ALU.add).then_inc(s_ac, 1)

            def group(k):
                return k * DC

            for e in range(E):
                hide(0, e, 0, None)
            for e in range(E):
                hide(E, e, 1, None)
            for m in range(DC):
                add(0, m)
            with dve.Fori(1, NG // 2) as q:
                for b in range(2):
                    for e in range(E):
                        hide(q * (2 * E) + b * E, e, b, q * (2 * DC) + (b - 1) * DC)
                    for m in range(DC):
                        add(q * (2 * DC) + (b - 1) * DC, m)
            for m in range(DC):
                add((NG - 1) * DC, m)
            dve.wait_ge(s_ac, NG * DC)

        @block.tensor
        def _(pe):
            def first(i0, e, wait):
                r = e % UR
                pe.wait_ge(s_u[r], i0 * (16 // UR) + (e // UR + 1) * 16)
                if wait is not None:
                    pe.wait_ge(s_ge, wait)
                for j in range(2):
                    for k in range(DC):
                        last = nc.tensor.matmul(pu[:, e % 2, j, 0:HALF], u[:, r, k, :],
                                                xn[:, k, j * HALF:(j + 1) * HALF], start=(k == 0), stop=(k == DC - 1))
                last.then_inc(s_pu, 1)

            def second(g, b):
                pe.wait_ge(s_v, g * 16 + 16)
                pe.wait_ge(s_h, g * E + E)
                for m in range(DC):
                    if isinstance(g, int) and g == 0:
                        if m >= 2:
                            pe.wait_ge(s_ac, m - 1)
                    else:
                        pe.wait_ge(s_ac, g * DC + (m - 1))
                    for j in range(2):
                        for e in range(E):
                            last = nc.tensor.matmul(pv[:, m % 2, j, 0:HALF], v[:, e, m * P:(m + 1) * P],
                                                    H[:, b, e, j * HALF:(j + 1) * HALF],
                                                    start=(e == 0), stop=(e == E - 1))
                    last.then_inc(s_pv, 1)

            for e in range(E):
                first(0, e, e - 1 if e >= 2 else None)
            for e in range(E):
                first(E, e, E + e - 1)
            second(0, 0)
            with pe.Fori(1, NG // 2) as q:
                for b in range(2):
                    for e in range(E):
                        first(q * (2 * E) + b * E, e, q * (2 * E) + (b * E + e - 1))
                    second(q * 2 + (b - 1), (b + 1) % 2)
            second(NG - 1, 1)


def per_layer_input(nc, I, c, xn, x):
    RING = 4
    PC = 2
    with ExitStack() as ctx:
        a = Alloc(nc, ctx)
        ring = a.sb("pl_ring", [P, RING, DC + PC, P])
        pT = a.sb("pl_p", [P, PC, N])
        sg = a.sb("pl_sig", [P, 2, N])
        gd = a.sb("pl_gated", [P, 2, N])
        pa = a.ps("pl_ps_a", [P, 2, 2, 512])
        pb = a.ps("pl_ps_b", [P, 2, 2, 512])
        s_w = [a.sem(f"pl_loaded{r}") for r in range(RING)]
        s_i, s_p, s_s, s_g, s_x = (a.sem("pl_" + k) for k in ("p_loaded", "products", "sigmoid", "gated", "added"))
        block = ctx.enter_context(nc.Block())

        @block.sync
        def _(sp):
            sp.dma_start(pT[:, :, :], I["pT"]).then_inc(s_i, 16)
            for n in range(DC):
                if n >= RING:
                    sp.wait_ge(s_p, n - RING + 1)
                sp.dma_start(ring[:, n % RING], I["w_gp"][n]).then_inc(s_w[n % RING], 16)

        @block.tensor
        def _(pe):
            pe.wait_ge(s_i, 16)
            for n in range(DC):
                pe.wait_ge(s_w[n % RING], 16 * (n // RING + 1))
                if n >= 2:
                    pe.wait_ge(s_g, n - 1)
                for ps, src, k0, kn in ((pa, xn, 0, DC), (pb, pT, DC, PC)):
                    for j in range(2):
                        for k in range(kn):
                            last = nc.tensor.matmul(ps[:, n % 2, j, 0:HALF], ring[:, n % RING, k0 + k, :],
                                                    src[:, k, j * HALF:(j + 1) * HALF],
                                                    start=(k == 0), stop=(k == kn - 1))
                last.then_inc(s_p, 1)

        @block.scalar
        def _(act):
            for n in range(DC):
                act.wait_ge(s_p, n + 1)
                if n >= 2:
                    act.wait_ge(s_g, n - 1)
                nc.scalar.activation(halves(sg[:, n % 2, :]), pa[:, n % 2, :, 0:HALF], ACT.Sigmoid).then_inc(s_s, 1)

        @block.vector
        def _(dve):
            for n in range(DC):
                dve.wait_ge(s_s, n + 1)
                if n >= 2:
                    dve.wait_ge(s_x, n - 1)
                nc.vector.tensor_tensor(halves(gd[:, n % 2, :]), pb[:, n % 2, :, 0:HALF], halves(sg[:, n % 2, :]),
                                        ALU.mult).then_inc(s_g, 1)
                dve.wait_ge(s_g, n + 1)
                nc.vector.tensor_tensor(x[:, n, :], x[:, n, :], gd[:, n % 2, :], ALU.add).then_inc(s_x, 1)
            dve.wait_ge(s_x, DC)


def store(nc, a, y, dst):
    s_o = a.sem("y_stored")
    with nc.Block() as block:
        @block.sync
        def _(sp):
            sp.dma_start(dst, y[:, :, :]).then_inc(s_o, 16)
            sp.wait_ge(s_o, 16)


class Tiles:
    pass


def build(nc, I, O, scratch):
    with ExitStack() as ctx:
        a = Alloc(nc, ctx)
        c = Tiles()
        c.ones, c.ident, c.causal, c.tri, c.iota = (a.sb(k, [P, P]) for k in ("ones", "ident", "causal", "tri", "iota"))
        c.reset = a.sb("reset", [P, TP])
        c.sel_b, c.sel_h = a.sb("sel_b", [TS, TS, NH]), a.sb("sel_h", [TS, TS, NH])
        c.selT = a.sb("selT", [TS * NH, TS])
        c.pick = a.sb("pick", [TS, TS, P])
        c.rb = a.sb("rb", [NB + 1, NH])
        c.eps = a.sb("eps", [P, 1])
        rms_sems = [a.sem("rms_" + k) for k in ("squared", "mean", "root", "recip", "scaled")]
        c.x = a.sb("x", [P, DC, N])
        c.small = {k: a.sb("c_" + k, s) for k, s in (("g_mix", [P, DC]), ("g_ffn", [P, DC]), ("g_ple", [P, DC]),
                                                     ("g_final", [P, DC]), ("g_hgrn", [P, 1]), ("lbl", [P, 2, HG]))}
        c.small["pages"] = a.sb("c_pages", [1, TS * NPG], I32)
        x = c.x
        h = a.sb("h", [P, DC, N])
        with ExitStack() as mid:
            b = Alloc(nc, mid)
            constants(nc, a, I, c)
            proj = b.sb("proj", [P, MT, N])
            vtok = b.sb("vtok", [P, NT + 1, P])
            hitok = b.sb("hitok", [P, NT + 1, 512])
            iwtok = b.sb("iwtok", [P, NT + 1, NH])
            ikT = b.sb("ikT", [P, N])
            rms_block(nc, 0, rms_sems, x, h, c.small["g_mix"], c.ones, c.eps)
            project(nc, I, O, c, h, proj, ikT, vtok, hitok, iwtok)
            attT, hgoT = h[:, 0:4, :], h[:, 4:8, :]
            with ExitStack() as att:
                d = Alloc(nc, att)
                rev = d.sb("rev", [NH, REV])
                with ExitStack() as pro:
                    e = Alloc(nc, pro)
                    maskp = e.sb("maskp", [P, NT, TP])
                    toep = e.sb("toep", [P, NH, TP])
                    index_prompt(nc, c, proj, ikT, iwtok, maskp)
                    bias_table(nc, c, I["onehot"], rev, scratch["rev"], toep)
                    attend_prompt(nc, c, proj, vtok, maskp, toep, attT)
                sample_attention(nc, I, c, proj, ikT, vtok, iwtok, rev, attT)
            hgrn(nc, I, O, c, proj, hitok, hgoT)
            merge(nc, I, c, proj, attT, hgoT, x)
        rms_block(nc, 1, rms_sems, x, h, c.small["g_ffn"], c.ones, c.eps)
        with ExitStack() as mid:
            b = Alloc(nc, mid)
            i1T, i2T, gT = (b.sb(k, [P, N]) for k in ("i1T", "i2T", "gT"))
            route(nc, I, c, h, i1T, i2T, gT)
            routing_weights(nc, c, i1T, i2T, gT, scratch["W"])
        experts(nc, I, h, scratch["W"], x)
        rms_block(nc, 2, rms_sems, x, h, c.small["g_ple"], c.ones, c.eps)
        per_layer_input(nc, I, c, h, x)
        rms_block(nc, 3, rms_sems, x, h, c.small["g_final"], c.ones, c.eps)
        store(nc, a, h, O["yT"])


def bucket_onehot():
    dist = PAST - np.arange(REV)
    n = np.maximum(dist, 0)
    nf = np.maximum(n, 1).astype(np.float32)
    large = 16 + (np.log(nf / np.float32(16)) / np.float32(math.log(128 / 16)) * np.float32(16)).astype(np.int32)
    b = np.where(n < 16, n, np.minimum(large, NB - 1))
    b = np.where(dist < 0, NB, b)
    out = np.zeros((NB + 1, REV), np.float32)
    out[b, np.arange(REV)] = 1.0
    return out


def kernel(**inputs):
    import concourse.bacc as bacc
    from concourse.bass_utils import run_bass_kernel_spmd

    g = {k: np.asarray(v) for k, v in inputs.items()}

    def tiles(w):
        k, m = w.shape
        return np.ascontiguousarray(w.reshape(k // P, P, m // P, P).transpose(2, 1, 0, 3))

    def cols(v):
        return np.ascontiguousarray(v.reshape(-1, P).T)

    w_in = g["w_in"][0]
    o = np.cumsum([0, 512, 128, 128, 512, 64, 8, 512, 512, 512, 512, 1024, 1024]).tolist()
    aq, ak, av, iq, ik, iw, hq, hf, hi, hg, za, zb = (w_in[:, o[i]:o[i + 1]] for i in range(12))
    order = [x for m in range(4) for x in (m, m + 4)]
    aq = aq.reshape(D, NH, HD)[:, order].reshape(D, 512)
    w_a = g["w_branch_a"][0].reshape(NH, HD, D)[order].reshape(512, D)
    xT = np.concatenate([g["x_prompt"][0], g["x_sample"][:, 0]]).T
    pT = np.concatenate([g["p_prompt"][0, 0], g["p_sample"][0, :, 0]]).T
    arrays = {
        "xT": xT.reshape(DC, P, N).transpose(1, 0, 2),
        "pT": pT.reshape(2, P, N).transpose(1, 0, 2),
        "w_t": tiles(np.concatenate([aq, ak, iq, hq, hg, hf, za, zb], axis=1)),
        "w_ik": ik.reshape(DC, P, HD).transpose(1, 0, 2),
        "w_tok": np.concatenate([av, hi, iw], axis=1).reshape(DC, P, 648).transpose(1, 0, 2),
        "w_ab": np.concatenate([tiles(w_a), tiles(g["w_branch_b"][0])], axis=2),
        "w_out": tiles(g["w_out"][0]),
        "w_q": tiles(g["peer_wq"][0]),
        "w_gp": np.concatenate([tiles(g["w_ple_gate"][0]), tiles(g["w_ple_proj"][0])], axis=2),
        "subkeys": g["peer_subkeys"][0].transpose(2, 0, 1),
        "uT": tiles(g["peer_u"][0].T),
        "v": g["peer_v"][0],
        "g_mix": cols(g["g_mix"][0]), "g_ffn": cols(g["g_ffn"][0]), "g_ple": cols(g["g_ple"][0]),
        "g_final": cols(g["g_final"]), "g_hgrn": cols(g["g_hgrn"][0]),
        "lbl": g["lb_logits"].reshape(2, HG, P).transpose(2, 0, 1),
        "rel_bias": g["rel_bias"],
        "onehot": bucket_onehot(),
        "pages": g["page_table"].reshape(1, -1),
        "kidxT": g["cache_kidx"][0].transpose(0, 2, 1),
        "kT": g["cache_k"][0].reshape(-1, PG, P).transpose(0, 2, 1),
        "vC": g["cache_v"][0].reshape(-1, PG, P),
        "state": g["state_hgrn"][0].transpose(2, 0, 1, 3),
    }
    nc = bacc.Bacc("TRN2", target_bir_lowering=False, num_devices=1)
    I, sent = {}, {}
    for name, arr in arrays.items():
        arr = np.ascontiguousarray(arr)
        sent["in_" + name] = arr
        I[name] = nc.dram_tensor("in_" + name, arr.shape, mybir.dt.from_np(arr.dtype), kind="ExternalInput").ap()
    shapes = {"yT": [P, DC, N], "kT": [P, N], "v_p": [TP, P], "v_s": [TS, P], "ikT": [HD, N],
              "hg_p": [P, HG, P], "hg_s": [P, TS, HG, P]}
    O = {k: nc.dram_tensor("out_" + k, s, F32, kind="ExternalOutput").ap() for k, s in shapes.items()}
    scratch = {"rev": nc.dram_tensor("scratch_rev", [NH, P, SK], F32).ap(),
               "W": nc.dram_tensor("scratch_w", [E1, P, N], F32).ap()}
    build(nc, I, O, scratch)
    r = run_bass_kernel_spmd(nc, [sent], core_ids=[0]).results[0]
    got = {k: r["out_" + k] for k in shapes}
    y = got["yT"].transpose(2, 1, 0).reshape(N, D)
    k = got["kT"].T.reshape(N, 2, HD)
    kidx = got["ikT"].T
    return (y[None, :TP], y[TP:, None],
            k[None, None, :TP], got["v_p"].reshape(1, 1, TP, 2, HD), kidx[None, None, :TP],
            got["hg_p"].transpose(1, 0, 2)[None, None],
            k[TP:][None, :, None], got["v_s"].reshape(1, TS, 1, 2, HD), kidx[TP:][None, :, None],
            got["hg_s"].transpose(1, 2, 0, 3)[None])
```

```python
from contextlib import ExitStack
import math

import numpy as np
import concourse.bass as bass
from concourse import mybir

F32 = mybir.dt.float32
U32 = mybir.dt.uint32
I32 = mybir.dt.int32
ALU = mybir.AluOpType
ACT = mybir.ActivationFunctionType
X = mybir.AxisListType.X

P = 128
D = 1024
DC = D // P
TP = 512
NT = TP // P
TS = 8
N = TP + TS
HALF = N // 2
HD = 64
NH = 8
NQ = NH * HD // P
HG = 4
CH = 32
NCH = TP // CH
PAST = 1024
PG = 128
NPG = PAST // PG
L = PAST + 1
TOPP = min(256, TP // 4)
TOPS = min(256, L // 4)
SK = TP + P
REV = PAST + P
NB = 32
PH = 8
PK = 16
SLOT = PH * PK
E1 = 128
SENT = -3.0e38
LOW = -1.0e38
OFF = -1.0e30
EPS = 1e-6
AQ, AK, IQ, HQ, HGT, HF, ZA, ZB, MT = 0, 4, 5, 9, 13, 17, 21, 29, 37


def halves(ap):
    return ap.rearrange("p (j n) -> p j n", j=2)


class Alloc:

    def __init__(self, nc, ctx):
        self.nc, self.ctx = nc, ctx

    def sb(self, name, shape, dt=F32):
        return self.ctx.enter_context(self.nc.sbuf_tensor(name, shape, dt))

    def ps(self, name, shape):
        return self.ctx.enter_context(self.nc.psum_tensor(name, shape, F32))

    def sem(self, name):
        return self.nc.alloc_semaphore(name)


class Chain:

    def __init__(self, eng, sem):
        self.eng, self.sem, self.n = eng, sem, 0

    def __call__(self, ins):
        self.n += 1
        ins.then_inc(self.sem, 1)
        self.eng.wait_ge(self.sem, self.n)


def rms_block(nc, turn, sems, src, dst, gain, ones, eps):
    s_sq, s_ms, s_rt, s_rs, s_h = sems
    with ExitStack() as ctx:
        a = Alloc(nc, ctx)
        sq = a.sb(f"rms{turn}_sq", [P, DC, N])
        rt = a.sb(f"rms{turn}_rt", [P, N])
        rs = a.sb(f"rms{turn}_rs", [P, N])
        pm = a.ps(f"rms{turn}_pm", [P, 2, 512])
        block = ctx.enter_context(nc.Block())

        @block.scalar
        def _(act):
            for c in range(DC):
                nc.scalar.activation(sq[:, c, :], src[:, c, :], ACT.Square).then_inc(s_sq, 1)
            act.wait_ge(s_ms, turn + 1)
            nc.scalar.activation(halves(rt[:, :]), pm[:, :, 0:HALF], ACT.Sqrt, scale=1.0 / D,
                                 bias=eps[:, 0:1]).then_inc(s_rt, 1)

        @block.tensor
        def _(pe):
            for c in range(DC):
                pe.wait_ge(s_sq, turn * DC + c + 1)
                for j in range(2):
                    last = nc.tensor.matmul(pm[:, j, 0:HALF], ones[:, :], sq[:, c, j * HALF:(j + 1) * HALF],
                                            start=(c == 0), stop=(c == DC - 1))
            last.then_inc(s_ms, 1)

        @block.vector
        def _(dve):
            dve.wait_ge(s_rt, turn + 1)
            nc.vector.reciprocal(rs[:, :], rt[:, :]).then_inc(s_rs, 1)
            dve.wait_ge(s_rs, turn + 1)
            for c in range(DC):
                nc.vector.scalar_tensor_tensor(out=dst[:, c, :], in0=src[:, c, :], scalar=gain[:, c:c + 1],
                                               in1=rs[:, :], op0=ALU.mult, op1=ALU.mult).then_inc(s_h, 1)
            dve.wait_ge(s_h, (turn + 1) * DC)


def constants(nc, a, I, c):
    s_c, s_c2, s_d = a.sem("const_made"), a.sem("bias_row_set"), a.sem("const_loaded")
    with nc.Block() as block:
        @block.gpsimd
        def _(pool):
            link = Chain(pool, s_c)
            link(nc.gpsimd.memset(c.ones[:, :], 1.0))
            link(nc.gpsimd.memset(c.eps[:, :], EPS))
            link(nc.gpsimd.memset(c.ident[:, :], 0.0))
            link(nc.gpsimd.affine_select(out=c.ident[:, :], in_=c.ident[:, :], compare_op=ALU.not_equal,
                                         fill=1.0, base=0, pattern=[[-1, P]], channel_multiplier=1))
            link(nc.gpsimd.memset(c.causal[:, :], 0.0))
            link(nc.gpsimd.affine_select(out=c.causal[:, :], in_=c.causal[:, :], compare_op=ALU.is_ge,
                                         fill=LOW, base=0, pattern=[[-1, P]], channel_multiplier=1))
            link(nc.gpsimd.memset(c.tri[:, :], 1.0))
            link(nc.gpsimd.affine_select(out=c.tri[:, :], in_=c.tri[:, :], compare_op=ALU.is_ge,
                                         fill=0.0, base=0, pattern=[[1, P]], channel_multiplier=-1))
            for k in range(P // CH):
                v = c.tri[:, k * CH:(k + 1) * CH]
                link(nc.gpsimd.affine_select(out=v, in_=v, compare_op=ALU.is_ge, fill=0.0, base=-k * CH,
                                             pattern=[[0, CH]], channel_multiplier=1))
            link(nc.gpsimd.memset(c.reset[:, :], 1.0))
            link(nc.gpsimd.memset(c.reset[:, :].rearrange("p (c k) -> p c k", k=CH)[:, :, 0:1], 0.0))
            for t in (c.sel_b, c.sel_h):
                link(nc.gpsimd.memset(t[:, :, :], 0.0))
            link(nc.gpsimd.affine_select(out=c.sel_b[:, :, :], in_=c.sel_b[:, :, :], compare_op=ALU.not_equal,
                                         fill=1.0, base=0, pattern=[[-1, 8], [0, 8]], channel_multiplier=1))
            link(nc.gpsimd.affine_select(out=c.sel_h[:, :, :], in_=c.sel_h[:, :, :], compare_op=ALU.not_equal,
                                         fill=1.0, base=0, pattern=[[0, 8], [-1, 8]], channel_multiplier=1))
            link(nc.gpsimd.memset(c.pick[:, :, :], 0.0))
            link(nc.gpsimd.affine_select(out=c.pick[:, :, :], in_=c.pick[:, :, :], compare_op=ALU.not_equal,
                                         fill=1.0, base=0, pattern=[[-1, 8], [0, P]], channel_multiplier=1))
            link(nc.gpsimd.memset(c.selT[:, :], 1.0))
            link(nc.gpsimd.affine_select(out=c.selT[:, :], in_=c.selT[:, :], compare_op=ALU.is_ge, fill=0.0,
                                         base=0, pattern=[[-NH, TS]], channel_multiplier=1))
            link(nc.gpsimd.affine_select(out=c.selT[:, :], in_=c.selT[:, :], compare_op=ALU.is_ge, fill=0.0,
                                         base=NH - 1, pattern=[[NH, TS]], channel_multiplier=-1))
            link(nc.gpsimd.iota(c.iota[:, :], pattern=[[1, P]], base=0, channel_multiplier=0,
                                allow_small_or_imprecise_dtypes=True))

        @block.sync
        def _(sp):
            sp.dma_start(c.x[:, :, :], I["xT"]).then_inc(s_d, 16)
            for k in ("g_mix", "g_ffn", "g_ple", "g_final", "g_hgrn", "lbl", "pages"):
                sp.dma_start(c.small[k][:, :, :] if k == "lbl" else c.small[k][:, :], I[k]).then_inc(s_d, 16)
            sp.dma_start(c.rb[0:NB, :], I["rel_bias"]).then_inc(s_d, 16)
            sp.wait_ge(s_d, 144)

        @block.vector
        def _(dve):
            nc.vector.memset(c.rb[NB:NB + 1, :], OFF).then_inc(s_c2, 1)
            dve.wait_ge(s_c2, 1)


def project(nc, I, O, c, h, proj, ikT, vtok, hitok, iwtok):
    RING = 4
    with ExitStack() as ctx:
        a = Alloc(nc, ctx)
        ring = a.sb("w_ring", [P, RING, DC, P])
        wtok = a.sb("w_tok", [P, DC, 648])
        wik = a.sb("w_ik", [P, DC, HD])
        pp = a.ps("proj_ps", [P, 2, 2, 512])
        pt = a.ps("tok_ps", [P, 2, 2, 512])
        s_w = [a.sem(f"w_loaded{r}") for r in range(RING)]
        s_wt, s_wi = a.sem("wtok_loaded"), a.sem("wik_loaded")
        s_pt, s_ct = a.sem("tok_product"), a.sem("tok_copied")
        s_pp, s_cp = a.sem("tile_product"), a.sem("tile_copied")
        s_ik, s_ikc, s_o = a.sem("ik_product"), a.sem("ik_copied"), a.sem("kv_stored")
        block = ctx.enter_context(nc.Block())
        TT = NT + 1

        @block.sync
        def _(sp):
            sp.dma_start(wtok[:, :, :], I["w_tok"]).then_inc(s_wt, 16)
            for r in range(RING):
                sp.dma_start(ring[:, r], I["w_t"][r]).then_inc(s_w[r], 16)
            sp.dma_start(wik[:, :, :], I["w_ik"]).then_inc(s_wi, 16)
            with sp.Fori(1, MT // RING) as i:
                for r in range(RING):
                    sp.wait_ge(s_pp, (i - 1) * RING + r + 1)
                    sp.dma_start(ring[:, r], I["w_t"][i * RING + r]).then_inc(s_w[r], 16)
            sp.wait_ge(s_pp, MT - RING)
            sp.dma_start(ring[:, 0], I["w_t"][MT - 1]).then_inc(s_w[0], 16)
            sp.wait_ge(s_ct, 2 * TT)
            sp.dma_start(O["v_p"].rearrange("(t p) n -> p t n", p=P), vtok[:, 0:NT, :]).then_inc(s_o, 16)
            sp.dma_start(O["v_s"], vtok[0:TS, NT, :]).then_inc(s_o, 16)
            sp.wait_ge(s_cp, MT)
            sp.dma_start(O["kT"], proj[:, AK, :]).then_inc(s_o, 16)
            sp.wait_ge(s_ikc, 2)
            sp.dma_start(O["ikT"], ikT[0:HD, :]).then_inc(s_o, 16)
            sp.wait_ge(s_o, 64)

        @block.tensor
        def _(pe):
            pe.wait_ge(s_wt, 16)
            for t in range(TT):
                m = P if t < NT else TS
                if t >= 2:
                    pe.wait_ge(s_ct, 2 * (t - 1))
                for c0, c1, j in ((0, 324, 0), (324, 648, 1)):
                    for k in range(DC):
                        last = nc.tensor.matmul(pt[0:m, t % 2, j, 0:324], h[:, k, t * P:t * P + m],
                                                wtok[:, k, c0:c1], start=(k == 0), stop=(k == DC - 1))
                last.then_inc(s_pt, 1)

            def tile(r, done, base):
                pe.wait_ge(s_w[r], done)
                pe.wait_ge(s_cp, base)
                for j in range(2):
                    for k in range(DC):
                        last = nc.tensor.matmul(pp[:, r % 2, j, 0:HALF], ring[:, r, k, :],
                                                h[:, k, j * HALF:(j + 1) * HALF],
                                                start=(k == 0), stop=(k == DC - 1))
                last.then_inc(s_pp, 1)

            for r in range(RING):
                tile(r, 16, max(0, r - 1))
            with pe.Fori(1, MT // RING) as i:
                for r in range(RING):
                    tile(r, i * 16 + 16, i * RING + r - 1)
            tile(0, 16 * (MT // RING + 1), MT - 2)
            pe.wait_ge(s_wi, 16)
            pe.wait_ge(s_cp, MT - 1)
            for j in range(2):
                for k in range(DC):
                    last = nc.tensor.matmul(pp[0:HD, 1, j, 0:HALF], wik[:, k, :], h[:, k, j * HALF:(j + 1) * HALF],
                                            start=(k == 0), stop=(k == DC - 1))
            last.then_inc(s_ik, 1)

        @block.vector
        def _(dve):
            for t in range(TT):
                m = P if t < NT else TS
                dve.wait_ge(s_pt, t + 1)
                nc.vector.tensor_copy(vtok[0:m, t, :], pt[0:m, t % 2, 0, 0:P])
                nc.vector.tensor_copy(hitok[0:m, t, 0:196], pt[0:m, t % 2, 0, P:324]).then_inc(s_ct, 1)
                nc.vector.tensor_copy(hitok[0:m, t, 196:512], pt[0:m, t % 2, 1, 0:316])
                nc.vector.tensor_scalar(iwtok[0:m, t, :], pt[0:m, t % 2, 1, 316:324], NH ** -0.5, None,
                                        ALU.mult).then_inc(s_ct, 1)
            dve.wait_ge(s_ik, 1)
            nc.vector.tensor_copy(halves(ikT[0:HD, :]), pp[0:HD, 1, :, 0:HALF]).then_inc(s_ikc, 1)
            nc.vector.tensor_copy(halves(ikT[HD:P, :]), pp[0:HD, 1, :, 0:HALF]).then_inc(s_ikc, 1)

        @block.scalar
        def _(act):
            def evacuate(m, r, func):
                act.wait_ge(s_pp, m + 1)
                nc.scalar.activation(halves(proj[:, m, :]), pp[:, r, :, 0:HALF], func).then_inc(s_cp, 1)

            with act.Fori(0, (HF - 1) // 2) as i:
                for r in range(2):
                    evacuate(i * 2 + r, r, ACT.Identity)
            evacuate(HF - 1, 0, ACT.Identity)
            with act.Fori(0, (MT - HF) // 2) as i:
                for r in range(2):
                    evacuate(i * 2 + HF + r, (HF + r) % 2, ACT.Sigmoid)


def index_prompt(nc, c, proj, ikT, iwtok, maskp):
    with ExitStack() as ctx:
        a = Alloc(nc, ctx)
        ps = a.ps("ix_ps", [P, 4, 512])
        rl = a.sb("ix_relu", [P, 4, TP])
        sc = a.sb("ix_score", [P, 2, TP])
        wk = a.sb("ix_work", [P, TP])
        m8 = a.sb("ix_max8", [P, 8])
        s_ps, s_rl, s_ac, s_v = (a.sem("ix_" + x) for x in ("product", "relu", "accumulated", "chain"))
        block = ctx.enter_context(nc.Block())

        @block.tensor
        def _(pe):
            n = 0
            for t in range(1, NT):
                S = (t + 1) * P
                for h in range(NH):
                    r = HD * (h % 2)
                    if n >= 4:
                        pe.wait_ge(s_rl, n - 3)
                    nc.tensor.matmul(ps[:, n % 4, 0:S], proj[r:r + HD, IQ + h // 2, t * P:(t + 1) * P],
                                     ikT[r:r + HD, 0:S], start=True, stop=True).then_inc(s_ps, 1)
                    n += 1

        @block.scalar
        def _(act):
            n = 0
            for t in range(1, NT):
                S = (t + 1) * P
                for h in range(NH):
                    act.wait_ge(s_ps, n + 1)
                    if n >= 4:
                        act.wait_ge(s_ac, n - 3)
                    nc.scalar.activation(rl[:, n % 4, 0:S], ps[:, n % 4, 0:S], ACT.Relu,
                                         scale=HD ** -0.5).then_inc(s_rl, 1)
                    n += 1

        @block.vector
        def _(dve):
            link = Chain(dve, s_v)
            nc.vector.memset(maskp[:, 0, :], 0.0)
            n = 0
            for t in range(1, NT):
                S = (t + 1) * P
                for h in range(NH):
                    dve.wait_ge(s_rl, n + 1)
                    if h == 0:
                        ins = nc.vector.tensor_scalar(sc[:, 0, 0:S], rl[:, n % 4, 0:S], iwtok[:, t, 0:1], None,
                                                      ALU.mult)
                    else:
                        ins = nc.vector.scalar_tensor_tensor(out=sc[:, h % 2, 0:S], in0=rl[:, n % 4, 0:S],
                                                             scalar=iwtok[:, t, h:h + 1],
                                                             in1=sc[:, (h - 1) % 2, 0:S],
                                                             op0=ALU.mult, op1=ALU.add)
                    n += 1
                    ins.then_inc(s_ac, 1)
                    dve.wait_ge(s_ac, n)
                f = sc[:, 1, :]
                link(nc.vector.tensor_tensor(f[:, t * P:S], f[:, t * P:S], c.causal[:, :], ALU.add))
                for k in range(TOPP // 8):
                    src = f if k == 0 else wk
                    link(nc.vector.max(m8[:, :], src[:, 0:S]))
                    link(nc.vector.match_replace(wk[:, 0:S], m8[:, :], src[:, 0:S], SENT))
                link(nc.vector.tensor_scalar(maskp[:, t, 0:S], wk[:, 0:S], SENT, OFF, ALU.not_equal, ALU.mult))


def bias_table(nc, c, onehot, rev, scratch, toep):
    with ExitStack() as ctx:
        a = Alloc(nc, ctx)
        pb = a.ps("bias_ps", [P, 3, 512])
        oh = a.sb("bias_onehot", [NB + 1, REV])
        s_h = a.sem("bias_onehot_loaded")
        s_p, s_c, s_o, s_i = (a.sem("bias_" + x) for x in ("product", "copied", "stored", "loaded"))
        block = ctx.enter_context(nc.Block())
        W = REV // 3

        @block.tensor
        def _(pe):
            pe.wait_ge(s_h, 16)
            for j in range(3):
                last = nc.tensor.matmul(pb[0:NH, j, 0:W], c.rb[:, :], oh[:, j * W:(j + 1) * W],
                                        start=True, stop=True)
            last.then_inc(s_p, 1)

        @block.vector
        def _(dve):
            dve.wait_ge(s_p, 1)
            nc.vector.tensor_copy(rev[:, :].rearrange("h (j w) -> h j w", j=3), pb[0:NH, :, 0:W]).then_inc(s_c, 1)

        @block.sync
        def _(sp):
            sp.dma_start(oh[:, :], onehot).then_inc(s_h, 16)
            sp.wait_ge(s_c, 1)
            sp.dma_start(scratch[:, :, 0:SK - 1],
                         rev[:, REV - SK + 1:REV].unsqueeze(1).to_broadcast([NH, P, SK - 1])).then_inc(s_o, 16)
            sp.wait_ge(s_o, 16)
            src = bass.AP(tensor=scratch.tensor, offset=P - 1, ap=[[SK - 1, P], [P * SK, NH], [1, TP]])
            sp.dma_start(toep[:, :, :], src).then_inc(s_i, 16)
            sp.wait_ge(s_i, 16)


def attend_prompt(nc, c, proj, vtok, maskp, toep, attT):
    with ExitStack() as ctx:
        a = Alloc(nc, ctx)
        pl = a.ps("at_logit_ps", [P, 2, 512])
        px = a.ps("at_turn_ps", [P, 2, 512])
        po = a.ps("at_out_ps", [P, 2, 512])
        pa = a.ps("at_att_ps", [P, 1, 512])
        lg = a.sb("at_logit", [P, 2, TP])
        lm = a.sb("at_masked", [P, 2, TP])
        pr = a.sb("at_prob", [P, 2, TP])
        pT = a.sb("at_probT", [P, 2, TP])
        mx = a.sb("at_max", [P, NT, NH])
        nm = a.sb("at_negmax", [P, NT, NH])
        sm = a.sb("at_sum", [P, NT, NH])
        rc = a.sb("at_recip", [P, NT, NH])
        at = a.sb("at_att", [P, 2, 512])
        s_l, s_b, s_m, s_n, s_e, s_x, s_c, s_o, s_r, s_a, s_t, s_f = (a.sem("at_" + x) for x in (
            "product", "biased", "masked", "negmax_made", "exp", "turned", "turn_copied", "pv", "recip_made",
            "normalised", "att_turned", "att_copied"))
        block = ctx.enter_context(nc.Block())
        work = [(t, m, g) for t in range(NT) for m in range(4) for g in range(2)]

        @block.tensor
        def _(pe):
            def logits(n):
                t, m, g = work[n]
                S = (t + 1) * P
                if n >= 2:
                    pe.wait_ge(s_b, n - 1)
                nc.tensor.matmul(pl[:, n % 2, 0:S], proj[HD * g:HD * g + HD, AQ + m, t * P:S],
                                 proj[HD * g:HD * g + HD, AK, 0:S], start=True, stop=True).then_inc(s_l, 1)

            def turn(n):
                t, m, g = work[n]
                pe.wait_ge(s_e, n + 1)
                if n >= 2:
                    pe.wait_ge(s_c, n - 1)
                for k in range(t + 1):
                    last = nc.tensor.transpose(px[:, n % 2, k * P:(k + 1) * P], pr[:, n % 2, k * P:(k + 1) * P],
                                               c.ident[:, :])
                last.then_inc(s_x, 1)

            def pv(n):
                t, m, g = work[n]
                pe.wait_ge(s_c, n + 1)
                if n % 8 == 0 and t >= 2:
                    pe.wait_ge(s_a, t - 1)
                o = (2 * m + g) * HD
                for k in range(t + 1):
                    last = nc.tensor.matmul(po[:, t % 2, o:o + HD], pT[:, n % 2, k * P:(k + 1) * P],
                                            vtok[:, k, g * HD:g * HD + HD], start=(k == 0), stop=(k == t))
                last.then_inc(s_o, 1)

            def att(t):
                pe.wait_ge(s_a, t + 1)
                if t >= 1:
                    pe.wait_ge(s_f, t)
                for m in range(4):
                    last = nc.tensor.transpose(pa[:, 0, m * P:(m + 1) * P], at[:, t % 2, m * P:(m + 1) * P],
                                               c.ident[:, :])
                last.then_inc(s_t, 1)

            logits(0)
            for n in range(len(work)):
                if n + 1 < len(work):
                    logits(n + 1)
                turn(n)
                pv(n)
                if n % 8 == 7:
                    att(n // 8)

        @block.vector
        def _(dve):
            def score(n):
                t, m, g = work[n]
                S = (t + 1) * P
                h = m + 4 * g
                u = TP - S
                dve.wait_ge(s_l, n + 1)
                nc.vector.scalar_tensor_tensor(out=lg[:, n % 2, 0:S], in0=pl[:, n % 2, 0:S], scalar=HD ** -0.5,
                                               in1=toep[:, h, u:TP], op0=ALU.mult, op1=ALU.add).then_inc(s_b, 1)
                dve.wait_ge(s_b, n + 1)
                if n >= 2:
                    dve.wait_ge(s_e, n - 1)
                nc.vector.tensor_tensor_reduce(out=lm[:, n % 2, 0:S], in0=lg[:, n % 2, 0:S],
                                               in1=maskp[:, t, 0:S], scale=1.0, scalar=-3.0e38, op0=ALU.add,
                                               op1=ALU.max, accum_out=mx[:, t, h:h + 1]).then_inc(s_m, 1)
                dve.wait_ge(s_m, n + 1)
                nc.vector.tensor_scalar(nm[:, t, h:h + 1], mx[:, t, h:h + 1], -1.0, None, ALU.mult).then_inc(s_n, 1)

            def turned(n):
                t, m, g = work[n]
                S = (t + 1) * P
                dve.wait_ge(s_x, n + 1)
                if n >= 2:
                    dve.wait_ge(s_o, n - 1)
                nc.vector.tensor_copy(pT[:, n % 2, 0:S], px[:, n % 2, 0:S]).then_inc(s_c, 1)

            score(0)
            for n in range(len(work)):
                if n + 1 < len(work):
                    score(n + 1)
                turned(n)
                if n % 8 == 7:
                    t = n // 8
                    dve.wait_ge(s_e, n + 1)
                    nc.vector.reciprocal(rc[:, t, :], sm[:, t, :]).then_inc(s_r, 1)
                    dve.wait_ge(s_r, t + 1)
                    dve.wait_ge(s_o, n + 1)
                    if t >= 2:
                        dve.wait_ge(s_t, t - 1)
                    r = rc[:, t, :].rearrange("p (g m) -> p m g", g=2).unsqueeze(3).to_broadcast([P, 4, 2, HD])
                    nc.vector.tensor_tensor(at[:, t % 2, :].rearrange("p (m g d) -> p m g d", m=4, g=2),
                                            po[:, t % 2, :].rearrange("p (m g d) -> p m g d", m=4, g=2),
                                            r, ALU.mult).then_inc(s_a, 1)
                    dve.wait_ge(s_t, t + 1)
                    nc.vector.tensor_copy(attT[:, :, t * P:(t + 1) * P],
                                          pa[:, 0, :].rearrange("p (m n) -> p m n", m=4)).then_inc(s_f, 1)

        @block.scalar
        def _(act):
            for n, (t, m, g) in enumerate(work):
                S = (t + 1) * P
                h = m + 4 * g
                act.wait_ge(s_n, n + 1)
                if n >= 2:
                    act.wait_ge(s_x, n - 1)
                nc.scalar.activation(pr[:, n % 2, 0:S], lm[:, n % 2, 0:S], ACT.Exp, bias=nm[:, t, h:h + 1],
                                     accum_out=sm[:, t, h:h + 1]).then_inc(s_e, 1)


def sample_attention(nc, I, c, proj, ikT, vtok, iwtok, rev, attT):
    R = TS * NH
    with ExitStack() as ctx:
        a = Alloc(nc, ctx)
        kx = a.sb("sa_kidx", [HD, 2, NPG, PG])
        kc = a.sb("sa_k", [P, 2, NPG, PG])
        vc = a.sb("sa_v", [P, 4, NPG, P])
        qi = a.sb("sa_iq", [HD, TS, TS, NH])
        qa = a.sb("sa_q", [P, TS, TS, NH])
        wx = a.sb("sa_iw", [TS, TS, NH])
        wb = a.sb("sa_iwT", [R, TS])
        rl = a.sb("sa_relu", [R, L])
        wk = a.sb("sa_work", [TS, L])
        m8 = a.sb("sa_max8", [TS, 8])
        mk = a.sb("sa_mask", [TS, L])
        mx = a.sb("sa_max", [R, 4])
        pr = a.sb("sa_prob", [R, L])
        pT = a.sb("sa_probT", [P, NPG, R])
        pn = a.sb("sa_new", [R, TS])
        pnT = a.sb("sa_newT", [TS, R])
        pS = a.ps("sa_ps", [P, 3, 512])
        pC = a.ps("sa_score_ps", [P, 3, 512])
        pX = a.ps("sa_turn_ps", [P, 1, 512])
        pO = a.ps("sa_out_ps", [P, 1, 512])
        s_xl, s_kl = [a.sem(f"sa_kidx_loaded{i}") for i in range(2)], [a.sem(f"sa_k_loaded{i}") for i in range(2)]
        s_vl = [a.sem(f"sa_v_loaded{i}") for i in range(4)]
        s_z, s_g, s_q = a.sem("sa_zeroed"), a.sem("sa_iwmask"), a.sem("sa_qblocks")
        s_px, s_pk, s_v, s_wT, s_e = (a.sem("sa_" + x) for x in ("ixprod", "kprod", "dve_chain", "iwturned", "exp"))
        s_sc, s_rl, s_cp, s_mk, s_tn, s_tc, s_ov = (a.sem("sa_" + x) for x in (
            "scores", "relued", "iwT_copied", "mask_made", "turned", "turn_copied", "out"))
        s_nm = a.sem("sa_negmax")
        block = ctx.enter_context(nc.Block())
        pSf = pS[:, :, :].rearrange("p a b -> p (a b)")
        pCf = pC[:, :, :].rearrange("p a b -> p (a b)")
        pieces = ((0, 512), (512, 1024), (1024, L))

        def load(eng, src, dst, b, s):
            for g in range(NPG):
                page = eng.value_load(c.small["pages"][0:1, b * NPG + g:b * NPG + g + 1], min_val=0, max_val=79)
                eng.dma_start(dst[:, g, :], src[bass.ds(page, 1), :, :].rearrange("a p n -> p (a n)")).then_inc(s, 16)

        @block.sync
        def _(sp):
            for b in range(TS):
                if b >= 2:
                    sp.wait_ge(s_px, b - 1)
                load(sp, I["kidxT"], kx[:, b % 2], b, s_xl[b % 2])
            for b in range(TS):
                if b >= 4:
                    sp.wait_ge(s_ov, b - 3)
                load(sp, I["vC"], vc[:, b % 4], b, s_vl[b % 4])

        @block.gpsimd
        def _(pool):
            nc.gpsimd.memset(qi[:, :, :, :], 0.0).then_inc(s_z, 1)
            nc.gpsimd.memset(qa[:, :, :, :], 0.0).then_inc(s_z, 1)
            nc.gpsimd.tensor_tensor(wx[:, :, :], c.sel_b[:, :, :],
                                    iwtok[0:TS, NT, :].unsqueeze(1).to_broadcast([TS, TS, NH]), ALU.mult).then_inc(s_g, 1)

        @block.scalar
        def _(act):
            for b in range(TS):
                if b >= 2:
                    act.wait_ge(s_pk, b - 1)
                load(act, I["kT"], kc[:, b % 2], b, s_kl[b % 2])
                if b == 1:
                    act.wait_ge(s_px, TS)
                    nc.scalar.activation(rl[:, :], pSf[0:R, 0:L], ACT.Relu, scale=HD ** -0.5).then_inc(s_rl, 1)
            act.wait_ge(s_nm, 1)
            nc.scalar.activation(pr[:, :], pSf[0:R, 0:L], ACT.Exp, bias=mx[:, 1:2],
                                 accum_out=mx[:, 2:3]).then_inc(s_e, 1)

        @block.vector
        def _(dve):
            link = Chain(dve, s_v)
            dve.wait_ge(s_z, 2)
            for h in range(NH):
                r = HD * (h % 2)
                d = qi[:, :, :, :].rearrange("p a b h -> p (a b h)")[:, h:h + 72 * 7 + 1:72]
                nc.vector.tensor_copy(d, proj[r:r + HD, IQ + h // 2, TP:N]).then_inc(s_q, 1)
            for m in range(4):
                for g in range(2):
                    h = m + 4 * g
                    d = qa[:, :, :, :].rearrange("p a b h -> p (a b h)")[HD * g:HD * g + HD, h:h + 72 * 7 + 1:72]
                    nc.vector.tensor_scalar(d, proj[HD * g:HD * g + HD, AQ + m, TP:N], HD ** -0.5, None,
                                            ALU.mult).then_inc(s_q, 1)
            dve.wait_ge(s_wT, 1)
            nc.vector.tensor_copy(wb[:, :], pX[0:R, 0, 0:TS]).then_inc(s_cp, 1)
            dve.wait_ge(s_sc, 1)
            for k in range(TOPS // 8):
                src = pCf[0:TS, 0:L] if k == 0 else wk[:, :]
                link(nc.vector.max(m8[:, :], src))
                link(nc.vector.match_replace(wk[:, :], m8[:, :], src, SENT))
            nc.vector.tensor_scalar(mk[:, :], wk[:, :], SENT, OFF, ALU.not_equal, ALU.mult).then_inc(s_mk, 1)
            dve.wait_ge(s_pk, TS + 1)
            link(nc.vector.tensor_reduce(mx[:, 0:1], pSf[0:R, 0:L], X, ALU.max))
            nc.vector.tensor_scalar(mx[:, 1:2], mx[:, 0:1], -1.0, None, ALU.mult).then_inc(s_nm, 1)
            dve.wait_ge(s_e, 1)
            link(nc.vector.reciprocal(mx[:, 3:4], mx[:, 2:3]))
            link(nc.vector.tensor_scalar(pr[:, :], pr[:, :], mx[:, 3:4], None, ALU.mult))
            link(nc.vector.tensor_scalar(pn[:, :], c.selT[:, :], pr[:, PAST:L], None, ALU.mult))
            dve.wait_ge(s_tn, 1)
            nc.vector.tensor_copy(pT[:, :, :], pX[:, 0, :].rearrange("p (g r) -> p g r", r=R)).then_inc(s_tc, 1)
            dve.wait_ge(s_tn, 2)
            nc.vector.tensor_copy(pnT[:, :], pC[0:TS, 0, 0:R]).then_inc(s_tc, 1)
            dve.wait_ge(s_ov, TS)
            for m in range(4):
                for g in range(2):
                    h = m + 4 * g
                    src = pO[HD * g:HD * g + HD, 0, 0:R].rearrange("p (b h) -> p b h", h=NH)[:, :, h]
                    nc.vector.tensor_copy(attT[HD * g:HD * g + HD, m, TP:N], src).then_inc(s_tc, 1)

        @block.tensor
        def _(pe):
            pe.wait_ge(s_g, 1)
            nc.tensor.transpose(pX[0:R, 0, 0:TS], wx[:, :, :].rearrange("p a b -> p (a b)"),
                                c.ident[0:TS, 0:TS]).then_inc(s_wT, 1)
            pe.wait_ge(s_q, 16)
            for b in range(TS):
                pe.wait_ge(s_xl[b % 2], 16 * NPG * (b // 2 + 1))
                q = qi[:, b, :, :].rearrange("p b h -> p (b h)")
                for s0, s1 in pieces:
                    k = (kx[:, b % 2].rearrange("p g n -> p (g n)")[:, s0:s1] if s0 < PAST
                         else ikT[0:HD, TP + b:TP + b + 1])
                    last = nc.tensor.matmul(pSf[0:R, s0:s1], q, k, start=(b == 0), stop=(b == TS - 1))
                last.then_inc(s_px, 1)
            pe.wait_ge(s_rl, 1)
            pe.wait_ge(s_cp, 1)
            for s0, s1 in pieces:
                last = nc.tensor.matmul(pCf[0:TS, s0:s1], wb[:, :], rl[:, s0:s1], start=True, stop=True)
            last.then_inc(s_sc, 1)
            for b in range(TS):
                pe.wait_ge(s_kl[b % 2], 16 * NPG * (b // 2 + 1))
                q = qa[:, b, :, :].rearrange("p b h -> p (b h)")
                for s0, s1 in pieces:
                    k = (kc[:, b % 2].rearrange("p g n -> p (g n)")[:, s0:s1] if s0 < PAST
                         else proj[:, AK, TP + b:TP + b + 1])
                    last = nc.tensor.matmul(pSf[0:R, s0:s1], q, k, start=(b == 0), stop=False)
                last.then_inc(s_pk, 1)
            pe.wait_ge(s_mk, 1)
            for s0, s1 in pieces:
                nc.tensor.matmul(pSf[0:R, s0:s1], c.sel_h[:, :, :].rearrange("p a b -> p (a b)"), rev[:, s0:s1],
                                 start=False, stop=False)
                last = nc.tensor.matmul(pSf[0:R, s0:s1], c.sel_b[:, :, :].rearrange("p a b -> p (a b)"), mk[:, s0:s1],
                                        start=False, stop=True)
            last.then_inc(s_pk, 1)
            pe.wait_ge(s_v, 2 * (TOPS // 8) + 4)
            for g in range(NPG):
                last = nc.tensor.transpose(pX[:, 0, g * R:(g + 1) * R], pr[:, g * PG:(g + 1) * PG], c.ident[0:R, 0:R])
            last.then_inc(s_tn, 1)
            nc.tensor.transpose(pC[0:TS, 0, 0:R], pn[:, :], c.ident[0:R, 0:R]).then_inc(s_tn, 1)
            pe.wait_ge(s_tc, 2)
            nc.tensor.matmul(pO[:, 0, 0:R], vtok[0:TS, NT, :], pnT[:, :], start=True, stop=False,
                             skip_group_check=True)
            for b in range(TS):
                pe.wait_ge(s_vl[b % 4], 16 * NPG * (b // 4 + 1))
                for g in range(NPG):
                    last = nc.tensor.matmul(pO[:, 0, b * NH:(b + 1) * NH], vc[:, b % 4, g, :],
                                            pT[:, g, b * NH:(b + 1) * NH], start=False,
                                            stop=(b == TS - 1 and g == NPG - 1), skip_group_check=True)
                last.then_inc(s_ov, 1)


def hgrn(nc, I, O, c, proj, hitok, hgoT):
    M = CH // 2 - 1
    RS = 2 * (P // CH) + 1
    with ExitStack() as ctx:
        a = Alloc(nc, ctx)
        lb = a.sb("hg_lb", [P, 8, HG])
        kk = a.sb("hg_k", [P, HG, N])
        ff = proj[:, HF:HF + HG, :]
        q1, k1 = proj[:, AQ:AQ + HG, 0:TP], proj[:, IQ:IQ + HG, 0:TP]
        bb = a.sb("hg_b", [P, HG, TP])
        k2T = bb[:, :, :].rearrange("p h (t n) -> p h t n", t=NT)
        dd = a.sb("hg_d", [P, HG, N])
        q2 = a.sb("hg_q2", [P, HG, TP])
        el = a.sb("hg_decay", [P, HG, NCH])
        be = a.sb("hg_b_end", [P, HG, NCH])
        AT = a.sb("hg_scores", [P, 2, HG, P])
        st = a.sb("hg_state", [P, RS, HG, P])
        oT = hgoT
        ss = a.sb("hg_sample_state", [P, TS, HG, P])
        kv = a.sb("hg_sample_kv", [P, 2, HG, P])
        epsc = a.sb("hg_eps", [P, 1])
        pA = a.ps("hg_ps_a", [P, 2, 512])
        pB = a.ps("hg_ps_b", [P, 2, 512])
        pO = a.ps("hg_ps_o", [P, 4, 512])
        s_v, s_a, s_d, s_o = a.sem("hg_dve_chain"), a.sem("hg_act"), a.sem("hg_loaded"), a.sem("hg_stored")
        s_lb, s_f, s_b, s_d1, s_d2, s_w = (a.sem("hg_" + x) for x in (
            "lbdiff", "f_made", "b_made", "mid_diff", "end_diff", "weighted"))
        s_x, s_xc, s_s, s_sc, s_u, s_st, s_oo, s_oc = (a.sem("hg_" + x) for x in (
            "turned", "turn_copied", "scores_made", "scores_masked", "kv_made", "state", "out_made", "out_copied"))
        s_vc, s_n = a.sem("hg_v_used"), a.sem("hg_norm_chain")
        s_vb, s_ss, s_so, s_sq, s_ms, s_rt, s_e = (a.sem("hg_" + x) for x in (
            "v_spread", "sample_state_made", "sample_out", "squared", "mean", "root", "exps"))

        def chunks(t, h):
            return t[:, h, 0:TP].rearrange("p (c k) -> p c k", k=CH)

        with nc.Block() as block:
            @block.sync
            def _(sp):
                sp.dma_start(ss[:, :, :, :], I["state"]).then_inc(s_d, 16)

            @block.scalar
            def _(act):
                act.wait_ge(s_lb, 1)
                nc.scalar.activation(lb[:, 3:5, :], lb[:, 1:3, :], ACT.Exp).then_inc(s_a, 1)
                act.wait_ge(s_f, HG)
                for h in range(HG):
                    nc.scalar.activation(dd[:, h, 0:TP], ff[:, h, 0:TP], ACT.Ln).then_inc(s_a, 1)
                for h in range(HG):
                    act.wait_ge(s_d1, h + 1)
                    nc.scalar.activation(q1[:, h, :], dd[:, h, 0:TP], ACT.Exp).then_inc(s_e, 1)
                    nc.scalar.activation(k1[:, h, :], dd[:, h, 0:TP], ACT.Exp, scale=-1.0).then_inc(s_e, 1)
                    nc.scalar.activation(q2[:, h, :], bb[:, h, :], ACT.Exp).then_inc(s_e, 1)
                    nc.scalar.activation(el[:, h, :], chunks(bb, h)[:, :, CH - 1], ACT.Exp).then_inc(s_e, 1)
                for h in range(HG):
                    act.wait_ge(s_d2, h + 1)
                    nc.scalar.activation(dd[:, h, 0:TP], bb[:, h, :], ACT.Exp, scale=-1.0).then_inc(s_e, 1)

            @block.vector
            def _(dve):
                link = Chain(dve, s_v)
                l = c.small["lbl"]
                link(nc.vector.tensor_tensor(lb[:, 0, :], l[:, 0, :], l[:, 1, :], ALU.max))
                link(nc.vector.tensor_tensor(lb[:, 1, :], l[:, 0, :], lb[:, 0, :], ALU.subtract))
                nc.vector.tensor_tensor(lb[:, 2, :], l[:, 1, :], lb[:, 0, :], ALU.subtract).then_inc(s_lb, 1)
                dve.wait_ge(s_a, 1)
                link(nc.vector.tensor_tensor(lb[:, 5, :], lb[:, 3, :], lb[:, 4, :], ALU.add))
                link(nc.vector.reciprocal(lb[:, 6, :], lb[:, 5, :]))
                link(nc.vector.tensor_tensor(lb[:, 7, :], lb[:, 3, :], lb[:, 6, :], ALU.mult))
                link(nc.vector.tensor_scalar(lb[:, 0, :], lb[:, 7, :], -1.0, 1.0, ALU.mult, ALU.add))
                for h in range(HG):
                    nc.vector.tensor_scalar(ff[:, h, :], proj[:, HF + h, :], lb[:, 0, h:h + 1], lb[:, 7, h:h + 1],
                                            ALU.mult, ALU.add).then_inc(s_f, 1)
                dve.wait_ge(s_f, HG)
                for h in range(HG):
                    nc.vector.tensor_scalar(kk[:, h, :], ff[:, h, :], -1.0, 1.0, ALU.mult, ALU.add).then_inc(s_f, 1)
                for h in range(HG):
                    dve.wait_ge(s_a, 2 + h)
                    nc.vector.tensor_tensor_scan(bb[:, h, :], c.reset[:, :], dd[:, h, 0:TP], 0.0, ALU.mult,
                                                 ALU.add).then_inc(s_b, 1)
                for h in range(HG):
                    dve.wait_ge(s_b, h + 1)
                    b = chunks(bb, h)
                    nc.vector.tensor_tensor(chunks(dd, h), b, b[:, :, M:M + 1].to_broadcast([P, NCH, CH]),
                                            ALU.subtract).then_inc(s_d1, 1)
                dve.wait_ge(s_f, 2 * HG)
                for h in range(HG):
                    dve.wait_ge(s_e, 4 * h + 4)
                    b = chunks(bb, h)
                    link(nc.vector.tensor_copy(be[:, h, :], b[:, :, CH - 1]))
                    nc.vector.tensor_tensor(b, b, be[:, h, :].unsqueeze(2).to_broadcast([P, NCH, CH]),
                                            ALU.subtract).then_inc(s_d2, 1)
                    nc.vector.tensor_tensor(q1[:, h, :], q1[:, h, :], proj[:, HQ + h, 0:TP], ALU.mult).then_inc(s_w, 1)
                    nc.vector.tensor_tensor(k1[:, h, :], k1[:, h, :], kk[:, h, 0:TP], ALU.mult).then_inc(s_w, 1)
                    nc.vector.tensor_tensor(q2[:, h, :], q2[:, h, :], proj[:, HQ + h, 0:TP], ALU.mult).then_inc(s_w, 1)
                for h in range(HG):
                    dve.wait_ge(s_e, 4 * HG + h + 1)
                    nc.vector.tensor_tensor(dd[:, h, 0:TP], dd[:, h, 0:TP], kk[:, h, 0:TP], ALU.mult).then_inc(s_w, 1)
                dve.wait_ge(s_w, 4 * HG)

        s_m = a.sem("hg_zero_state")
        with nc.Block() as block:
            @block.tensor
            def _(pe):
                for h in range(HG):
                    if h >= 2:
                        pe.wait_ge(s_xc, h - 1)
                    for t in range(NT):
                        last = nc.tensor.transpose(pA[:, h % 2, t * P:(t + 1) * P], dd[:, h, t * P:(t + 1) * P],
                                                   c.ident[:, :])
                    last.then_inc(s_x, 1)
                pe.wait_ge(s_xc, HG)

                def kv_of(n):
                    t, r = n * CH // P, n * CH % P
                    if n >= 2:
                        pe.wait_ge(s_st, (n - 1) * HG)
                    for h in range(HG):
                        last = nc.tensor.matmul(pB[:, n % 2, h * P:(h + 1) * P], k2T[r:r + CH, h, t, :],
                                                hitok[r:r + CH, t, h * P:(h + 1) * P], start=True, stop=True)
                    last.then_inc(s_u, 1)

                def scores(t):
                    if t >= 2:
                        pe.wait_ge(s_sc, t - 1)
                    for h in range(HG):
                        last = nc.tensor.matmul(pA[:, t % 2, h * P:(h + 1) * P], k1[:, h, t * P:(t + 1) * P],
                                                q1[:, h, t * P:(t + 1) * P], start=True, stop=True)
                    last.then_inc(s_s, 1)

                def out(t):
                    pe.wait_ge(s_sc, t + 1)
                    pe.wait_ge(s_st, (4 * t + 3) * HG)
                    if t >= 2:
                        pe.wait_ge(s_oc, t - 1)
                    for h in range(HG):
                        o = pO[:, t % 2, h * P:(h + 1) * P]
                        nc.tensor.matmul(o, hitok[:, t, h * P:(h + 1) * P], AT[:, t % 2, h, :],
                                         start=True, stop=False, skip_group_check=True)
                        for j in range(P // CH):
                            n = t * (P // CH) + j
                            last = nc.tensor.matmul(o[:, j * CH:(j + 1) * CH], st[:, n % RS, h, :],
                                                    q2[:, h, n * CH:(n + 1) * CH], start=False,
                                                    stop=(j == P // CH - 1), skip_group_check=True)
                    last.then_inc(s_oo, 1)

                for t in range(NT):
                    scores(t)
                    for j in range(P // CH):
                        kv_of(t * (P // CH) + j)
                    out(t)
                for b in range(TS):
                    if b >= 2:
                        pe.wait_ge(s_vc, b - 1)
                    nc.tensor.matmul(pO[:, 2 + b % 2, :], c.pick[:, b, :], hitok[0:TS, NT, :],
                                     start=True, stop=True).then_inc(s_vb, 1)
                pe.wait_ge(s_ss, TS)
                pe.wait_ge(s_st, NCH * HG)
                for b in range(TS):
                    for h in range(HG):
                        last = nc.tensor.matmul(pB[:, 0, h * TS + b:h * TS + b + 1], ss[:, b, h, :],
                                                proj[:, HQ + h, TP + b:TP + b + 1], start=True, stop=True)
                last.then_inc(s_so, 1)

            @block.vector
            def _(dve):
                nc.vector.memset(st[:, 0, :, :], 0.0).then_inc(s_m, 1)
                nc.vector.memset(epsc[:, :], EPS).then_inc(s_m, 1)
                for h in range(HG):
                    dve.wait_ge(s_x, h + 1)
                    nc.vector.tensor_copy(k2T[:, h, :, :], pA[:, h % 2, :].rearrange("p (t n) -> p t n", t=NT)
                                          ).then_inc(s_xc, 1)
                dve.wait_ge(s_m, 2)
                for t in range(NT):
                    dve.wait_ge(s_s, t + 1)
                    if t >= 2:
                        dve.wait_ge(s_oo, t - 1)
                    for h in range(HG):
                        ins = nc.vector.scalar_tensor_tensor(out=AT[:, t % 2, h, :], in0=pA[:, t % 2, h * P:(h + 1) * P],
                                                             scalar=3.0e38, in1=c.tri[:, :], op0=ALU.min, op1=ALU.mult)
                    ins.then_inc(s_sc, 1)
                    for j in range(P // CH):
                        n = t * (P // CH) + j
                        dve.wait_ge(s_u, n + 1)
                        if n >= 1:
                            dve.wait_ge(s_st, n * HG)
                        for h in range(HG):
                            nc.vector.scalar_tensor_tensor(out=st[:, (n + 1) % RS, h, :], in0=st[:, n % RS, h, :],
                                                           scalar=el[:, h, n:n + 1], in1=pB[:, n % 2, h * P:(h + 1) * P],
                                                           op0=ALU.mult, op1=ALU.add).then_inc(s_st, 1)
                    dve.wait_ge(s_oo, t + 1)
                    nc.vector.tensor_copy(oT[:, :, t * P:(t + 1) * P], pO[:, t % 2, :].rearrange("p (h n) -> p h n", h=HG)
                                          ).then_inc(s_oc, 1)
                dve.wait_ge(s_d, 16)
                for b in range(TS):
                    dve.wait_ge(s_vb, b + 1)
                    if b >= 2:
                        dve.wait_ge(s_ss, b - 1)
                    for h in range(HG):
                        ins = nc.vector.tensor_scalar(kv[:, b % 2, h, :], pO[:, 2 + b % 2, h * P:(h + 1) * P],
                                                      kk[:, h, TP + b:TP + b + 1], None, ALU.mult)
                    ins.then_inc(s_vc, 1)
                    dve.wait_ge(s_vc, b + 1)
                    for h in range(HG):
                        ins = nc.vector.scalar_tensor_tensor(out=ss[:, b, h, :], in0=ss[:, b, h, :],
                                                             scalar=ff[:, h, TP + b:TP + b + 1], in1=kv[:, b % 2, h, :],
                                                             op0=ALU.mult, op1=ALU.add)
                    ins.then_inc(s_ss, 1)
                dve.wait_ge(s_so, 1)
                nc.vector.tensor_copy(oT[:, :, TP:N], pB[:, 0, 0:HG * TS].rearrange("p (h b) -> p h b", h=HG)
                                      ).then_inc(s_oc, 1)
                dve.wait_ge(s_oc, NT + 1)

            @block.sync
            def _(sp):
                sp.wait_ge(s_st, NCH * HG)
                sp.dma_start(O["hg_p"], st[:, NCH % RS, :, :]).then_inc(s_o, 16)
                sp.wait_ge(s_ss, TS)
                sp.dma_start(O["hg_s"], ss[:, :, :, :]).then_inc(s_o, 16)
                sp.wait_ge(s_o, 32)

        sq, rt, sg = kk, ff, dd
        with nc.Block() as block:
            @block.scalar
            def _(act):
                for h in range(HG):
                    nc.scalar.activation(sq[:, h, :], oT[:, h, :], ACT.Square).then_inc(s_sq, 1)
                for h in range(HG):
                    act.wait_ge(s_ms, h + 1)
                    nc.scalar.activation(halves(rt[:, h, :]), pO[:, 2 * (h % 2):2 * (h % 2) + 2, 0:HALF], ACT.Sqrt,
                                         scale=1.0 / P, bias=epsc[:, 0:1]).then_inc(s_rt, 1)
                for h in range(HG):
                    nc.scalar.activation(sg[:, h, :], proj[:, HGT + h, :], ACT.Sigmoid).then_inc(s_rt, 1)

            @block.tensor
            def _(pe):
                for h in range(HG):
                    pe.wait_ge(s_sq, h + 1)
                    if h >= 2:
                        pe.wait_ge(s_rt, h - 1)
                    for j in range(2):
                        last = nc.tensor.matmul(pO[:, 2 * (h % 2) + j, 0:HALF], c.ones[:, :],
                                                sq[:, h, j * HALF:(j + 1) * HALF], start=True, stop=True)
                    last.then_inc(s_ms, 1)

            @block.vector
            def _(dve):
                link = Chain(dve, s_n)
                for h in range(HG):
                    dve.wait_ge(s_rt, h + 1)
                    link(nc.vector.reciprocal(rt[:, h, :], rt[:, h, :]))
                    link(nc.vector.scalar_tensor_tensor(out=oT[:, h, :], in0=oT[:, h, :],
                                                        scalar=c.small["g_hgrn"][:, 0:1], in1=rt[:, h, :],
                                                        op0=ALU.mult, op1=ALU.mult))
                    link(nc.vector.tensor_tensor(oT[:, h, :], oT[:, h, :], proj[:, HGT + h, :], ALU.mult))
                for h in range(HG):
                    dve.wait_ge(s_rt, HG + h + 1)
                    link(nc.vector.tensor_tensor(hgoT[:, h, :], oT[:, h, :], sg[:, h, :], ALU.mult))


def merge(nc, I, c, proj, attT, hgoT, x):
    RING = 4
    with ExitStack() as ctx:
        a = Alloc(nc, ctx)
        ring = a.sb("mg_ring", [P, RING, DC, P])
        mix = a.sb("mg_mix", [P, DC, N])
        ta = a.sb("mg_a", [P, 2, N])
        tb = a.sb("mg_b", [P, 2, N])
        pa = a.ps("mg_ps_a", [P, 2, 2, 512])
        pb = a.ps("mg_ps_b", [P, 2, 2, 512])
        s_w = [a.sem(f"mg_loaded{r}") for r in range(RING)]
        s_p, s_g, s_m, s_o, s_x = (a.sem("mg_" + k) for k in ("products", "gated", "mixed", "out_product", "added"))
        block = ctx.enter_context(nc.Block())

        @block.sync
        def _(sp):
            for n in range(2 * DC):
                if n >= RING:
                    k = n - RING
                    sp.wait_ge(s_p if k < DC else s_o, k % DC + 1)
                src = I["w_ab"][n] if n < DC else I["w_out"][n - DC]
                sp.dma_start(ring[:, n % RING], src).then_inc(s_w[n % RING], 16)

        @block.tensor
        def _(pe):
            for n in range(2 * DC):
                pe.wait_ge(s_w[n % RING], 16 * (n // RING + 1))
                m = n % DC
                if n < DC:
                    if n >= 2:
                        pe.wait_ge(s_g, 2 * (n - 1))
                    for ps, src, k0 in ((pa, attT, 0), (pb, hgoT, 4)):
                        for j in range(2):
                            for k in range(4):
                                last = nc.tensor.matmul(ps[:, n % 2, j, 0:HALF], ring[:, n % RING, k0 + k, :],
                                                        src[:, k, j * HALF:(j + 1) * HALF],
                                                        start=(k == 0), stop=(k == 3))
                    last.then_inc(s_p, 1)
                else:
                    if m == 0:
                        pe.wait_ge(s_m, DC)
                    if m >= 2:
                        pe.wait_ge(s_x, m - 1)
                    for j in range(2):
                        for k in range(DC):
                            last = nc.tensor.matmul(pa[:, n % 2, j, 0:HALF], ring[:, n % RING, k, :],
                                                    mix[:, k, j * HALF:(j + 1) * HALF],
                                                    start=(k == 0), stop=(k == DC - 1))
                    last.then_inc(s_o, 1)

        @block.vector
        def _(dve):
            for m in range(DC):
                dve.wait_ge(s_p, m + 1)
                if m >= 2:
                    dve.wait_ge(s_m, m - 1)
                nc.vector.tensor_tensor(halves(ta[:, m % 2, :]), pa[:, m % 2, :, 0:HALF], halves(proj[:, ZA + m, :]),
                                        ALU.mult).then_inc(s_g, 1)
                nc.vector.tensor_tensor(halves(tb[:, m % 2, :]), pb[:, m % 2, :, 0:HALF], halves(proj[:, ZB + m, :]),
                                        ALU.mult).then_inc(s_g, 1)
                dve.wait_ge(s_g, 2 * m + 2)
                nc.vector.tensor_tensor(mix[:, m, :], ta[:, m % 2, :], tb[:, m % 2, :], ALU.add).then_inc(s_m, 1)
            for m in range(DC):
                dve.wait_ge(s_o, m + 1)
                nc.vector.tensor_tensor(halves(x[:, m, :]), pa[:, m % 2, :, 0:HALF], halves(x[:, m, :]),
                                        ALU.add).then_inc(s_x, 1)
            dve.wait_ge(s_x, DC)


def queries(nc, I, xn, S, scratch):
    RING = 4
    NG = 2 * PH
    TT = NT + 1
    with ExitStack() as ctx:
        a = Alloc(nc, ctx)
        ring = a.sb("rt_ring", [P, RING, DC, P])
        sk = a.sb("rt_keys", [P, 2, P])
        q = scratch.rearrange("p (g n) -> p g n", g=NG)
        pq = a.ps("rt_ps_q", [P, 2, 2, 512])
        ps = a.ps("rt_ps_s", [P, 4, 512])
        s_w = [a.sem(f"rt_loaded{r}") for r in range(RING)]
        s_k, s_p, s_c = a.sem("rt_keys_loaded"), a.sem("rt_product"), a.sem("rt_copied")
        s_s, s_sc = a.sem("rt_scores_made"), a.sem("rt_scores_copied")
        block = ctx.enter_context(nc.Block())

        @block.sync
        def _(sp):
            sp.dma_start(sk[:, :, :], I["subkeys"]).then_inc(s_k, 16)
            for n in range(NG):
                if n >= RING:
                    sp.wait_ge(s_p, n - RING + 1)
                sp.dma_start(ring[:, n % RING], I["w_q"][n]).then_inc(s_w[n % RING], 16)

        @block.tensor
        def _(pe):
            for n in range(NG):
                pe.wait_ge(s_w[n % RING], 16 * (n // RING + 1))
                if n >= 2:
                    pe.wait_ge(s_c, n - 1)
                for j in range(2):
                    for k in range(DC):
                        last = nc.tensor.matmul(pq[:, n % 2, j, 0:HALF], ring[:, n % RING, k, :],
                                                xn[:, k, j * HALF:(j + 1) * HALF],
                                                start=(k == 0), stop=(k == DC - 1))
                last.then_inc(s_p, 1)
            pe.wait_ge(s_k, 16)
            pe.wait_ge(s_c, NG)
            for t in range(TT):
                m = P if t < NT else TS
                for g in range(NG):
                    if t >= 1 and g % 4 == 0:
                        pe.wait_ge(s_sc, (t - 1) * 4 + g // 4 + 1)
                    last = nc.tensor.matmul(ps[0:m, g // 4, (g % 4) * P:(g % 4 + 1) * P], q[:, g, t * P:t * P + m],
                                            sk[:, g % 2, :], start=True, stop=True)
                    if g % 4 == 3:
                        last.then_inc(s_s, 1)

        @block.scalar
        def _(act):
            for n in range(NG):
                act.wait_ge(s_p, n + 1)
                nc.scalar.activation(halves(q[:, n, :]), pq[:, n % 2, :, 0:HALF], ACT.Identity).then_inc(s_c, 1)
            for t in range(TT):
                m = P if t < NT else TS
                for k in range(4):
                    act.wait_ge(s_s, t * 4 + k + 1)
                    nc.scalar.copy(S[0:m, t, 4 * k:4 * k + 4, :].rearrange("p g k -> p (g k)"),
                                   ps[0:m, k, :]).then_inc(s_sc, 1)


def pick_and_expand(nc, I, c, xn, stage, A_dram, W_dram):
    UR, GR = 4, 8
    NG = 2 * PH
    TT = NT + 1
    BODY = E1 // UR
    PLAIN, LATE = 14, 2
    NK = TP // GR
    assert NK == (BODY - PLAIN - LATE) * UR
    GB = P // GR
    with ExitStack() as ctx:
        a = Alloc(nc, ctx)
        u = a.sb("ex_u", [P, UR, DC, P])
        ge = a.sb("ex_gelu", [P, UR, N])
        B = a.sb("rw_b", [P, 2, GR // 2, P])
        A = a.sb("rw_a", [P, 2, GR // 2, P])
        iT = a.sb("rw_slots", [P, 3, N])
        S = stage[:, 1, 0:TT * NG * P].rearrange("p (t g k) -> p t g k", t=TT, g=NG)
        free = [0]

        def view(*shape):
            n = int(np.prod(shape))
            v = stage[:, 0, free[0]:free[0] + n]
            free[0] += n
            return v

        wk = view(2, P).rearrange("p (a k) -> p a k", a=2)
        v = view(NG, PK).rearrange("p (g k) -> p g k", g=NG)
        ix = view(NG, PK).bitcast(U32).rearrange("p (g k) -> p g k", g=NG)
        ixf = view(NG, PK).rearrange("p (g k) -> p g k", g=NG)
        cd = view(PH, PK, PK).rearrange("p (h a b) -> p h a b", h=PH, a=PK)
        cw = view(PK, PK)
        sv = view(PH, PK).rearrange("p (h k) -> p h k", h=PH)
        ci = view(PH, PK).bitcast(U32).rearrange("p (h k) -> p h k", h=PH)
        cb = view(2, PH, PK).bitcast(U32).rearrange("p (a h k) -> p a h k", a=2, h=PH)
        cf = view(2, PH, PK).rearrange("p (a h k) -> p a h k", a=2, h=PH)
        oh = view(SLOT, PK).rearrange("p (s k) -> p s k", k=PK)
        se = view(TT, 3, PH, PK).rearrange("p (t j h k) -> p t j h k", t=TT, j=3, h=PH)
        ex = view(TT, PH, PK).rearrange("p (t h k) -> p t h k", t=TT, h=PH)
        sm = view(TT, 2, PH).rearrange("p (t j h) -> p t j h", t=TT, j=2)
        assert free[0] <= P * P
        pu = a.ps("ex_ps_u", [P, 2, 2, 512])
        pw = a.ps("rw_ps", [P, 2, 2, 512])
        s_u = [a.sem(f"ex_u_loaded{r}") for r in range(UR)]
        s_as = [a.sem(f"ex_gelu_stored{r}") for r in range(UR)]
        s_ws = [a.sem(f"rw_stored{r}") for r in range(2)]
        s_pu, s_ge, s_v, s_e, s_ex, s_t, s_x, s_xc, s_b, s_pw, s_wc = (a.sem("ex_" + k) for k in (
            "u_product", "gelu", "pick_chain", "gates_shifted", "gates_exp", "slots_made", "slots_turned",
            "slots_copied", "onehot_made", "w_product", "w_copied"))
        block = ctx.enter_context(nc.Block())

        @block.sync
        def _(sp):
            def load(tile, r):
                sp.dma_start(u[:, r], I["uT"][tile]).then_inc(s_u[r], 16)

            def put(tile, r):
                dst = (A_dram[tile] if isinstance(tile, int) else
                       A_dram[bass.ds(tile, 1), :, :].rearrange("a p n -> p (a n)"))
                sp.dma_start(dst, ge[:, r, :]).then_inc(s_as[r], 16)

            for r in range(UR):
                load(r, r)
            with sp.Fori(1, BODY) as i:
                for r in range(UR):
                    sp.wait_ge(s_pu, i * UR + (r - UR + 1))
                    load(i * UR + r, r)
                    sp.wait_ge(s_ge, i * UR + (r - UR + 1))
                    put(i * UR + (r - UR), r)
            for r in range(UR):
                sp.wait_ge(s_ge, E1 - UR + r + 1)
                put(E1 - UR + r, r)
            for r in range(UR):
                sp.wait_ge(s_as[r], 16 * BODY)

        def staged(b):
            return stage[:, b % 2, :].rearrange("p (i n) -> p i n", n=P)

        @block.tensor
        def _(pe):
            def expand(tile, loaded, r, free):
                pe.wait_ge(s_u[r], loaded)
                if free is not None:
                    pe.wait_ge(s_ge, free)
                for j in range(2):
                    for k in range(DC):
                        last = nc.tensor.matmul(pu[:, r % 2, j, 0:HALF], u[:, r, k, :],
                                                xn[:, k, j * HALF:(j + 1) * HALF], start=(k == 0), stop=(k == DC - 1))
                last.then_inc(s_pu, 1)

            def weights(b, before, copied):
                if copied is not None:
                    pe.wait_ge(s_wc, copied)
                for q in range(2):
                    pe.wait_ge(s_b, before + (q + 1))
                    for g in range(GR // 2):
                        last = nc.tensor.matmul(pw[:, b, q, g * P:(g + 1) * P], B[:, q, g, :], A[:, q, g, :],
                                                start=True, stop=True)
                    last.then_inc(s_pw, 1)

            for r in range(UR):
                expand(r, 16, r, r - 1 if r >= 2 else None)
            with pe.Fori(1, PLAIN + LATE) as i:
                for r in range(UR):
                    expand(i * UR + r, i * 16 + 16, r, i * UR + (r - 1))
            for t in range(TT):
                m = P if t < NT else TS
                pe.wait_ge(s_t, t + 1)
                if t == NT:
                    pe.wait_ge(s_xc, 1)
                o = pw[:, t // 2, t % 2, 0:3 * P] if t < NT else pw[:, 0, 0, 3 * P:3 * P + 3 * TS]
                for j in range(3):
                    last = nc.tensor.transpose(o[:, j * m:(j + 1) * m], se[0:m, t, j].rearrange("p h k -> p (h k)"),
                                               c.ident[0:m, 0:m])
                last.then_inc(s_x, 1)
            pe.wait_ge(s_xc, TT)
            first = (PLAIN + LATE) * UR
            for r in range(UR):
                expand(first + r, (PLAIN + LATE + 1) * 16, r, first + r - 1)
                weights(r % 2, 2 * r, 2 * (r - 1) if r >= 2 else None)
            with pe.Fori(1, BODY - PLAIN - LATE) as i:
                for r in range(UR):
                    expand(None, i * 16 + (PLAIN + LATE + 1) * 16, r, i * UR + (first + r - 1))
                    weights(r % 2, i * (2 * UR) + 2 * r, i * (2 * UR) + 2 * (r - 1))
            weights(0, 2 * NK, 2 * (NK - 1))

        @block.scalar
        def _(act):
            def gelu(made, r, stored):
                act.wait_ge(s_pu, made)
                if stored is not None:
                    act.wait_ge(s_as[r], stored)
                nc.scalar.activation(halves(ge[:, r, :]), pu[:, r % 2, :, 0:HALF], ACT.Gelu).then_inc(s_ge, 1)

            def stage_group(b, before, r, n0):
                for q in range(2):
                    act.wait_ge(s_pw, before + (q + 1))
                    nc.scalar.copy(staged(b)[:, :, bass.ds(n0 + 4 * q, 4) if not isinstance(n0, int) else
                                             slice(n0 + 4 * q, n0 + 4 * q + 4)],
                                   pw[:, r % 2, q, :].rearrange("p (n i) -> p i n", n=4)).then_inc(s_wc, 1)

            def put_block(b, m):
                act.wait_ge(s_wc, 2 * min((b + 1) * GB, NK + 1))
                act.dma_start(W_dram[:, :, b * P:b * P + m].rearrange("i p n -> p i n"),
                              staged(b)[:, :, 0:m]).then_inc(s_ws[b % 2], 16)

            for r in range(UR):
                gelu(r + 1, r, None)
            with act.Fori(1, PLAIN) as i:
                for r in range(UR):
                    gelu(i * UR + (r + 1), r, i * 16)
            act.wait_ge(s_e, TT)
            for t in range(TT):
                m = P if t < NT else TS
                nc.scalar.activation(ex[0:m, t], se[0:m, t, 2], ACT.Exp).then_inc(s_ex, 1)
            with act.Fori(PLAIN, PLAIN + LATE) as i:
                for r in range(UR):
                    gelu(i * UR + (r + 1), r, i * 16)
            act.wait_ge(s_xc, TT)
            i0 = PLAIN + LATE
            for b in range(NT):
                if b >= 2:
                    act.wait_ge(s_ws[b % 2], 16)
                per = GB // UR
                with act.Fori(0, per) as i:
                    for r in range(UR):
                        gelu(i * UR + ((i0 + b * per) * UR + r + 1), r, i * 16 + (i0 + b * per) * 16)
                        stage_group(b, i * (2 * UR) + 2 * (b * GB + r), r, i * (UR * GR) + r * GR)
                put_block(b, P)
            act.wait_ge(s_ws[0], 32)
            stage_group(NT, 2 * NK, 0, 0)
            put_block(NT, TS)
            act.wait_ge(s_ws[0], 48)
            act.wait_ge(s_ws[1], 32)

        @block.vector
        def _(dve):
            link = Chain(dve, s_v)
            for t in range(TT):
                m = P if t < NT else TS
                for g in range(NG):
                    s = S[0:m, t, g, :]
                    w = wk[0:m, g % 2, :]
                    link(nc.vector.max(v[0:m, g, 0:8], s))
                    nc.vector.max_index(ix[0:m, g, 0:8], v[0:m, g, 0:8], s)
                    link(nc.vector.match_replace(w, v[0:m, g, 0:8], s, SENT))
                    link(nc.vector.max(v[0:m, g, 8:16], w))
                    link(nc.vector.max_index(ix[0:m, g, 8:16], v[0:m, g, 8:16], w))
                vv = v[0:m].rearrange("p (h a) k -> p h a k", a=2)
                link(nc.vector.tensor_tensor(cd[0:m], vv[:, :, 0, :].unsqueeze(3).to_broadcast([m, PH, PK, PK]),
                                             vv[:, :, 1, :].unsqueeze(2).to_broadcast([m, PH, PK, PK]), ALU.add))
                for h in range(PH):
                    s = cd[0:m, h].rearrange("p a b -> p (a b)")
                    w = cw[0:m, :]
                    link(nc.vector.max(sv[0:m, h, 0:8], s))
                    nc.vector.max_index(ci[0:m, h, 0:8], sv[0:m, h, 0:8], s)
                    link(nc.vector.match_replace(w, sv[0:m, h, 0:8], s, SENT))
                    link(nc.vector.max(sv[0:m, h, 8:16], w))
                    link(nc.vector.max_index(ci[0:m, h, 8:16], sv[0:m, h, 8:16], w))
                nc.vector.tensor_tensor(se[0:m, t, 2], sv[0:m], sv[0:m, :, 0:1].to_broadcast([m, PH, PK]),
                                        ALU.subtract).then_inc(s_e, 1)
                nc.vector.tensor_scalar(cb[0:m, 0], ci[0:m], 4, None, ALU.logical_shift_right)
                link(nc.vector.tensor_scalar(cb[0:m, 1], ci[0:m], PK - 1, None, ALU.bitwise_and))
                nc.vector.tensor_copy(cf[0:m], cb[0:m])
                link(nc.vector.tensor_copy(ixf[0:m], ix[0:m]))
                iv = ixf[0:m].rearrange("p (h a) k -> p h a k", a=2)
                o3 = oh[0:m]
                o4 = oh[0:m].rearrange("p (h s) k -> p h s k", h=PH)
                for j in range(2):
                    part = cf[0:m, j].rearrange("p h k -> p (h k)").unsqueeze(2).to_broadcast([m, SLOT, PK])
                    link(nc.vector.tensor_tensor(o3, part, c.iota[0:m, 0:PK].unsqueeze(1).to_broadcast(
                        [m, SLOT, PK]), ALU.is_equal))
                    link(nc.vector.tensor_tensor(o4, o4, iv[:, :, j, :].unsqueeze(2).to_broadcast(
                        [m, PH, PK, PK]), ALU.mult))
                    link(nc.vector.tensor_reduce(se[0:m, t, j].rearrange("p h k -> p (h k)"), o3, X, ALU.add))
            for t in range(TT):
                m = P if t < NT else TS
                dve.wait_ge(s_ex, t + 1)
                link(nc.vector.tensor_reduce(sm[0:m, t, 0], ex[0:m, t], X, ALU.add))
                link(nc.vector.reciprocal(sm[0:m, t, 1], sm[0:m, t, 0]))
                nc.vector.tensor_tensor(se[0:m, t, 2], ex[0:m, t], sm[0:m, t, 1].unsqueeze(2).to_broadcast(
                    [m, PH, PK]), ALU.mult).then_inc(s_t, 1)
            for t in range(TT):
                m = P if t < NT else TS
                dve.wait_ge(s_x, t + 1)
                o = pw[:, t // 2, t % 2, 0:3 * P] if t < NT else pw[:, 0, 0, 3 * P:3 * P + 3 * TS]
                nc.vector.tensor_copy(iT[:, :, t * P:t * P + m], o.rearrange("p (j n) -> p j n", j=3)).then_inc(s_xc, 1)
            dve.wait_ge(s_xc, TT)

            def rows(n, q, used):
                if used is not None:
                    dve.wait_ge(s_pw, used)
                for g in range(GR // 2):
                    at = slice(n + g, n + g + 1) if isinstance(n, int) else bass.ds(n + g, 1)
                    nc.vector.tensor_scalar(B[:, q, g, :], c.iota[:, :], iT[:, 1, at], None, ALU.is_equal)
                    last = nc.vector.tensor_scalar(A[:, q, g, :], c.iota[:, :], iT[:, 0, at], iT[:, 2, at],
                                                   ALU.is_equal, ALU.mult)
                last.then_inc(s_b, 1)

            for q in range(2):
                rows(q * (GR // 2), q, None)
            with dve.Fori(1, NK) as i:
                for q in range(2):
                    rows(i * GR + q * (GR // 2), q, i * 2 + (q - 1))
            for q in range(2):
                rows(TP + q * (GR // 2), q, 2 * NK + q - 1)


def gather_experts(nc, I, A_dram, W_dram, x):
    E = 8
    NG = E1 // E
    with ExitStack() as ctx:
        a = Alloc(nc, ctx)
        v = a.sb("ev_v", [P, 2, E, D])
        w = a.sb("ev_w", [P, 2, E, N])
        H = a.sb("ev_h", [P, 2, E, N])
        pv = a.ps("ev_ps", [P, 4, 2, 512])
        s_v, s_w, s_a = ([a.sem(f"ev_{k}_loaded{b}") for b in range(2)] for k in ("v", "w", "a"))
        s_h, s_pv, s_ac = (a.sem("ev_" + k) for k in ("hidden", "product", "added"))
        block = ctx.enter_context(nc.Block())
        vsrc = I["v"].rearrange("(g e p) d -> g p e d", p=P, e=E)
        asrc = A_dram.rearrange("(g e) p n -> g p e n", e=E)
        wsrc = W_dram.rearrange("(g e) p n -> g p e n", e=E)

        def pick(src, g):
            return src[g] if isinstance(g, int) else src[bass.ds(g, 1)].rearrange("g p e d -> p (g e) d")

        @block.sync
        def _(sp):
            def load(g, b):
                sp.dma_start(H[:, b], pick(asrc, g)).then_inc(s_a[b], 16)
                sp.dma_start(v[:, b], pick(vsrc, g)).then_inc(s_v[b], 16)

            for b in range(2):
                load(b, b)
            with sp.Fori(1, NG // 2) as i:
                for b in range(2):
                    sp.wait_ge(s_pv, i * (2 * DC) + (b - 1) * DC)
                    load(i * 2 + b, b)

        @block.scalar
        def _(act):
            def load(g, b):
                act.dma_start(w[:, b], pick(wsrc, g)).then_inc(s_w[b], 16)

            for b in range(2):
                load(b, b)
            with act.Fori(1, NG // 2) as i:
                for b in range(2):
                    act.wait_ge(s_h, i * (2 * E) + (b - 1) * E)
                    load(i * 2 + b, b)

        @block.vector
        def _(dve):
            def hide(b, loaded):
                dve.wait_ge(s_a[b], loaded)
                dve.wait_ge(s_w[b], loaded)
                for e in range(E):
                    nc.vector.tensor_tensor(H[:, b, e, :], H[:, b, e, :], w[:, b, e, :], ALU.mult).then_inc(s_h, 1)

            def add(m, made, before):
                dve.wait_ge(s_pv, made)
                if before is not None:
                    dve.wait_ge(s_ac, before)
                nc.vector.tensor_tensor(halves(x[:, m, :]), pv[:, m % 4, :, 0:HALF], halves(x[:, m, :]),
                                        ALU.add).then_inc(s_ac, 1)

            hide(0, 16)
            hide(1, 16)
            for m in range(DC):
                add(m, m + 1, None)
            with dve.Fori(1, NG // 2) as i:
                for b in range(2):
                    hide(b, i * 16 + 16)
                    for m in range(DC):
                        add(m, i * (2 * DC) + ((b - 1) * DC + m + 1), i * (2 * DC) + ((b - 2) * DC + m + 1))
            for m in range(DC):
                add(m, (NG - 1) * DC + m + 1, (NG - 2) * DC + m + 1)
            dve.wait_ge(s_ac, NG * DC)

        @block.tensor
        def _(pe):
            def group(b, loaded, hidden, free):
                pe.wait_ge(s_v[b], loaded)
                pe.wait_ge(s_h, hidden)
                for m in range(DC):
                    f = free(m)
                    if f is not None:
                        pe.wait_ge(s_ac, f)
                    for j in range(2):
                        for e in range(E):
                            last = nc.tensor.matmul(pv[:, m % 4, j, 0:HALF], v[:, b, e, m * P:(m + 1) * P],
                                                    H[:, b, e, j * HALF:(j + 1) * HALF],
                                                    start=(e == 0), stop=(e == E - 1))
                    last.then_inc(s_pv, 1)

            group(0, 16, E, lambda m: m - 3 if m >= 4 else None)
            group(1, 16, 2 * E, lambda m: DC + m - 3)
            with pe.Fori(1, NG // 2) as i:
                for b in range(2):
                    group(b, i * 16 + 16, i * (2 * E) + (b + 1) * E, lambda m: i * (2 * DC) + (b * DC + m - 3))


def per_layer_input(nc, I, c, xn, x):
    RING = 4
    PC = 2
    with ExitStack() as ctx:
        a = Alloc(nc, ctx)
        ring = a.sb("pl_ring", [P, RING, DC + PC, P])
        pT = a.sb("pl_p", [P, PC, N])
        sg = a.sb("pl_sig", [P, 2, N])
        gd = a.sb("pl_gated", [P, 2, N])
        pa = a.ps("pl_ps_a", [P, 2, 2, 512])
        pb = a.ps("pl_ps_b", [P, 2, 2, 512])
        s_w = [a.sem(f"pl_loaded{r}") for r in range(RING)]
        s_i, s_p, s_s, s_g, s_x = (a.sem("pl_" + k) for k in ("p_loaded", "products", "sigmoid", "gated", "added"))
        block = ctx.enter_context(nc.Block())

        @block.sync
        def _(sp):
            sp.dma_start(pT[:, :, :], I["pT"]).then_inc(s_i, 16)
            for n in range(DC):
                if n >= RING:
                    sp.wait_ge(s_p, n - RING + 1)
                sp.dma_start(ring[:, n % RING], I["w_gp"][n]).then_inc(s_w[n % RING], 16)

        @block.tensor
        def _(pe):
            pe.wait_ge(s_i, 16)
            for n in range(DC):
                pe.wait_ge(s_w[n % RING], 16 * (n // RING + 1))
                if n >= 2:
                    pe.wait_ge(s_g, n - 1)
                for ps, src, k0, kn in ((pa, xn, 0, DC), (pb, pT, DC, PC)):
                    for j in range(2):
                        for k in range(kn):
                            last = nc.tensor.matmul(ps[:, n % 2, j, 0:HALF], ring[:, n % RING, k0 + k, :],
                                                    src[:, k, j * HALF:(j + 1) * HALF],
                                                    start=(k == 0), stop=(k == kn - 1))
                last.then_inc(s_p, 1)

        @block.scalar
        def _(act):
            for n in range(DC):
                act.wait_ge(s_p, n + 1)
                if n >= 2:
                    act.wait_ge(s_g, n - 1)
                nc.scalar.activation(halves(sg[:, n % 2, :]), pa[:, n % 2, :, 0:HALF], ACT.Sigmoid).then_inc(s_s, 1)

        @block.vector
        def _(dve):
            for n in range(DC):
                dve.wait_ge(s_s, n + 1)
                if n >= 2:
                    dve.wait_ge(s_x, n - 1)
                nc.vector.tensor_tensor(halves(gd[:, n % 2, :]), pb[:, n % 2, :, 0:HALF], halves(sg[:, n % 2, :]),
                                        ALU.mult).then_inc(s_g, 1)
                dve.wait_ge(s_g, n + 1)
                nc.vector.tensor_tensor(x[:, n, :], x[:, n, :], gd[:, n % 2, :], ALU.add).then_inc(s_x, 1)
            dve.wait_ge(s_x, DC)


def store(nc, a, y, dst):
    s_o = a.sem("y_stored")
    with nc.Block() as block:
        @block.sync
        def _(sp):
            sp.dma_start(dst, y[:, :, :]).then_inc(s_o, 16)
            sp.wait_ge(s_o, 16)


class Tiles:
    pass


def build(nc, I, O, scratch):
    with ExitStack() as ctx:
        a = Alloc(nc, ctx)
        c = Tiles()
        c.ones, c.ident, c.iota = (a.sb(k, [P, P]) for k in ("ones", "ident", "iota"))
        c.sel_b, c.sel_h = a.sb("sel_b", [TS, TS, NH]), a.sb("sel_h", [TS, TS, NH])
        c.selT = a.sb("selT", [TS * NH, TS])
        c.rb = a.sb("rb", [NB + 1, NH])
        c.eps = a.sb("eps", [P, 1])
        rms_sems = [a.sem("rms_" + k) for k in ("squared", "mean", "root", "recip", "scaled")]
        c.x = a.sb("x", [P, DC, N])
        c.small = {k: a.sb("c_" + k, s) for k, s in (("g_mix", [P, DC]), ("g_ffn", [P, DC]), ("g_ple", [P, DC]),
                                                     ("g_final", [P, DC]), ("g_hgrn", [P, 1]), ("lbl", [P, 2, HG]))}
        c.small["pages"] = a.sb("c_pages", [1, TS * NPG], I32)
        x = c.x
        h = a.sb("h", [P, DC, N])
        with ExitStack() as mid:
            b = Alloc(nc, mid)
            c.causal, c.tri = (b.sb(k, [P, P]) for k in ("causal", "tri"))
            c.reset = b.sb("reset", [P, TP])
            c.pick = b.sb("pick", [TS, TS, P])
            constants(nc, a, I, c)
            proj = b.sb("proj", [P, MT, N])
            vtok = b.sb("vtok", [P, NT + 1, P])
            hitok = b.sb("hitok", [P, NT + 1, 512])
            iwtok = b.sb("iwtok", [P, NT + 1, NH])
            ikT = b.sb("ikT", [P, N])
            rms_block(nc, 0, rms_sems, x, h, c.small["g_mix"], c.ones, c.eps)
            project(nc, I, O, c, h, proj, ikT, vtok, hitok, iwtok)
            attT, hgoT = h[:, 0:4, :], h[:, 4:8, :]
            with ExitStack() as att:
                d = Alloc(nc, att)
                rev = d.sb("rev", [NH, REV])
                with ExitStack() as pro:
                    e = Alloc(nc, pro)
                    maskp = e.sb("maskp", [P, NT, TP])
                    toep = e.sb("toep", [P, NH, TP])
                    index_prompt(nc, c, proj, ikT, iwtok, maskp)
                    bias_table(nc, c, I["onehot"], rev, scratch["rev"], toep)
                    attend_prompt(nc, c, proj, vtok, maskp, toep, attT)
                sample_attention(nc, I, c, proj, ikT, vtok, iwtok, rev, attT)
            hgrn(nc, I, O, c, proj, hitok, hgoT)
            merge(nc, I, c, proj, attT, hgoT, x)
        rms_block(nc, 1, rms_sems, x, h, c.small["g_ffn"], c.ones, c.eps)
        with ExitStack() as mid:
            stage = Alloc(nc, mid).sb("stage", [P, 2, P * P])
            S = stage[:, 1, 0:(NT + 1) * 2 * PH * P].rearrange("p (t g k) -> p t g k", t=NT + 1, g=2 * PH)
            queries(nc, I, h, S, stage[:, 0, 0:2 * PH * N])
            pick_and_expand(nc, I, c, h, stage, scratch["A"], scratch["W"])
        gather_experts(nc, I, scratch["A"], scratch["W"], x)
        rms_block(nc, 2, rms_sems, x, h, c.small["g_ple"], c.ones, c.eps)
        per_layer_input(nc, I, c, h, x)
        rms_block(nc, 3, rms_sems, x, h, c.small["g_final"], c.ones, c.eps)
        store(nc, a, h, O["yT"])


def bucket_onehot():
    dist = PAST - np.arange(REV)
    n = np.maximum(dist, 0)
    nf = np.maximum(n, 1).astype(np.float32)
    large = 16 + (np.log(nf / np.float32(16)) / np.float32(math.log(128 / 16)) * np.float32(16)).astype(np.int32)
    b = np.where(n < 16, n, np.minimum(large, NB - 1))
    b = np.where(dist < 0, NB, b)
    out = np.zeros((NB + 1, REV), np.float32)
    out[b, np.arange(REV)] = 1.0
    return out


def kernel(**inputs):
    import concourse.bacc as bacc
    from concourse.bass_utils import run_bass_kernel_spmd

    g = {k: np.asarray(v) for k, v in inputs.items()}

    def tiles(w):
        k, m = w.shape
        return np.ascontiguousarray(w.reshape(k // P, P, m // P, P).transpose(2, 1, 0, 3))

    def cols(v):
        return np.ascontiguousarray(v.reshape(-1, P).T)

    w_in = g["w_in"][0]
    o = np.cumsum([0, 512, 128, 128, 512, 64, 8, 512, 512, 512, 512, 1024, 1024]).tolist()
    aq, ak, av, iq, ik, iw, hq, hf, hi, hg, za, zb = (w_in[:, o[i]:o[i + 1]] for i in range(12))
    order = [x for m in range(4) for x in (m, m + 4)]
    aq = aq.reshape(D, NH, HD)[:, order].reshape(D, 512)
    w_a = g["w_branch_a"][0].reshape(NH, HD, D)[order].reshape(512, D)
    xT = np.concatenate([g["x_prompt"][0], g["x_sample"][:, 0]]).T
    pT = np.concatenate([g["p_prompt"][0, 0], g["p_sample"][0, :, 0]]).T
    arrays = {
        "xT": xT.reshape(DC, P, N).transpose(1, 0, 2),
        "pT": pT.reshape(2, P, N).transpose(1, 0, 2),
        "w_t": tiles(np.concatenate([aq, ak, iq, hq, hg, hf, za, zb], axis=1)),
        "w_ik": ik.reshape(DC, P, HD).transpose(1, 0, 2),
        "w_tok": np.concatenate([av, hi, iw], axis=1).reshape(DC, P, 648).transpose(1, 0, 2),
        "w_ab": np.concatenate([tiles(w_a), tiles(g["w_branch_b"][0])], axis=2),
        "w_out": tiles(g["w_out"][0]),
        "w_q": tiles(g["peer_wq"][0]),
        "w_gp": np.concatenate([tiles(g["w_ple_gate"][0]), tiles(g["w_ple_proj"][0])], axis=2),
        "subkeys": g["peer_subkeys"][0].transpose(2, 0, 1),
        "uT": tiles(g["peer_u"][0].T),
        "v": g["peer_v"][0],
        "g_mix": cols(g["g_mix"][0]), "g_ffn": cols(g["g_ffn"][0]), "g_ple": cols(g["g_ple"][0]),
        "g_final": cols(g["g_final"]), "g_hgrn": cols(g["g_hgrn"][0]),
        "lbl": g["lb_logits"].reshape(2, HG, P).transpose(2, 0, 1),
        "rel_bias": g["rel_bias"],
        "onehot": bucket_onehot(),
        "pages": g["page_table"].reshape(1, -1),
        "kidxT": g["cache_kidx"][0].transpose(0, 2, 1),
        "kT": g["cache_k"][0].reshape(-1, PG, P).transpose(0, 2, 1),
        "vC": g["cache_v"][0].reshape(-1, PG, P),
        "state": g["state_hgrn"][0].transpose(2, 0, 1, 3),
    }
    nc = bacc.Bacc("TRN2", target_bir_lowering=False, num_devices=1)
    I, sent = {}, {}
    for name, arr in arrays.items():
        arr = np.ascontiguousarray(arr)
        sent["in_" + name] = arr
        I[name] = nc.dram_tensor("in_" + name, arr.shape, mybir.dt.from_np(arr.dtype), kind="ExternalInput").ap()
    shapes = {"yT": [P, DC, N], "kT": [P, N], "v_p": [TP, P], "v_s": [TS, P], "ikT": [HD, N],
              "hg_p": [P, HG, P], "hg_s": [P, TS, HG, P]}
    O = {k: nc.dram_tensor("out_" + k, s, F32, kind="ExternalOutput").ap() for k, s in shapes.items()}
    scratch = {"rev": nc.dram_tensor("scratch_rev", [NH, P, SK], F32).ap(),
               "A": nc.dram_tensor("scratch_a", [E1, P, N], F32).ap(),
               "W": nc.dram_tensor("scratch_w", [E1, P, N], F32).ap()}
    build(nc, I, O, scratch)
    r = run_bass_kernel_spmd(nc, [sent], core_ids=[0]).results[0]
    got = {k: r["out_" + k] for k in shapes}
    y = got["yT"].transpose(2, 1, 0).reshape(N, D)
    k = got["kT"].T.reshape(N, 2, HD)
    kidx = got["ikT"].T
    return (y[None, :TP], y[TP:, None],
            k[None, None, :TP], got["v_p"].reshape(1, 1, TP, 2, HD), kidx[None, None, :TP],
            got["hg_p"].transpose(1, 0, 2)[None, None],
            k[TP:][None, :, None], got["v_s"].reshape(1, TS, 1, 2, HD), kidx[TP:][None, :, None],
            got["hg_s"].transpose(1, 2, 0, 3)[None])
```

```python
from contextlib import ExitStack
import math

import numpy as np
import concourse.bass as bass
from concourse import mybir

F32 = mybir.dt.float32
U32 = mybir.dt.uint32
I32 = mybir.dt.int32
ALU = mybir.AluOpType
ACT = mybir.ActivationFunctionType
X = mybir.AxisListType.X

P = 128
D = 1024
DC = D // P
TP = 512
NT = TP // P
TS = 8
N = TP + TS
HALF = N // 2
HD = 64
NH = 8
NQ = NH * HD // P
HG = 4
CH = 32
NCH = TP // CH
PAST = 1024
PG = 128
NPG = PAST // PG
L = PAST + 1
TOPP = min(256, TP // 4)
TOPS = min(256, L // 4)
SK = TP + P
REV = PAST + P
NB = 32
PH = 8
PK = 16
SLOT = PH * PK
E1 = 128
SENT = -3.0e38
LOW = -1.0e38
OFF = -1.0e30
EPS = 1e-6
AQ, AK, IQ, HQ, HGT, HF, ZA, ZB, MT = 0, 4, 5, 9, 13, 17, 21, 29, 37


def halves(ap):
    return ap.rearrange("p (j n) -> p j n", j=2)


class Alloc:

    def __init__(self, nc, ctx):
        self.nc, self.ctx = nc, ctx

    def sb(self, name, shape, dt=F32):
        return self.ctx.enter_context(self.nc.sbuf_tensor(name, shape, dt))

    def ps(self, name, shape):
        return self.ctx.enter_context(self.nc.psum_tensor(name, shape, F32))

    def sem(self, name):
        return self.nc.alloc_semaphore(name)


class Chain:

    def __init__(self, eng, sem):
        self.eng, self.sem, self.n = eng, sem, 0

    def __call__(self, ins):
        self.n += 1
        ins.then_inc(self.sem, 1)
        self.eng.wait_ge(self.sem, self.n)


class Slots:

    def __init__(self, a, n):
        self.sems = [a.sem(f"weights_loaded{r}") for r in range(n)]
        self.before = [0] * n

    def landed(self, n):
        k = len(self.sems)
        return self.sems[n % k], self.before[n % k] + 16 * (n // k + 1)

    def stage_ends(self, tiles):
        for n in range(tiles):
            self.before[n % len(self.sems)] += 16


class NormSems:
    def __init__(self, a):
        self.squared, self.mean, self.root, self.recip, self.scaled = (
            a.sem("norm_" + k) for k in ("squared", "mean", "root", "recip", "scaled"))


class Norm:

    def __init__(self, nc, c, turn, gain, sq, rt, ps):
        self.nc, self.c, self.turn, self.gain = nc, c, turn, c.small[gain]
        self.sq, self.rt, self.ps = sq, rt, ps

    def squares(self, act):
        s = self.c.norm_sems
        for k in range(DC):
            self.nc.scalar.activation(self.sq[:, k, :], self.c.x[:, k, :], ACT.Square).then_inc(s.squared, 1)
        act.wait_ge(s.mean, self.turn + 1)
        self.nc.scalar.activation(halves(self.rt), self.ps, ACT.Sqrt, scale=1.0 / D,
                                  bias=self.c.eps[:, 0:1]).then_inc(s.root, 1)

    def sums(self, pe):
        s = self.c.norm_sems
        for k in range(DC):
            pe.wait_ge(s.squared, self.turn * DC + k + 1)
            for j in range(2):
                last = self.nc.tensor.matmul(self.ps[:, j, :], self.c.ones[:, :],
                                             self.sq[:, k, j * HALF:(j + 1) * HALF],
                                             start=(k == 0), stop=(k == DC - 1))
        last.then_inc(s.mean, 1)

    def scale(self, dve):
        s, c = self.c.norm_sems, self.c
        dve.wait_ge(s.root, self.turn + 1)
        self.nc.vector.reciprocal(self.rt, self.rt).then_inc(s.recip, 1)
        dve.wait_ge(s.recip, self.turn + 1)
        for k in range(DC):
            self.nc.vector.scalar_tensor_tensor(out=c.h[:, k, :], in0=c.x[:, k, :], scalar=self.gain[:, k:k + 1],
                                                in1=self.rt, op0=ALU.mult, op1=ALU.mult).then_inc(s.scaled, 1)
        dve.wait_ge(s.scaled, self.scaled(DC - 1)[1])

    def scaled(self, k):
        return self.c.norm_sems.scaled, self.turn * DC + k + 1


def constants(nc, a, I, c):
    s_c, s_c2, s_d = a.sem("const_made"), a.sem("bias_row_set"), a.sem("const_loaded")
    with nc.Block() as block:
        @block.gpsimd
        def _(pool):
            link = Chain(pool, s_c)
            link(nc.gpsimd.memset(c.ones[:, :], 1.0))
            link(nc.gpsimd.memset(c.eps[:, :], EPS))
            link(nc.gpsimd.memset(c.ident[:, :], 0.0))
            link(nc.gpsimd.affine_select(out=c.ident[:, :], in_=c.ident[:, :], compare_op=ALU.not_equal,
                                         fill=1.0, base=0, pattern=[[-1, P]], channel_multiplier=1))
            link(nc.gpsimd.memset(c.causal[:, :], 0.0))
            link(nc.gpsimd.affine_select(out=c.causal[:, :], in_=c.causal[:, :], compare_op=ALU.is_ge,
                                         fill=LOW, base=0, pattern=[[-1, P]], channel_multiplier=1))
            link(nc.gpsimd.memset(c.tri[:, :], 1.0))
            link(nc.gpsimd.affine_select(out=c.tri[:, :], in_=c.tri[:, :], compare_op=ALU.is_ge,
                                         fill=0.0, base=0, pattern=[[1, P]], channel_multiplier=-1))
            for k in range(P // CH):
                v = c.tri[:, k * CH:(k + 1) * CH]
                link(nc.gpsimd.affine_select(out=v, in_=v, compare_op=ALU.is_ge, fill=0.0, base=-k * CH,
                                             pattern=[[0, CH]], channel_multiplier=1))
            link(nc.gpsimd.memset(c.reset[:, :], 1.0))
            link(nc.gpsimd.memset(c.reset[:, :].rearrange("p (c k) -> p c k", k=CH)[:, :, 0:1], 0.0))
            for t in (c.sel_b, c.sel_h):
                link(nc.gpsimd.memset(t[:, :, :], 0.0))
            link(nc.gpsimd.affine_select(out=c.sel_b[:, :, :], in_=c.sel_b[:, :, :], compare_op=ALU.not_equal,
                                         fill=1.0, base=0, pattern=[[-1, 8], [0, 8]], channel_multiplier=1))
            link(nc.gpsimd.affine_select(out=c.sel_h[:, :, :], in_=c.sel_h[:, :, :], compare_op=ALU.not_equal,
                                         fill=1.0, base=0, pattern=[[0, 8], [-1, 8]], channel_multiplier=1))
            link(nc.gpsimd.memset(c.pick[:, :, :], 0.0))
            link(nc.gpsimd.affine_select(out=c.pick[:, :, :], in_=c.pick[:, :, :], compare_op=ALU.not_equal,
                                         fill=1.0, base=0, pattern=[[-1, 8], [0, P]], channel_multiplier=1))
            link(nc.gpsimd.memset(c.selT[:, :], 1.0))
            link(nc.gpsimd.affine_select(out=c.selT[:, :], in_=c.selT[:, :], compare_op=ALU.is_ge, fill=0.0,
                                         base=0, pattern=[[-NH, TS]], channel_multiplier=1))
            link(nc.gpsimd.affine_select(out=c.selT[:, :], in_=c.selT[:, :], compare_op=ALU.is_ge, fill=0.0,
                                         base=NH - 1, pattern=[[NH, TS]], channel_multiplier=-1))
            link(nc.gpsimd.iota(c.iota[:, :], pattern=[[1, P]], base=0, channel_multiplier=0,
                                allow_small_or_imprecise_dtypes=True))

        @block.sync
        def _(sp):
            sp.dma_start(c.x[:, :, :], I["xT"]).then_inc(c.x_loaded, 16)
            for k in ("g_mix", "g_ffn", "g_ple", "g_final", "g_hgrn", "lbl", "pages"):
                sp.dma_start(c.small[k][:, :, :] if k == "lbl" else c.small[k][:, :], I[k]).then_inc(s_d, 16)
            sp.dma_start(c.rb[0:NB, :], I["rel_bias"]).then_inc(s_d, 16)
            sp.wait_ge(s_d, 128)

        @block.vector
        def _(dve):
            nc.vector.memset(c.rb[NB:NB + 1, :], OFF).then_inc(s_c2, 1)
            dve.wait_ge(s_c2, 1)


def project_first(nc, I, O, c, h, proj, ikT, vtok, hitok, iwtok, rev, skew, work):
    RING = 4
    NTL = HQ
    W = REV // 3
    with ExitStack() as ctx:
        a = Alloc(nc, ctx)
        ring = ring_of(work)
        wtok = a.sb("w_tok", [P, DC, 648])
        wik = a.sb("w_ik", [P, DC, HD])
        oh = a.sb("bias_onehot", [NB + 1, REV])
        pp = a.ps("proj_ps", [P, 2, 2, 512])
        pt = a.ps("tok_ps", [P, 2, 2, 512])
        s_wt, s_wi = a.sem("wtok_loaded"), a.sem("wik_loaded")
        s_pt, s_ct = a.sem("tok_product"), a.sem("tok_copied")
        s_pp, s_cp = a.sem("tile_product"), a.sem("tile_copied")
        s_ik, s_ikc, s_o = a.sem("ik_product"), a.sem("ik_copied"), a.sem("kv_stored")
        s_oh, s_bp, s_bc = a.sem("bias_onehot_loaded"), a.sem("bias_product"), a.sem("bias_copied")
        norm = Norm(nc, c, 0, "g_mix", proj[:, ZA:ZA + DC, :], proj[:, ZB, :], pp[:, 0, :, 0:HALF])
        block = ctx.enter_context(nc.Block())
        TT = NT + 1

        @block.sync
        def _(sp):
            sp.dma_start(oh[:, :], I["onehot"]).then_inc(s_oh, 16)
            sp.dma_start(wtok[:, :, :], I["w_tok"]).then_inc(s_wt, 16)
            for r in range(RING):
                sp.dma_start(ring[:, r], I["w_t"][r]).then_inc(c.slots.sems[r], 16)
            sp.dma_start(wik[:, :, :], I["w_ik"]).then_inc(s_wi, 16)
            for n in range(RING, NTL):
                sp.wait_ge(s_pp, n - RING + 1)
                sp.dma_start(ring[:, n % RING], I["w_t"][n]).then_inc(c.slots.sems[n % RING], 16)
            sp.wait_ge(s_bc, 1)
            sp.dma_start(skew[:, :, 0:SK - 1],
                         rev[:, REV - SK + 1:REV].unsqueeze(1).to_broadcast([NH, P, SK - 1])).then_inc(s_o, 16)
            sp.wait_ge(s_ct, 2 * TT)
            sp.dma_start(O["v_p"].rearrange("(t p) n -> p t n", p=P), vtok[:, 0:NT, :]).then_inc(s_o, 16)
            sp.dma_start(O["v_s"], vtok[0:TS, NT, :]).then_inc(s_o, 16)
            sp.wait_ge(s_cp, NTL)
            sp.dma_start(O["kT"], proj[:, AK, :]).then_inc(s_o, 16)
            sp.wait_ge(s_ikc, 2)
            sp.dma_start(O["ikT"], ikT[0:HD, :]).then_inc(s_o, 16)
            sp.wait_ge(s_o, 80)

        @block.tensor
        def _(pe):
            pe.wait_ge(s_oh, 16)
            for j in range(3):
                last = nc.tensor.matmul(pt[0:NH, j // 2, j % 2, 0:W], c.rb[:, :], oh[:, j * W:(j + 1) * W],
                                        start=True, stop=True)
            last.then_inc(s_bp, 1)
            norm.sums(pe)
            pe.wait_ge(s_bc, 1)
            pe.wait_ge(s_wt, 16)
            for t in range(TT):
                m = P if t < NT else TS
                if t >= 2:
                    pe.wait_ge(s_ct, 2 * (t - 1))
                for c0, c1, j in ((0, 324, 0), (324, 648, 1)):
                    for k in range(DC):
                        if t == 0 and j == 0:
                            pe.wait_ge(*norm.scaled(k))
                        last = nc.tensor.matmul(pt[0:m, t % 2, j, 0:324], h[:, k, t * P:t * P + m],
                                                wtok[:, k, c0:c1], start=(k == 0), stop=(k == DC - 1))
                last.then_inc(s_pt, 1)
            for n in range(NTL):
                pe.wait_ge(*c.slots.landed(n))
                if n >= 2:
                    pe.wait_ge(s_cp, n - 1)
                for j in range(2):
                    for k in range(DC):
                        last = nc.tensor.matmul(pp[:, n % 2, j, 0:HALF], ring[:, n % RING, k, :],
                                                h[:, k, j * HALF:(j + 1) * HALF],
                                                start=(k == 0), stop=(k == DC - 1))
                last.then_inc(s_pp, 1)
            pe.wait_ge(s_wi, 16)
            pe.wait_ge(s_cp, NTL - 1)
            for j in range(2):
                for k in range(DC):
                    last = nc.tensor.matmul(pp[0:HD, 1, j, 0:HALF], wik[:, k, :], h[:, k, j * HALF:(j + 1) * HALF],
                                            start=(k == 0), stop=(k == DC - 1))
            last.then_inc(s_ik, 1)

        @block.vector
        def _(dve):
            dve.wait_ge(s_bp, 1)
            nc.vector.tensor_copy(rev[:, 0:2 * W].rearrange("h (j w) -> h j w", j=2), pt[0:NH, 0, :, 0:W])
            nc.vector.tensor_copy(rev[:, 2 * W:REV], pt[0:NH, 1, 0, 0:W]).then_inc(s_bc, 1)
            dve.wait_ge(c.x_loaded, 16)
            norm.scale(dve)
            for t in range(TT):
                m = P if t < NT else TS
                dve.wait_ge(s_pt, t + 1)
                nc.vector.tensor_copy(vtok[0:m, t, :], pt[0:m, t % 2, 0, 0:P])
                nc.vector.tensor_copy(hitok[0:m, t, 0:196], pt[0:m, t % 2, 0, P:324]).then_inc(s_ct, 1)
                nc.vector.tensor_copy(hitok[0:m, t, 196:512], pt[0:m, t % 2, 1, 0:316])
                nc.vector.tensor_scalar(iwtok[0:m, t, :], pt[0:m, t % 2, 1, 316:324], NH ** -0.5, None,
                                        ALU.mult).then_inc(s_ct, 1)
            dve.wait_ge(s_ik, 1)
            nc.vector.tensor_copy(halves(ikT[0:HD, :]), pp[0:HD, 1, :, 0:HALF]).then_inc(s_ikc, 1)
            nc.vector.tensor_copy(halves(ikT[HD:P, :]), pp[0:HD, 1, :, 0:HALF]).then_inc(s_ikc, 1)

        @block.scalar
        def _(act):
            act.wait_ge(c.x_loaded, 16)
            norm.squares(act)
            for n in range(NTL):
                act.wait_ge(s_pp, n + 1)
                nc.scalar.activation(halves(proj[:, n, :]), pp[:, n % 2, :, 0:HALF], ACT.Identity).then_inc(s_cp, 1)


def ring_of(work):
    return work[:, 0:4 * DC * P].rearrange("p (r c n) -> p r c n", r=4, c=DC)


def rest_of(work):
    rest = work[:, 4 * DC * P:4 * DC * P + 4 * TP].rearrange("p (k b n) -> p k b n", k=2, b=2)
    return rest[:, 0], rest[:, 1]


class HalfTiles:

    RING = 4

    def __init__(self, nc, a, c, I, h, proj, work, name, first, count):
        self.nc, self.I, self.h, self.proj, self.first, self.count = nc, I, h, proj, first, count
        self.ring = ring_of(work)
        self.pp = a.ps(name + "_ps", [P, 2, 512])
        self.slots = c.slots
        self.made, self.copied = a.sem(name + "_product"), a.sem(name + "_copied")

    def load(self, eng, n):
        if n >= self.RING:
            eng.wait_ge(self.made, 2 * (n - self.RING) + 2)
        eng.dma_start(self.ring[:, n % self.RING], self.I["w_t"][self.first + n]).then_inc(
            self.slots.sems[n % self.RING], 16)

    def product(self, pe, i):
        n, j = i // 2, i % 2
        if j == 0:
            pe.wait_ge(*self.slots.landed(n))
        if n >= 1:
            pe.wait_ge(self.copied, i - 1)
        for k in range(DC):
            last = self.nc.tensor.matmul(self.pp[:, j, 0:HALF], self.ring[:, n % self.RING, k, :],
                                         self.h[:, k, j * HALF:(j + 1) * HALF], start=(k == 0), stop=(k == DC - 1))
        last.then_inc(self.made, 1)

    def copy(self, act, i, func):
        act.wait_ge(self.made, i + 1)
        self.nc.scalar.activation(self.proj[:, self.first + i // 2, (i % 2) * HALF:(i % 2 + 1) * HALF],
                                  self.pp[:, i % 2, 0:HALF], func).then_inc(self.copied, 1)


def index_keys(nc, I, c, h, proj, ikT, iwtok, maskp, maskS, work):
    R = TS * NH
    KR = 4
    with ExitStack() as ctx:
        a = Alloc(nc, ctx)
        tiles = HalfTiles(nc, a, c, I, h, proj, work, "hgw", HQ, ZA - HQ)
        ps = a.ps("ix_ps", [P, 2, 512])
        pS = a.ps("sx_ps", [P, 3, 512])
        pX = a.ps("sx_turn_ps", [P, 1, 512])
        rl, sc = rest_of(work)
        wk = a.sb("ix_work", [P, TP])
        m8 = a.sb("ix_max8", [P, 8])
        kx = a.sb("sx_kidx", [HD, KR, NPG, PG])
        qi = a.sb("sx_iq", [HD, TS, TS, NH])
        wx = a.sb("sx_iw", [TS, TS, NH])
        wb = a.sb("sx_iwT", [R, TS])
        srl = a.sb("sx_relu", [R, L])
        s_ps, s_rl, s_ac, s_v = (a.sem("ix_" + x) for x in ("product", "relu", "accumulated", "chain"))
        s_xl = [a.sem(f"sx_kidx_loaded{i}") for i in range(KR)]
        s_z, s_g, s_q, s_px, s_wT, s_sc, s_srl, s_cp = (a.sem("sx_" + x) for x in (
            "zeroed", "iwmask", "qblocks", "product", "iwturned", "scores", "relued", "iwT_copied"))
        block = ctx.enter_context(nc.Block())
        pSf = pS[:, :, :].rearrange("p a b -> p (a b)")
        pieces = ((0, 512), (512, 1024), (1024, L))
        steps = [(t, hd) for t in range(1, NT) for hd in range(NH)]
        first = 2 * NH
        more = tiles.RING + TS // 4

        def load_keys(eng, b):
            if b >= KR:
                eng.wait_ge(s_px, b - KR + 1)
            load_pages(eng, c, I["kidxT"], kx[:, b % KR], b, s_xl[b % KR])

        @block.sync
        def _(sp):
            for n in range(tiles.RING):
                tiles.load(sp, n)
            for b in range(0, TS, 2):
                load_keys(sp, b)
                if b == 2:
                    for n in range(tiles.RING, more):
                        tiles.load(sp, n)
            for n in range(more, tiles.count):
                tiles.load(sp, n)

        @block.gpsimd
        def _(pool):
            nc.gpsimd.memset(qi[:, :, :, :], 0.0).then_inc(s_z, 1)
            nc.gpsimd.tensor_tensor(wx[:, :, :], c.sel_b[:, :, :],
                                    iwtok[0:TS, NT, :].unsqueeze(1).to_broadcast([TS, TS, NH]), ALU.mult).then_inc(s_g, 1)
            for b in range(1, TS, 2):
                load_keys(pool, b)

        @block.tensor
        def _(pe):
            def score(n):
                t, hd = steps[n]
                S = (t + 1) * P
                r = HD * (hd % 2)
                if n >= 2:
                    pe.wait_ge(s_rl, n - 1)
                nc.tensor.matmul(ps[:, n % 2, 0:S], proj[r:r + HD, IQ + hd // 2, t * P:(t + 1) * P],
                                 ikT[r:r + HD, 0:S], start=True, stop=True).then_inc(s_ps, 1)

            for n in range(first):
                score(n)
                if n % 2:
                    tiles.product(pe, n // 2)
            pe.wait_ge(s_g, 1)
            nc.tensor.transpose(pX[0:R, 0, 0:TS], wx[:, :, :].rearrange("p a b -> p (a b)"),
                                c.ident[0:TS, 0:TS]).then_inc(s_wT, 1)
            pe.wait_ge(s_q, NH)
            for b in range(TS):
                pe.wait_ge(s_xl[b % KR], 16 * NPG * (b // KR + 1))
                q = qi[:, b, :, :].rearrange("p b h -> p (b h)")
                for s0, s1 in pieces:
                    k = (kx[:, b % KR].rearrange("p g n -> p (g n)")[:, s0:s1] if s0 < PAST
                         else ikT[0:HD, TP + b:TP + b + 1])
                    last = nc.tensor.matmul(pSf[0:R, s0:s1], q, k, start=(b == 0), stop=(b == TS - 1))
                last.then_inc(s_px, 1)
                if b % 2:
                    tiles.product(pe, first // 2 + b // 2)
            pe.wait_ge(s_srl, 1)
            pe.wait_ge(s_cp, 1)
            for s0, s1 in pieces:
                last = nc.tensor.matmul(pSf[0:TS, s0:s1], wb[:, :], srl[:, s0:s1], start=True, stop=True)
            last.then_inc(s_sc, 1)
            i = first // 2 + TS // 2
            for n in range(first, len(steps)):
                score(n)
                for _ in range({1: 3, 5: 1}.get(n % NH, 0)):
                    tiles.product(pe, i)
                    i += 1
            while i < 2 * tiles.count:
                tiles.product(pe, i)
                i += 1

        @block.scalar
        def _(act):
            def relu(n):
                t, hd = steps[n]
                S = (t + 1) * P
                act.wait_ge(s_ps, n + 1)
                if n >= 2:
                    act.wait_ge(s_ac, n - 1)
                nc.scalar.activation(rl[:, n % 2, 0:S], ps[:, n % 2, 0:S], ACT.Relu,
                                     scale=HD ** -0.5).then_inc(s_rl, 1)

            def copy(i):
                tiles.copy(act, i, ACT.Identity if i < 2 * (HF - HQ) else ACT.Sigmoid)

            for n in range(first):
                relu(n)
                if n % 2:
                    copy(n // 2)
            for i in range(first // 2, first // 2 + TS // 2):
                copy(i)
            act.wait_ge(s_px, TS)
            nc.scalar.activation(srl[:, :], pSf[0:R, 0:L], ACT.Relu, scale=HD ** -0.5).then_inc(s_srl, 1)
            i = first // 2 + TS // 2
            for n in range(first, len(steps)):
                relu(n)
                for _ in range({1: 3, 5: 1}.get(n % NH, 0)):
                    copy(i)
                    i += 1
            while i < 2 * tiles.count:
                copy(i)
                i += 1

        @block.vector
        def _(dve):
            link = Chain(dve, s_v)
            dve.wait_ge(s_z, 1)
            for hd in range(NH):
                r = HD * (hd % 2)
                d = qi[:, :, :, :].rearrange("p a b h -> p (a b h)")[:, hd:hd + 72 * 7 + 1:72]
                nc.vector.tensor_copy(d, proj[r:r + HD, IQ + hd // 2, TP:N]).then_inc(s_q, 1)
            nc.vector.memset(maskp[:, 0, :], 0.0)
            for n, (t, hd) in enumerate(steps):
                S = (t + 1) * P
                dve.wait_ge(s_rl, n + 1)
                if hd == 0:
                    ins = nc.vector.tensor_scalar(sc[:, 0, 0:S], rl[:, n % 2, 0:S], iwtok[:, t, 0:1], None, ALU.mult)
                else:
                    ins = nc.vector.scalar_tensor_tensor(out=sc[:, hd % 2, 0:S], in0=rl[:, n % 2, 0:S],
                                                         scalar=iwtok[:, t, hd:hd + 1],
                                                         in1=sc[:, (hd - 1) % 2, 0:S], op0=ALU.mult, op1=ALU.add)
                ins.then_inc(s_ac, 1)
                dve.wait_ge(s_ac, n + 1)
                if hd < NH - 1:
                    continue
                if t == 2:
                    dve.wait_ge(s_wT, 1)
                    nc.vector.tensor_copy(wb[:, :], pX[0:R, 0, 0:TS]).then_inc(s_cp, 1)
                f = sc[:, 1, :]
                link(nc.vector.tensor_tensor(f[:, t * P:S], f[:, t * P:S], c.causal[:, :], ALU.add))
                for k in range(TOPP // 8):
                    src = f if k == 0 else wk
                    link(nc.vector.max(m8[:, :], src[:, 0:S]))
                    link(nc.vector.match_replace(wk[:, 0:S], m8[:, :], src[:, 0:S], SENT))
                link(nc.vector.tensor_scalar(maskp[:, t, 0:S], wk[:, 0:S], SENT, OFF, ALU.not_equal, ALU.mult))
            dve.wait_ge(s_sc, 1)
            link(nc.vector.max(m8[0:TS, :], pSf[0:TS, 0:L]))
            link(nc.vector.match_replace(maskS[:, :], m8[0:TS, :], pSf[0:TS, 0:L], SENT))


def load_pages(eng, c, src, dst, b, sem):
    for g in range(NPG):
        page = eng.value_load(c.small["pages"][0:1, b * NPG + g:b * NPG + g + 1], min_val=0, max_val=c.n_phys - 1)
        eng.dma_start(dst[:, g, :], src[bass.ds(page, 1), :, :].rearrange("a p n -> p (a n)")).then_inc(sem, 16)


def attend_prompt(nc, I, c, h, proj, vtok, maskp, maskS, skew, attT, work):
    with ExitStack() as ctx:
        a = Alloc(nc, ctx)
        pl = a.ps("at_logit_ps", [P, 2, 512])
        px = a.ps("at_turn_ps", [P, 2, 512])
        po = a.ps("at_out_ps", [P, 1, 512])
        pa = a.ps("at_att_ps", [P, 1, 512])
        tiles = HalfTiles(nc, a, c, I, h, proj, work, "gate", ZA, MT - ZA)
        toep = a.sb("toep", [P, NH, TP])
        s_i = [a.sem(f"at_bias_loaded{k}") for k in range(NH // 2)]
        lg, pr = rest_of(work)
        lm = lg
        pT = a.sb("at_probT", [P, 2, TP])
        m8 = a.sb("at_max8", [TS, 8])
        s_k = a.sem("at_topk_chain")
        mx = a.sb("at_max", [P, NT, NH])
        nm = a.sb("at_negmax", [P, NT, NH])
        sm = a.sb("at_sum", [P, NT, NH])
        rc = a.sb("at_recip", [P, NT, NH])
        at = a.sb("at_att", [P, 1, 512])
        s_l, s_b, s_m, s_n, s_e, s_x, s_c, s_o, s_r, s_a, s_t, s_f = (a.sem("at_" + x) for x in (
            "product", "biased", "masked", "negmax_made", "exp", "turned", "turn_copied", "pv", "recip_made",
            "normalised", "att_turned", "att_copied"))
        block = ctx.enter_context(nc.Block())
        heads = [(t, m, g) for t in range(NT) for m in range(4) for g in range(2)]

        @block.sync
        def _(sp):
            tiles.load(sp, 0)
            for k in range(NH // 2):
                part = bass.AP(tensor=skew.tensor, offset=P - 1 + k * P * SK,
                               ap=[[SK - 1, P], [NH // 2 * P * SK, 2], [1, TP]])
                sp.dma_start(toep[:, k::NH // 2, :], part).then_inc(s_i[k], 16)
            for n in range(1, tiles.count):
                tiles.load(sp, n)

        @block.tensor
        def _(pe):
            def logits(n):
                t, m, g = heads[n]
                S = (t + 1) * P
                if n >= 2:
                    pe.wait_ge(s_b, n - 1)
                nc.tensor.matmul(pl[:, n % 2, 0:S], proj[HD * g:HD * g + HD, AQ + m, t * P:S],
                                 proj[HD * g:HD * g + HD, AK, 0:S], start=True, stop=True).then_inc(s_l, 1)

            def turn(n):
                t, m, g = heads[n]
                pe.wait_ge(s_e, n + 1)
                if n >= 2:
                    pe.wait_ge(s_c, n - 1)
                for k in range(t + 1):
                    last = nc.tensor.transpose(px[:, n % 2, k * P:(k + 1) * P], pr[:, n % 2, k * P:(k + 1) * P],
                                               c.ident[:, :])
                last.then_inc(s_x, 1)

            def pv(n):
                t, m, g = heads[n]
                pe.wait_ge(s_c, n + 1)
                if n % 8 == 0 and t >= 1:
                    pe.wait_ge(s_a, t)
                o = (2 * m + g) * HD
                for k in range(t + 1):
                    last = nc.tensor.matmul(po[:, 0, o:o + HD], pT[:, n % 2, k * P:(k + 1) * P],
                                            vtok[:, k, g * HD:g * HD + HD], start=(k == 0), stop=(k == t))
                last.then_inc(s_o, 1)

            def att(t):
                pe.wait_ge(s_a, t + 1)
                if t >= 1:
                    pe.wait_ge(s_f, t)
                for m in range(4):
                    last = nc.tensor.transpose(pa[:, 0, m * P:(m + 1) * P], at[:, 0, m * P:(m + 1) * P],
                                               c.ident[:, :])
                last.then_inc(s_t, 1)

            logits(0)
            for n in range(len(heads)):
                if n + 1 < len(heads):
                    logits(n + 1)
                if n == 0:
                    tiles.product(pe, 0)
                turn(n)
                if n > 0:
                    tiles.product(pe, n)
                pv(n)
                if n % 8 == 7:
                    att(n // 8)

        @block.vector
        def _(dve):
            def score(n):
                t, m, g = heads[n]
                S = (t + 1) * P
                h = m + 4 * g
                u = TP - S
                if t == 0 and g == 0:
                    dve.wait_ge(s_i[m], 16)
                dve.wait_ge(s_l, n + 1)
                if n >= 2:
                    dve.wait_ge(s_e, n - 1)
                nc.vector.scalar_tensor_tensor(out=lg[:, n % 2, 0:S], in0=pl[:, n % 2, 0:S], scalar=HD ** -0.5,
                                               in1=toep[:, h, u:TP], op0=ALU.mult, op1=ALU.add).then_inc(s_b, 1)
                dve.wait_ge(s_b, n + 1)
                nc.vector.tensor_tensor_reduce(out=lm[:, n % 2, 0:S], in0=lg[:, n % 2, 0:S],
                                               in1=maskp[:, t, 0:S], scale=1.0, scalar=-3.0e38, op0=ALU.add,
                                               op1=ALU.max, accum_out=mx[:, t, h:h + 1]).then_inc(s_m, 1)
                dve.wait_ge(s_m, n + 1)
                nc.vector.tensor_scalar(nm[:, t, h:h + 1], mx[:, t, h:h + 1], -1.0, None, ALU.mult).then_inc(s_n, 1)

            def turned(n):
                t, m, g = heads[n]
                S = (t + 1) * P
                dve.wait_ge(s_x, n + 1)
                if n >= 2:
                    dve.wait_ge(s_o, n - 1)
                nc.vector.tensor_copy(pT[:, n % 2, 0:S], px[:, n % 2, 0:S]).then_inc(s_c, 1)

            pick = Chain(dve, s_k)
            score(0)
            for n in range(len(heads)):
                if n + 1 < len(heads):
                    score(n + 1)
                turned(n)
                if n < TOPS // 8 - 1:
                    pick(nc.vector.max(m8[:, :], maskS[:, :]))
                    pick(nc.vector.match_replace(maskS[:, :], m8[:, :], maskS[:, :], SENT))
                elif n == TOPS // 8 - 1:
                    pick(nc.vector.tensor_scalar(maskS[:, :], maskS[:, :], SENT, OFF, ALU.not_equal, ALU.mult))
                if n % 8 == 7:
                    t = n // 8
                    dve.wait_ge(s_e, n + 1)
                    nc.vector.reciprocal(rc[:, t, :], sm[:, t, :]).then_inc(s_r, 1)
                    dve.wait_ge(s_r, t + 1)
                    dve.wait_ge(s_o, n + 1)
                    r = rc[:, t, :].rearrange("p (g m) -> p m g", g=2).unsqueeze(3).to_broadcast([P, 4, 2, HD])
                    nc.vector.tensor_tensor(at[:, 0, :].rearrange("p (m g d) -> p m g d", m=4, g=2),
                                            po[:, 0, :].rearrange("p (m g d) -> p m g d", m=4, g=2),
                                            r, ALU.mult).then_inc(s_a, 1)
                    dve.wait_ge(s_t, t + 1)
                    nc.vector.tensor_copy(attT[:, :, t * P:(t + 1) * P],
                                          pa[:, 0, :].rearrange("p (m n) -> p m n", m=4)).then_inc(s_f, 1)

        @block.scalar
        def _(act):
            def exp(n):
                t, m, g = heads[n]
                S = (t + 1) * P
                h = m + 4 * g
                act.wait_ge(s_n, n + 1)
                if n >= 2:
                    act.wait_ge(s_x, n - 1)
                nc.scalar.activation(pr[:, n % 2, 0:S], lm[:, n % 2, 0:S], ACT.Exp, bias=nm[:, t, h:h + 1],
                                     accum_out=sm[:, t, h:h + 1]).then_inc(s_e, 1)

            exp(0)
            for n in range(len(heads)):
                if n + 1 < len(heads):
                    exp(n + 1)
                tiles.copy(act, n, ACT.Sigmoid)


def sample_attention(nc, I, c, proj, vtok, rev, mk, attT, spare, dec):
    R = TS * NH
    with ExitStack() as ctx:
        a = Alloc(nc, ctx)
        kc = a.sb("sa_k", [P, 4, NPG, PG])
        vc = a.sb("sa_v", [P, 2, NPG, P])
        more = spare.rearrange("p h n -> p (h n)")[:, 0:2 * NPG * P].rearrange("p (b g n) -> p b g n", b=2, g=NPG)
        values = [vc[:, 0], vc[:, 1], more[:, 0], more[:, 1]] + [kc[:, k] for k in range(4)]
        qa = a.sb("sa_q", [P, TS, TS, NH])
        mx = a.sb("sa_max", [R, 4])
        pr = a.sb("sa_prob", [R, L])
        pT = a.sb("sa_probT", [P, NPG, R])
        pn = a.sb("sa_new", [R, TS])
        pnT = a.sb("sa_newT", [TS, R])
        out = pr[0:NH, 0:TS * P].rearrange("h (b d) -> h b d", b=TS)
        pS = a.ps("sa_ps", [P, 3, 512])
        pC = a.ps("sa_score_ps", [P, 3, 512])
        pX = a.ps("sa_turn_ps", [P, 1, 512])
        pO = a.ps("sa_out_ps", [P, 1, 512])
        s_kl = [a.sem(f"sa_k_loaded{i}") for i in range(4)]
        s_vl = [a.sem(f"sa_v_loaded{i}") for i in range(TS // 2)]
        s_z, s_q, s_pk, s_v, s_e, s_tn, s_tc, s_ov, s_nm = (a.sem("sa_" + x) for x in (
            "zeroed", "qblocks", "kprod", "dve_chain", "exp", "turned", "turn_copied", "out", "negmax"))
        block = ctx.enter_context(nc.Block())
        pSf = pS[:, :, :].rearrange("p a b -> p (a b)")
        pCf = pC[:, :, :].rearrange("p a b -> p (a b)")
        pieces = ((0, 512), (512, 1024), (1024, L))

        def load_k(eng, b):
            if b >= 4:
                eng.wait_ge(s_pk, b - 3)
            load_pages(eng, c, I["kT"], kc[:, b % 4], b, s_kl[b % 4])

        def load_v(eng, b):
            if b >= 4:
                eng.wait_ge(s_pk, b + 1)
            load_pages(eng, c, I["vC"], values[b], b, s_vl[b // 2])

        @block.sync
        def _(sp):
            for b in (0, 4, 5):
                load_k(sp, b)
            for b in (2, 3, 4, 5):
                load_v(sp, b)

        @block.gpsimd
        def _(pool):
            nc.gpsimd.memset(qa[:, :, :, :], 0.0).then_inc(s_z, 1)
            for b in (2, 3, 6, 7):
                load_k(pool, b)
            for b in (0, 1):
                load_v(pool, b)

        @block.scalar
        def _(act):
            load_k(act, 1)
            dec.exponentials(act)
            act.wait_ge(s_nm, 1)
            nc.scalar.activation(pr[:, :], pSf[0:R, 0:L], ACT.Exp, bias=mx[:, 1:2],
                                 accum_out=mx[:, 2:3]).then_inc(s_e, 1)
            for b in (6, 7):
                load_v(act, b)

        @block.vector
        def _(dve):
            link = Chain(dve, s_v)
            dve.wait_ge(s_z, 1)
            for m in range(4):
                for g in range(2):
                    h = m + 4 * g
                    d = qa[:, :, :, :].rearrange("p a b h -> p (a b h)")[HD * g:HD * g + HD, h:h + 72 * 7 + 1:72]
                    nc.vector.tensor_scalar(d, proj[HD * g:HD * g + HD, AQ + m, TP:N], HD ** -0.5, None,
                                            ALU.mult).then_inc(s_q, 1)
            dec.factors(dve)
            dve.wait_ge(s_pk, TS + 1)
            link(nc.vector.tensor_reduce(mx[:, 0:1], pSf[0:R, 0:L], X, ALU.max))
            nc.vector.tensor_scalar(mx[:, 1:2], mx[:, 0:1], -1.0, None, ALU.mult).then_inc(s_nm, 1)
            dve.wait_ge(s_e, 1)
            link(nc.vector.reciprocal(mx[:, 3:4], mx[:, 2:3]))
            link(nc.vector.tensor_scalar(pr[:, :], pr[:, :], mx[:, 3:4], None, ALU.mult))
            link(nc.vector.tensor_scalar(pn[:, :], c.selT[:, :], pr[:, PAST:L], None, ALU.mult))
            dve.wait_ge(s_tn, 1)
            nc.vector.tensor_copy(pT[:, :, :], pX[:, 0, :].rearrange("p (g r) -> p g r", r=R)).then_inc(s_tc, 1)
            dve.wait_ge(s_tn, 2)
            nc.vector.tensor_copy(pnT[:, :], pC[0:TS, 0, 0:R]).then_inc(s_tc, 1)
            for k in range(2):
                dve.wait_ge(s_ov, 4 * k + 4)
                nc.vector.tensor_copy(out[:, 4 * k:4 * k + 4, :].rearrange("h b d -> h (b d)"), pC[0:NH, 1 + k, :]
                                      ).then_inc(s_tc, 1)
            dve.wait_ge(s_tn, 3)
            for m in range(4):
                for g in range(2):
                    h = m + 4 * g
                    src = pO[HD * g:HD * g + HD, 0, 0:R].rearrange("p (b h) -> p b h", h=NH)[:, :, h]
                    nc.vector.tensor_copy(attT[HD * g:HD * g + HD, m, TP:N], src).then_inc(s_tc, 1)

        @block.tensor
        def _(pe):
            pe.wait_ge(s_q, NH)
            for b in range(TS):
                pe.wait_ge(s_kl[b % 4], 16 * NPG * (b // 4 + 1))
                q = qa[:, b, :, :].rearrange("p b h -> p (b h)")
                for s0, s1 in pieces:
                    k = (kc[:, b % 4].rearrange("p g n -> p (g n)")[:, s0:s1] if s0 < PAST
                         else proj[:, AK, TP + b:TP + b + 1])
                    last = nc.tensor.matmul(pSf[0:R, s0:s1], q, k, start=(b == 0), stop=False)
                last.then_inc(s_pk, 1)
            for s0, s1 in pieces:
                nc.tensor.matmul(pSf[0:R, s0:s1], c.sel_h[:, :, :].rearrange("p a b -> p (a b)"), rev[:, s0:s1],
                                 start=False, stop=False)
                last = nc.tensor.matmul(pSf[0:R, s0:s1], c.sel_b[:, :, :].rearrange("p a b -> p (a b)"), mk[:, s0:s1],
                                        start=False, stop=True)
            last.then_inc(s_pk, 1)
            pe.wait_ge(s_v, 4)
            for g in range(NPG):
                last = nc.tensor.transpose(pX[:, 0, g * R:(g + 1) * R], pr[:, g * PG:(g + 1) * PG], c.ident[0:R, 0:R])
            last.then_inc(s_tn, 1)
            nc.tensor.transpose(pC[0:TS, 0, 0:R], pn[:, :], c.ident[0:R, 0:R]).then_inc(s_tn, 1)
            pe.wait_ge(s_tc, 2)
            for b in range(TS):
                if b % 2 == 0:
                    pe.wait_ge(s_vl[b // 2], 16 * NPG * 2)
                o = pC[0:NH, 1 + b // 4, b % 4 * P:(b % 4 + 1) * P]
                nc.tensor.matmul(o, pnT[:, b * NH:(b + 1) * NH], vtok[0:TS, NT, :], start=True, stop=False,
                                 skip_group_check=True)
                for g in range(NPG):
                    last = nc.tensor.matmul(o, pT[:, g, b * NH:(b + 1) * NH], values[b][:, g, :], start=False,
                                            stop=(g == NPG - 1), skip_group_check=True)
                last.then_inc(s_ov, 1)
            pe.wait_ge(s_tc, 4)
            for b in range(TS):
                last = nc.tensor.transpose(pO[:, 0, b * NH:(b + 1) * NH], out[:, b, :], c.ident[0:NH, 0:NH])
            last.then_inc(s_tn, 1)


class Decays:

    M = CH // 2 - 1

    def __init__(self, nc, a, c, xn, proj, work):
        self.nc, self.c, self.proj = nc, c, proj
        self.free = work
        self.kk = xn[:, 0:HG, :]
        self.ff = proj[:, HF:HF + HG, :]
        self.q1, self.k1 = proj[:, AQ:AQ + HG, 0:TP], proj[:, IQ:IQ + HG, 0:TP]
        self.lb = a.sb("hg_lb", [P, 8, HG])
        w, n = self.free, HG * TP
        self.bb = w[:, 0:n].rearrange("p (h n) -> p h n", h=HG)
        self.q2 = w[:, n:2 * n].rearrange("p (h n) -> p h n", h=HG)
        self.dd = w[:, 2 * n:2 * n + HG * N].rearrange("p (h n) -> p h n", h=HG)
        self.el = a.sb("hg_decay", [P, HG, NCH])
        self.be = a.sb("hg_b_end", [P, HG, NCH])
        (self.s_v, self.s_a, self.s_lb, self.s_f, self.s_b, self.s_d1, self.s_d2, self.s_w, self.s_e) = (
            a.sem("hg_" + k) for k in ("dve_chain", "act", "lbdiff", "f_made", "b_made", "mid_diff",
                                       "end_diff", "weighted", "exps"))

    def exponentials(self, act):
        nc, lb, ff, bb, dd, q1, k1, q2, el = (self.nc, self.lb, self.ff, self.bb, self.dd, self.q1, self.k1,
                                              self.q2, self.el)
        s_a, s_lb, s_f, s_d1, s_d2, s_e = self.s_a, self.s_lb, self.s_f, self.s_d1, self.s_d2, self.s_e
        act.wait_ge(s_lb, 1)
        nc.scalar.activation(lb[:, 3:5, :], lb[:, 1:3, :], ACT.Exp).then_inc(s_a, 1)
        act.wait_ge(s_f, HG)
        for h in range(HG):
            nc.scalar.activation(dd[:, h, 0:TP], ff[:, h, 0:TP], ACT.Ln).then_inc(s_a, 1)
        for h in range(HG):
            act.wait_ge(s_d1, h + 1)
            nc.scalar.activation(q1[:, h, :], dd[:, h, 0:TP], ACT.Exp).then_inc(s_e, 1)
            nc.scalar.activation(k1[:, h, :], dd[:, h, 0:TP], ACT.Exp, scale=-1.0).then_inc(s_e, 1)
            nc.scalar.activation(q2[:, h, :], bb[:, h, :], ACT.Exp).then_inc(s_e, 1)
            nc.scalar.activation(el[:, h, :], chunks(bb, h)[:, :, CH - 1], ACT.Exp).then_inc(s_e, 1)
        for h in range(HG):
            act.wait_ge(s_d2, h + 1)
            nc.scalar.activation(dd[:, h, 0:TP], bb[:, h, :], ACT.Exp, scale=-1.0).then_inc(s_e, 1)

    def factors(self, dve):
        nc, c, proj, M = self.nc, self.c, self.proj, self.M
        lb, ff, kk, bb, dd, q1, k1, q2, be = (self.lb, self.ff, self.kk, self.bb, self.dd, self.q1, self.k1,
                                              self.q2, self.be)
        s_v, s_a, s_lb, s_f, s_b = self.s_v, self.s_a, self.s_lb, self.s_f, self.s_b
        s_d1, s_d2, s_w, s_e = self.s_d1, self.s_d2, self.s_w, self.s_e
        link = Chain(dve, s_v)
        l = c.small["lbl"]
        link(nc.vector.tensor_tensor(lb[:, 0, :], l[:, 0, :], l[:, 1, :], ALU.max))
        link(nc.vector.tensor_tensor(lb[:, 1, :], l[:, 0, :], lb[:, 0, :], ALU.subtract))
        nc.vector.tensor_tensor(lb[:, 2, :], l[:, 1, :], lb[:, 0, :], ALU.subtract).then_inc(s_lb, 1)
        dve.wait_ge(s_a, 1)
        link(nc.vector.tensor_tensor(lb[:, 5, :], lb[:, 3, :], lb[:, 4, :], ALU.add))
        link(nc.vector.reciprocal(lb[:, 6, :], lb[:, 5, :]))
        link(nc.vector.tensor_tensor(lb[:, 7, :], lb[:, 3, :], lb[:, 6, :], ALU.mult))
        link(nc.vector.tensor_scalar(lb[:, 0, :], lb[:, 7, :], -1.0, 1.0, ALU.mult, ALU.add))
        for h in range(HG):
            nc.vector.tensor_scalar(ff[:, h, :], proj[:, HF + h, :], lb[:, 0, h:h + 1], lb[:, 7, h:h + 1],
                                    ALU.mult, ALU.add).then_inc(s_f, 1)
        dve.wait_ge(s_f, HG)
        for h in range(HG):
            nc.vector.tensor_scalar(kk[:, h, :], ff[:, h, :], -1.0, 1.0, ALU.mult, ALU.add).then_inc(s_f, 1)
        for h in range(HG):
            dve.wait_ge(s_a, 2 + h)
            nc.vector.tensor_tensor_scan(bb[:, h, :], c.reset[:, :], dd[:, h, 0:TP], 0.0, ALU.mult,
                                         ALU.add).then_inc(s_b, 1)
        for h in range(HG):
            dve.wait_ge(s_b, h + 1)
            b = chunks(bb, h)
            nc.vector.tensor_tensor(chunks(dd, h), b, b[:, :, M:M + 1].to_broadcast([P, NCH, CH]),
                                    ALU.subtract).then_inc(s_d1, 1)
        dve.wait_ge(s_f, 2 * HG)
        for h in range(HG):
            dve.wait_ge(s_e, 4 * h + 4)
            b = chunks(bb, h)
            link(nc.vector.tensor_copy(be[:, h, :], b[:, :, CH - 1]))
            nc.vector.tensor_tensor(b, b, be[:, h, :].unsqueeze(2).to_broadcast([P, NCH, CH]),
                                    ALU.subtract).then_inc(s_d2, 1)
            nc.vector.tensor_tensor(q1[:, h, :], q1[:, h, :], proj[:, HQ + h, 0:TP], ALU.mult).then_inc(s_w, 1)
            nc.vector.tensor_tensor(k1[:, h, :], k1[:, h, :], kk[:, h, 0:TP], ALU.mult).then_inc(s_w, 1)
            nc.vector.tensor_tensor(q2[:, h, :], q2[:, h, :], proj[:, HQ + h, 0:TP], ALU.mult).then_inc(s_w, 1)
        for h in range(HG):
            dve.wait_ge(s_e, 4 * HG + h + 1)
            nc.vector.tensor_tensor(dd[:, h, 0:TP], dd[:, h, 0:TP], kk[:, h, 0:TP], ALU.mult).then_inc(s_w, 1)
        dve.wait_ge(s_w, 4 * HG)


def chunks(t, h):
    return t[:, h, 0:TP].rearrange("p (c k) -> p c k", k=CH)


def hgrn(nc, I, O, c, dec, proj, hitok, hgoT):
    RS = 2 * (P // CH) + 1
    with ExitStack() as ctx:
        a = Alloc(nc, ctx)
        kk, ff, dd, q1, k1, q2, el = dec.kk, dec.ff, dec.dd, dec.q1, dec.k1, dec.q2, dec.el
        k2T = dec.bb[:, :, :].rearrange("p h (t n) -> p h t n", t=NT)
        AT = a.sb("hg_scores", [P, 2, HG, P])
        st = a.sb("hg_state", [P, RS, HG, P])
        oT = hgoT
        ss = a.sb("hg_sample_state", [P, TS, HG, P])
        kv = a.sb("hg_sample_kv", [P, 2, HG, P])
        pA = a.ps("hg_ps_a", [P, 2, 512])
        pB = a.ps("hg_ps_b", [P, 2, 512])
        pO = a.ps("hg_ps_o", [P, 4, 512])
        s_d, s_o = a.sem("hg_loaded"), a.sem("hg_stored")
        s_x, s_xc, s_s, s_sc, s_u, s_st, s_oo, s_oc = (a.sem("hg_" + x) for x in (
            "turned", "turn_copied", "scores_made", "scores_masked", "kv_made", "state", "out_made", "out_copied"))
        s_vc, s_vb, s_ss, s_so = (a.sem("hg_" + x) for x in ("v_used", "v_spread", "sample_state_made", "sample_out"))
        s_m = a.sem("hg_zero_state")
        with nc.Block() as block:
            @block.tensor
            def _(pe):
                for h in range(HG):
                    if h >= 2:
                        pe.wait_ge(s_xc, h - 1)
                    for t in range(NT):
                        last = nc.tensor.transpose(pA[:, h % 2, t * P:(t + 1) * P], dd[:, h, t * P:(t + 1) * P],
                                                   c.ident[:, :])
                    last.then_inc(s_x, 1)
                pe.wait_ge(s_xc, HG)

                def kv_of(n):
                    t, r = n * CH // P, n * CH % P
                    if n >= 2:
                        pe.wait_ge(s_st, (n - 1) * HG)
                    for h in range(HG):
                        last = nc.tensor.matmul(pB[:, n % 2, h * P:(h + 1) * P], k2T[r:r + CH, h, t, :],
                                                hitok[r:r + CH, t, h * P:(h + 1) * P], start=True, stop=True)
                    last.then_inc(s_u, 1)

                def scores(t):
                    if t >= 2:
                        pe.wait_ge(s_sc, t - 1)
                    for h in range(HG):
                        last = nc.tensor.matmul(pA[:, t % 2, h * P:(h + 1) * P], k1[:, h, t * P:(t + 1) * P],
                                                q1[:, h, t * P:(t + 1) * P], start=True, stop=True)
                    last.then_inc(s_s, 1)

                def out(t):
                    pe.wait_ge(s_sc, t + 1)
                    pe.wait_ge(s_st, (4 * t + 3) * HG)
                    if t >= 2:
                        pe.wait_ge(s_oc, t - 1)
                    for h in range(HG):
                        o = pO[:, t % 2, h * P:(h + 1) * P]
                        nc.tensor.matmul(o, hitok[:, t, h * P:(h + 1) * P], AT[:, t % 2, h, :],
                                         start=True, stop=False, skip_group_check=True)
                        for j in range(P // CH):
                            n = t * (P // CH) + j
                            last = nc.tensor.matmul(o[:, j * CH:(j + 1) * CH], st[:, n % RS, h, :],
                                                    q2[:, h, n * CH:(n + 1) * CH], start=False,
                                                    stop=(j == P // CH - 1), skip_group_check=True)
                    last.then_inc(s_oo, 1)

                def spread(b):
                    if b >= 1:
                        pe.wait_ge(s_vc, b)
                    nc.tensor.matmul(pO[:, 2, :], c.pick[:, b, :], hitok[0:TS, NT, :],
                                     start=True, stop=True).then_inc(s_vb, 1)

                def sample_out(b):
                    pe.wait_ge(s_ss, b + 1)
                    for h in range(HG):
                        last = nc.tensor.matmul(pO[:, 3, h * TS + b:h * TS + b + 1], ss[:, b, h, :],
                                                proj[:, HQ + h, TP + b:TP + b + 1], start=True, stop=True)
                    last.then_inc(s_so, 1)

                for t in range(NT):
                    spread(2 * t)
                    scores(t)
                    for j in range(P // CH):
                        kv_of(t * (P // CH) + j)
                    if t >= 1:
                        sample_out(2 * t - 1)
                    out(t)
                    spread(2 * t + 1)
                    sample_out(2 * t)
                sample_out(TS - 1)

            @block.vector
            def _(dve):
                def sample(b):
                    if b == 0:
                        dve.wait_ge(s_d, 16)
                    dve.wait_ge(s_vb, b + 1)
                    for h in range(HG):
                        ins = nc.vector.tensor_scalar(kv[:, b % 2, h, :], pO[:, 2, h * P:(h + 1) * P],
                                                      kk[:, h, TP + b:TP + b + 1], None, ALU.mult)
                    ins.then_inc(s_vc, 1)
                    dve.wait_ge(s_vc, b + 1)
                    for h in range(HG):
                        ins = nc.vector.scalar_tensor_tensor(out=ss[:, b, h, :], in0=ss[:, b, h, :],
                                                             scalar=ff[:, h, TP + b:TP + b + 1], in1=kv[:, b % 2, h, :],
                                                             op0=ALU.mult, op1=ALU.add)
                    ins.then_inc(s_ss, 1)

                nc.vector.memset(st[:, 0, :, :], 0.0).then_inc(s_m, 1)
                for h in range(HG):
                    dve.wait_ge(s_x, h + 1)
                    nc.vector.tensor_copy(k2T[:, h, :, :], pA[:, h % 2, :].rearrange("p (t n) -> p t n", t=NT)
                                          ).then_inc(s_xc, 1)
                dve.wait_ge(s_m, 1)
                for t in range(NT):
                    dve.wait_ge(s_s, t + 1)
                    if t >= 2:
                        dve.wait_ge(s_oo, t - 1)
                    for h in range(HG):
                        ins = nc.vector.scalar_tensor_tensor(out=AT[:, t % 2, h, :], in0=pA[:, t % 2, h * P:(h + 1) * P],
                                                             scalar=3.0e38, in1=c.tri[:, :], op0=ALU.min, op1=ALU.mult)
                    ins.then_inc(s_sc, 1)
                    for j in range(P // CH):
                        n = t * (P // CH) + j
                        dve.wait_ge(s_u, n + 1)
                        if n >= 1:
                            dve.wait_ge(s_st, n * HG)
                        for h in range(HG):
                            nc.vector.scalar_tensor_tensor(out=st[:, (n + 1) % RS, h, :], in0=st[:, n % RS, h, :],
                                                           scalar=el[:, h, n:n + 1], in1=pB[:, n % 2, h * P:(h + 1) * P],
                                                           op0=ALU.mult, op1=ALU.add).then_inc(s_st, 1)
                    sample(2 * t)
                    dve.wait_ge(s_oo, t + 1)
                    nc.vector.tensor_copy(oT[:, :, t * P:(t + 1) * P], pO[:, t % 2, :].rearrange("p (h n) -> p h n", h=HG)
                                          ).then_inc(s_oc, 1)
                    sample(2 * t + 1)
                dve.wait_ge(s_so, TS)
                nc.vector.tensor_copy(oT[:, :, TP:N], pO[:, 3, 0:HG * TS].rearrange("p (h b) -> p h b", h=HG)
                                      ).then_inc(s_oc, 1)
                dve.wait_ge(s_oc, NT + 1)

            @block.sync
            def _(sp):
                sp.dma_start(ss[:, :, :, :], I["state"]).then_inc(s_d, 16)
                for b in range(0, TS - 2, 2):
                    sp.wait_ge(s_ss, b + 2)
                    sp.dma_start(O["hg_s"][:, b:b + 2], ss[:, b:b + 2]).then_inc(s_o, 16)
                sp.wait_ge(s_st, NCH * HG)
                sp.dma_start(O["hg_p"], st[:, NCH % RS, :, :]).then_inc(s_o, 16)
                for b in range(TS - 2, TS):
                    sp.wait_ge(s_ss, b + 1)
                    sp.dma_start(O["hg_s"][:, b], ss[:, b]).then_inc(s_o, 16)
                sp.wait_ge(s_o, 16 * (TS // 2 + 2))


def merge(nc, I, c, proj, attT, hgoT, dec, x):
    RING = 4
    with ExitStack() as ctx:
        a = Alloc(nc, ctx)
        ring = a.sb("mg_ring", [P, RING, 2, DC, P])
        mix = dec.free[:, 0:DC * N].rearrange("p (m n) -> p m n", m=DC)
        tb = a.sb("mg_b", [P, 2, N])
        pa = a.ps("mg_ps_a", [P, 2, 2, 512])
        pb = a.ps("mg_ps_b", [P, 2, 2, 512])
        s_p, s_q, s_ga, s_gb, s_m, s_o, s_x = (a.sem("mg_" + k) for k in (
            "att_product", "hgrn_product", "att_gated", "hgrn_gated", "mixed", "out_product", "added"))
        s_sq, s_ms, s_rt, s_sg, s_n = (a.sem("mg_" + k) for k in (
            "squared", "mean", "root", "sigmoid", "norm_chain"))
        sq, rt, sg = dec.kk, dec.ff, proj[:, AQ:AQ + HG, :]
        block = ctx.enter_context(nc.Block())

        @block.sync
        def _(sp):
            for n in range(DC):
                if n >= RING:
                    sp.wait_ge(s_q, 2 * (n - RING) + 2)
                src = I["w_ab"] if n < DC // 2 else I["w_out"]
                k = 2 * n % DC
                sp.dma_start(ring[:, n % RING], src[k:k + 2].rearrange("t p c n -> p t c n")
                             ).then_inc(c.slots.sems[n % RING], 16)

        @block.scalar
        def _(act):
            for h in range(HG):
                nc.scalar.activation(sq[:, h, :], hgoT[:, h, :], ACT.Square).then_inc(s_sq, 1)
            for h in range(HG):
                act.wait_ge(s_ms, h + 1)
                nc.scalar.activation(halves(rt[:, h, :]), pb[:, h % 2, :, 0:HALF], ACT.Sqrt,
                                     scale=1.0 / P, bias=c.eps[:, 0:1]).then_inc(s_rt, 1)
            for h in range(HG):
                nc.scalar.activation(sg[:, h, :], proj[:, HGT + h, :], ACT.Sigmoid).then_inc(s_sg, 1)

        @block.tensor
        def _(pe):
            for h in range(HG):
                pe.wait_ge(s_sq, h + 1)
                if h >= 2:
                    pe.wait_ge(s_rt, h - 1)
                for j in range(2):
                    last = nc.tensor.matmul(pb[:, h % 2, j, 0:HALF], c.ones[:, :],
                                            sq[:, h, j * HALF:(j + 1) * HALF], start=True, stop=True)
                last.then_inc(s_ms, 1)

            def half_width(m, ps, src, k0):
                for j in range(2):
                    for k in range(4):
                        last = nc.tensor.matmul(ps[:, m % 2, j, 0:HALF], ring[:, m // 2, m % 2, k0 + k, :],
                                                src[:, k, j * HALF:(j + 1) * HALF], start=(k == 0), stop=(k == 3))
                return last

            for m in range(DC):
                if m % 2 == 0:
                    pe.wait_ge(*c.slots.landed(m // 2))
                if m >= 2:
                    pe.wait_ge(s_ga, m - 1)
                half_width(m, pa, attT, 0).then_inc(s_p, 1)
            pe.wait_ge(s_n, 4 * HG)
            for m in range(DC):
                if m >= 2:
                    pe.wait_ge(s_gb, m - 1)
                half_width(m, pb, hgoT, 4).then_inc(s_q, 1)
            pe.wait_ge(s_ga, DC)
            for m in range(DC):
                if m == 0:
                    pe.wait_ge(s_m, DC)
                if m % 2 == 0:
                    pe.wait_ge(*c.slots.landed((DC + m) // 2))
                if m >= 2:
                    pe.wait_ge(s_x, m - 1)
                for j in range(2):
                    for k in range(DC):
                        last = nc.tensor.matmul(pa[:, m % 2, j, 0:HALF], ring[:, m // 2, m % 2, k, :],
                                                mix[:, k, j * HALF:(j + 1) * HALF],
                                                start=(k == 0), stop=(k == DC - 1))
                last.then_inc(s_o, 1)

        @block.vector
        def _(dve):
            link = Chain(dve, s_n)

            def norm(h):
                dve.wait_ge(s_rt, h + 1)
                link(nc.vector.reciprocal(rt[:, h, :], rt[:, h, :]))
                link(nc.vector.scalar_tensor_tensor(out=hgoT[:, h, :], in0=hgoT[:, h, :],
                                                    scalar=c.small["g_hgrn"][:, 0:1], in1=rt[:, h, :],
                                                    op0=ALU.mult, op1=ALU.mult))
                link(nc.vector.tensor_tensor(hgoT[:, h, :], hgoT[:, h, :], proj[:, HGT + h, :], ALU.mult))

            def gate_att(m):
                dve.wait_ge(s_p, m + 1)
                nc.vector.tensor_tensor(halves(mix[:, m, :]), pa[:, m % 2, :, 0:HALF], halves(proj[:, ZA + m, :]),
                                        ALU.mult).then_inc(s_ga, 1)

            norm(0)
            for h in range(1, HG):
                norm(h)
                gate_att(2 * h - 2)
                gate_att(2 * h - 1)
            for h in range(HG):
                dve.wait_ge(s_sg, h + 1)
                link(nc.vector.tensor_tensor(hgoT[:, h, :], hgoT[:, h, :], sg[:, h, :], ALU.mult))
            gate_att(DC - 2)
            gate_att(DC - 1)
            for m in range(DC):
                dve.wait_ge(s_q, m + 1)
                if m >= 2:
                    dve.wait_ge(s_m, m - 1)
                nc.vector.tensor_tensor(halves(tb[:, m % 2, :]), pb[:, m % 2, :, 0:HALF], halves(proj[:, ZB + m, :]),
                                        ALU.mult).then_inc(s_gb, 1)
                dve.wait_ge(s_gb, m + 1)
                dve.wait_ge(s_ga, m + 1)
                nc.vector.tensor_tensor(mix[:, m, :], mix[:, m, :], tb[:, m % 2, :], ALU.add).then_inc(s_m, 1)
            for m in range(DC):
                dve.wait_ge(s_o, m + 1)
                nc.vector.tensor_tensor(halves(x[:, m, :]), pa[:, m % 2, :, 0:HALF], halves(x[:, m, :]),
                                        ALU.add).then_inc(s_x, 1)
            dve.wait_ge(s_x, DC)


def queries(nc, I, c, xn, S, scratch):
    RING = 4
    NG = 2 * PH
    TT = NT + 1
    with ExitStack() as ctx:
        a = Alloc(nc, ctx)
        ring = a.sb("rt_ring", [P, RING, DC, P])
        sk = a.sb("rt_keys", [P, 2, P])
        q = scratch[:, 0:NG * N].rearrange("p (g n) -> p g n", g=NG)
        pq = a.ps("rt_ps_q", [P, 2, 2, 512])
        ps = a.ps("rt_ps_s", [P, 4, 512])
        s_k, s_p, s_c = a.sem("rt_keys_loaded"), a.sem("rt_product"), a.sem("rt_copied")
        s_s, s_sc = a.sem("rt_scores_made"), a.sem("rt_scores_copied")
        n0 = NG * N
        norm = Norm(nc, c, 1, "g_ffn", scratch[:, n0:n0 + DC * N].rearrange("p (k n) -> p k n", k=DC),
                    scratch[:, n0 + DC * N:n0 + (DC + 1) * N], ps[:, 0:2, 0:HALF])
        block = ctx.enter_context(nc.Block())

        @block.sync
        def _(sp):
            sp.dma_start(sk[:, :, :], I["subkeys"]).then_inc(s_k, 16)
            for n in range(NG):
                if n >= RING:
                    sp.wait_ge(s_p, n - RING + 1)
                sp.dma_start(ring[:, n % RING], I["w_q"][n]).then_inc(c.slots.sems[n % RING], 16)

        @block.tensor
        def _(pe):
            norm.sums(pe)
            for n in range(NG):
                pe.wait_ge(*c.slots.landed(n))
                if n >= 2:
                    pe.wait_ge(s_c, n - 1)
                for k in range(DC):
                    if n == 0:
                        pe.wait_ge(*norm.scaled(k))
                    for j in range(2):
                        last = nc.tensor.matmul(pq[:, n % 2, j, 0:HALF], ring[:, n % RING, k, :],
                                                xn[:, k, j * HALF:(j + 1) * HALF],
                                                start=(k == 0), stop=(k == DC - 1))
                last.then_inc(s_p, 1)
            pe.wait_ge(s_k, 16)
            pe.wait_ge(s_c, NG)
            for t in range(TT):
                m = P if t < NT else TS
                for g in range(NG):
                    if t >= 1 and g % 4 == 0:
                        pe.wait_ge(s_sc, (t - 1) * 4 + g // 4 + 1)
                    last = nc.tensor.matmul(ps[0:m, g // 4, (g % 4) * P:(g % 4 + 1) * P], q[:, g, t * P:t * P + m],
                                            sk[:, g % 2, :], start=True, stop=True)
                    if g % 4 == 3:
                        last.then_inc(s_s, 1)

        @block.vector
        def _(dve):
            norm.scale(dve)

        @block.scalar
        def _(act):
            norm.squares(act)
            for n in range(NG):
                act.wait_ge(s_p, n + 1)
                nc.scalar.activation(halves(q[:, n, :]), pq[:, n % 2, :, 0:HALF], ACT.Identity).then_inc(s_c, 1)
            for t in range(TT):
                m = P if t < NT else TS
                for k in range(4):
                    act.wait_ge(s_s, t * 4 + k + 1)
                    nc.scalar.copy(S[0:m, t, 4 * k:4 * k + 4, :].rearrange("p g k -> p (g k)"),
                                   ps[0:m, k, :]).then_inc(s_sc, 1)


def pick_and_expand(nc, I, c, xn, stage, A_dram, W_dram, gs):
    UR, GR = 4, 8
    NG = 2 * PH
    TT = NT + 1
    BODY = E1 // UR
    PLAIN, LATE = 11, 1
    NK = TP // GR
    WITH = NK // UR
    GB = P // GR
    with ExitStack() as ctx:
        a = Alloc(nc, ctx)
        u = a.sb("ex_u", [P, UR, DC, P])
        ge = a.sb("ex_gelu", [P, UR, N])
        B = a.sb("rw_b", [P, 2, GR // 2, P])
        A = a.sb("rw_a", [P, 2, GR // 2, P])
        iT = a.sb("rw_slots", [P, 3, N])
        S = stage[:, 1, 0:TT * NG * P].rearrange("p (t g k) -> p t g k", t=TT, g=NG)
        free = [0]

        def view(*shape):
            n = int(np.prod(shape))
            v = stage[:, 0, free[0]:free[0] + n]
            free[0] += n
            return v

        wk = view(2, P).rearrange("p (a k) -> p a k", a=2)
        v = view(NG, PK).rearrange("p (g k) -> p g k", g=NG)
        ix = view(NG, PK).bitcast(U32).rearrange("p (g k) -> p g k", g=NG)
        ixf = view(NG, PK).rearrange("p (g k) -> p g k", g=NG)
        cd = view(PH, PK, PK).rearrange("p (h a b) -> p h a b", h=PH, a=PK)
        cw = view(PK, PK)
        sv = view(PH, PK).rearrange("p (h k) -> p h k", h=PH)
        ci = view(PH, PK).bitcast(U32).rearrange("p (h k) -> p h k", h=PH)
        cb = view(2, PH, PK).bitcast(U32).rearrange("p (a h k) -> p a h k", a=2, h=PH)
        cf = view(2, PH, PK).rearrange("p (a h k) -> p a h k", a=2, h=PH)
        oh = view(SLOT, PK).rearrange("p (s k) -> p s k", k=PK)
        se = view(TT, 3, PH, PK).rearrange("p (t j h k) -> p t j h k", t=TT, j=3, h=PH)
        ex = view(TT, PH, PK).rearrange("p (t h k) -> p t h k", t=TT, h=PH)
        sm = view(TT, 2, PH).rearrange("p (t j h) -> p t j h", t=TT, j=2)
        assert free[0] <= P * P
        pu = a.ps("ex_ps_u", [P, 2, 2, 512])
        pw = a.ps("rw_ps", [P, 2, 2, 512])
        s_u = [a.sem(f"ex_u_loaded{r}") for r in range(UR)]
        s_as = [a.sem(f"ex_gelu_stored{r}") for r in range(UR)]
        s_ws = [a.sem(f"rw_stored{r}") for r in range(2)]
        s_pu, s_ge, s_v, s_e, s_ex, s_t, s_x, s_xc, s_b, s_pw, s_wc = (a.sem("ex_" + k) for k in (
            "u_product", "gelu", "pick_chain", "gates_shifted", "gates_exp", "slots_made", "slots_turned",
            "slots_copied", "onehot_made", "w_product", "w_copied"))
        block = ctx.enter_context(nc.Block())

        @block.gpsimd
        def _(pool):
            def load(dst, src, tile):
                pool.wait_ge(s_pu, tile)
                pool.dma_start(dst, src).then_inc(gs.s_first, 16)

            pool.wait_ge(s_ws[1], 16 * 2)
            load(gs.v[:, 0], gs.vsrc[0], E1 - 12)
            load(gs.v[:, 1], gs.vsrc[1], E1 - 9)
            pool.wait_ge(s_ws[0], 16 * 3)
            load(gs.w[:, 0], gs.wsrc[0], E1 - 7)
            for r in range(UR):
                pool.wait_ge(s_as[r], 16 * (gs.E // UR))
            load(gs.H0, gs.asrc[0], E1 - 5)
            load(gs.w[:, 1], gs.wsrc[1], E1 - 3)

        @block.sync
        def _(sp):
            def load(tile, r):
                sp.dma_start(u[:, r], I["uT"][tile]).then_inc(s_u[r], 16)

            def put(tile, r):
                dst = (A_dram[tile] if isinstance(tile, int) else
                       A_dram[bass.ds(tile, 1), :, :].rearrange("a p n -> p (a n)"))
                sp.dma_start(dst, ge[:, r, :]).then_inc(s_as[r], 16)

            for r in range(UR):
                load(r, r)
            with sp.Fori(1, BODY) as i:
                for r in range(UR):
                    sp.wait_ge(s_pu, i * UR + (r - UR + 1))
                    load(i * UR + r, r)
                    sp.wait_ge(s_ge, i * UR + (r - UR + 1))
                    put(i * UR + (r - UR), r)
            for r in range(UR):
                sp.wait_ge(s_ge, E1 - UR + r + 1)
                put(E1 - UR + r, r)
            for r in range(UR):
                sp.wait_ge(s_as[r], 16 * BODY)

        def staged(b):
            return stage[:, b % 2, :].rearrange("p (i n) -> p i n", n=P)

        @block.tensor
        def _(pe):
            def expand(tile, loaded, r, free):
                pe.wait_ge(s_u[r], loaded)
                if free is not None:
                    pe.wait_ge(s_ge, free)
                for j in range(2):
                    for k in range(DC):
                        last = nc.tensor.matmul(pu[:, r % 2, j, 0:HALF], u[:, r, k, :],
                                                xn[:, k, j * HALF:(j + 1) * HALF], start=(k == 0), stop=(k == DC - 1))
                last.then_inc(s_pu, 1)

            def weights(b, before, copied):
                if copied is not None:
                    pe.wait_ge(s_wc, copied)
                for q in range(2):
                    pe.wait_ge(s_b, before + (q + 1))
                    for g in range(GR // 2):
                        last = nc.tensor.matmul(pw[:, b, q, g * P:(g + 1) * P], B[:, q, g, :], A[:, q, g, :],
                                                start=True, stop=True)
                    last.then_inc(s_pw, 1)

            for r in range(UR):
                expand(r, 16, r, r - 1 if r >= 2 else None)
            with pe.Fori(1, PLAIN + LATE) as i:
                for r in range(UR):
                    expand(i * UR + r, i * 16 + 16, r, i * UR + (r - 1))
            for t in range(TT):
                m = P if t < NT else TS
                pe.wait_ge(s_t, t + 1)
                if t == NT:
                    pe.wait_ge(s_xc, 1)
                o = pw[:, t // 2, t % 2, 0:3 * P] if t < NT else pw[:, 0, 0, 3 * P:3 * P + 3 * TS]
                for j in range(3):
                    last = nc.tensor.transpose(o[:, j * m:(j + 1) * m], se[0:m, t, j].rearrange("p h k -> p (h k)"),
                                               c.ident[0:m, 0:m])
                last.then_inc(s_x, 1)
            pe.wait_ge(s_xc, TT)
            first = (PLAIN + LATE) * UR
            for r in range(UR):
                expand(first + r, (PLAIN + LATE + 1) * 16, r, first + r - 1)
                weights(r % 2, 2 * r, 2 * (r - 1) if r >= 2 else None)
            with pe.Fori(1, WITH) as i:
                for r in range(UR):
                    expand(None, i * 16 + (PLAIN + LATE + 1) * 16, r, i * UR + (first + r - 1))
                    weights(r % 2, i * (2 * UR) + 2 * r, i * (2 * UR) + 2 * (r - 1))
            weights(0, 2 * NK, 2 * (NK - 1))
            with pe.Fori(PLAIN + LATE + WITH, BODY) as i:
                for r in range(UR):
                    expand(i * UR + r, i * 16 + 16, r, i * UR + (r - 1))

        @block.scalar
        def _(act):
            def gelu(made, r, stored):
                act.wait_ge(s_pu, made)
                if stored is not None:
                    act.wait_ge(s_as[r], stored)
                nc.scalar.activation(halves(ge[:, r, :]), pu[:, r % 2, :, 0:HALF], ACT.Gelu).then_inc(s_ge, 1)

            def stage_group(b, before, r, n0):
                for q in range(2):
                    act.wait_ge(s_pw, before + (q + 1))
                    nc.scalar.copy(staged(b)[:, :, bass.ds(n0 + 4 * q, 4) if not isinstance(n0, int) else
                                             slice(n0 + 4 * q, n0 + 4 * q + 4)],
                                   pw[:, r % 2, q, :].rearrange("p (n i) -> p i n", n=4)).then_inc(s_wc, 1)

            def put_block(b, m):
                act.wait_ge(s_wc, 2 * min((b + 1) * GB, NK + 1))
                act.dma_start(W_dram[:, :, b * P:b * P + m].rearrange("i p n -> p i n"),
                              staged(b)[:, :, 0:m]).then_inc(s_ws[b % 2], 16)

            for r in range(UR):
                gelu(r + 1, r, None)
            with act.Fori(1, PLAIN) as i:
                for r in range(UR):
                    gelu(i * UR + (r + 1), r, i * 16)
            act.wait_ge(s_e, TT)
            for t in range(TT):
                m = P if t < NT else TS
                nc.scalar.activation(ex[0:m, t], se[0:m, t, 2], ACT.Exp).then_inc(s_ex, 1)
            with act.Fori(PLAIN, PLAIN + LATE) as i:
                for r in range(UR):
                    gelu(i * UR + (r + 1), r, i * 16)
            act.wait_ge(s_xc, TT)
            i0 = PLAIN + LATE
            for b in range(NT):
                if b >= 2:
                    act.wait_ge(s_ws[b % 2], 16)
                per = GB // UR
                with act.Fori(0, per) as i:
                    for r in range(UR):
                        gelu(i * UR + ((i0 + b * per) * UR + r + 1), r, i * 16 + (i0 + b * per) * 16)
                        stage_group(b, i * (2 * UR) + 2 * (b * GB + r), r, i * (UR * GR) + r * GR)
                put_block(b, P)
            act.wait_ge(s_ws[0], 32)
            stage_group(NT, 2 * NK, 0, 0)
            put_block(NT, TS)
            with act.Fori(PLAIN + LATE + WITH, BODY) as i:
                for r in range(UR):
                    gelu(i * UR + (r + 1), r, i * 16)

        @block.vector
        def _(dve):
            link = Chain(dve, s_v)
            for t in range(TT):
                m = P if t < NT else TS
                for g in range(NG):
                    s = S[0:m, t, g, :]
                    w = wk[0:m, g % 2, :]
                    link(nc.vector.max(v[0:m, g, 0:8], s))
                    nc.vector.max_index(ix[0:m, g, 0:8], v[0:m, g, 0:8], s)
                    link(nc.vector.match_replace(w, v[0:m, g, 0:8], s, SENT))
                    link(nc.vector.max(v[0:m, g, 8:16], w))
                    link(nc.vector.max_index(ix[0:m, g, 8:16], v[0:m, g, 8:16], w))
                vv = v[0:m].rearrange("p (h a) k -> p h a k", a=2)
                link(nc.vector.tensor_tensor(cd[0:m], vv[:, :, 0, :].unsqueeze(3).to_broadcast([m, PH, PK, PK]),
                                             vv[:, :, 1, :].unsqueeze(2).to_broadcast([m, PH, PK, PK]), ALU.add))
                for h in range(PH):
                    s = cd[0:m, h].rearrange("p a b -> p (a b)")
                    w = cw[0:m, :]
                    link(nc.vector.max(sv[0:m, h, 0:8], s))
                    nc.vector.max_index(ci[0:m, h, 0:8], sv[0:m, h, 0:8], s)
                    link(nc.vector.match_replace(w, sv[0:m, h, 0:8], s, SENT))
                    link(nc.vector.max(sv[0:m, h, 8:16], w))
                    link(nc.vector.max_index(ci[0:m, h, 8:16], sv[0:m, h, 8:16], w))
                nc.vector.tensor_tensor(se[0:m, t, 2], sv[0:m], sv[0:m, :, 0:1].to_broadcast([m, PH, PK]),
                                        ALU.subtract).then_inc(s_e, 1)
                nc.vector.tensor_scalar(cb[0:m, 0], ci[0:m], 4, None, ALU.logical_shift_right)
                link(nc.vector.tensor_scalar(cb[0:m, 1], ci[0:m], PK - 1, None, ALU.bitwise_and))
                nc.vector.tensor_copy(cf[0:m], cb[0:m])
                link(nc.vector.tensor_copy(ixf[0:m], ix[0:m]))
                iv = ixf[0:m].rearrange("p (h a) k -> p h a k", a=2)
                o3 = oh[0:m]
                o4 = oh[0:m].rearrange("p (h s) k -> p h s k", h=PH)
                for j in range(2):
                    part = cf[0:m, j].rearrange("p h k -> p (h k)").unsqueeze(2).to_broadcast([m, SLOT, PK])
                    link(nc.vector.tensor_tensor(o3, part, c.iota[0:m, 0:PK].unsqueeze(1).to_broadcast(
                        [m, SLOT, PK]), ALU.is_equal))
                    link(nc.vector.tensor_tensor(o4, o4, iv[:, :, j, :].unsqueeze(2).to_broadcast(
                        [m, PH, PK, PK]), ALU.mult))
                    link(nc.vector.tensor_reduce(se[0:m, t, j].rearrange("p h k -> p (h k)"), o3, X, ALU.add))
            for t in range(TT):
                m = P if t < NT else TS
                dve.wait_ge(s_ex, t + 1)
                link(nc.vector.tensor_reduce(sm[0:m, t, 0], ex[0:m, t], X, ALU.add))
                link(nc.vector.reciprocal(sm[0:m, t, 1], sm[0:m, t, 0]))
                nc.vector.tensor_tensor(se[0:m, t, 2], ex[0:m, t], sm[0:m, t, 1].unsqueeze(2).to_broadcast(
                    [m, PH, PK]), ALU.mult).then_inc(s_t, 1)
            for t in range(TT):
                m = P if t < NT else TS
                dve.wait_ge(s_x, t + 1)
                o = pw[:, t // 2, t % 2, 0:3 * P] if t < NT else pw[:, 0, 0, 3 * P:3 * P + 3 * TS]
                nc.vector.tensor_copy(iT[:, :, t * P:t * P + m], o.rearrange("p (j n) -> p j n", j=3)).then_inc(s_xc, 1)
            dve.wait_ge(s_xc, TT)

            def rows(n, q, used):
                if used is not None:
                    dve.wait_ge(s_pw, used)
                for g in range(GR // 2):
                    at = slice(n + g, n + g + 1) if isinstance(n, int) else bass.ds(n + g, 1)
                    nc.vector.tensor_scalar(B[:, q, g, :], c.iota[:, :], iT[:, 1, at], None, ALU.is_equal)
                    last = nc.vector.tensor_scalar(A[:, q, g, :], c.iota[:, :], iT[:, 0, at], iT[:, 2, at],
                                                   ALU.is_equal, ALU.mult)
                last.then_inc(s_b, 1)

            for q in range(2):
                rows(q * (GR // 2), q, None)
            with dve.Fori(1, NK) as i:
                for q in range(2):
                    rows(i * GR + q * (GR // 2), q, i * 2 + (q - 1))
            for q in range(2):
                rows(TP + q * (GR // 2), q, 2 * NK + q - 1)


class Gather:
    E = 8

    def __init__(self, a, I, stage, A_dram, W_dram):
        E = self.E
        n = E * N
        self.v = stage[:, 1, :].rearrange("p (b e d) -> p b e d", b=2, e=E)
        self.w = stage[:, 0, 0:2 * n].rearrange("p (b e n) -> p b e n", b=2, e=E)
        self.H0 = stage[:, 0, 2 * n:3 * n].rearrange("p (e n) -> p e n", e=E)
        self.s_v, self.s_w, self.s_a = ([a.sem(f"ev_{k}_loaded{b}") for b in range(2)] for k in ("v", "w", "a"))
        self.s_first = a.sem("ev_first_loaded")
        self.vsrc = I["v"].rearrange("(g e p) d -> g p e d", p=P, e=E)
        self.asrc = A_dram.rearrange("(g e) p n -> g p e n", e=E)
        self.wsrc = W_dram.rearrange("(g e) p n -> g p e n", e=E)


def gather_experts(nc, gs, x):
    E = gs.E
    NG = E1 // E
    with ExitStack() as ctx:
        a = Alloc(nc, ctx)
        v, w = gs.v, gs.w
        s_v, s_w, s_a = gs.s_v, gs.s_w, gs.s_a
        H = [gs.H0, a.sb("ev_h1", [P, E, N])]
        pv = a.ps("ev_ps", [P, 4, 2, 512])
        s_h, s_pv, s_ac = (a.sem("ev_" + k) for k in ("hidden", "product", "added"))
        block = ctx.enter_context(nc.Block())

        def pick(src, g):
            return src[bass.ds(g, 1)].rearrange("g p e d -> p (g e) d")

        @block.sync
        def _(sp):
            sp.dma_start(H[1][:, :, :], gs.asrc[1]).then_inc(s_a[1], 16)
            with sp.Fori(1, NG // 2) as i:
                for b in range(2):
                    sp.wait_ge(s_pv, i * (2 * DC) + (b - 1) * DC)
                    sp.dma_start(H[b][:, :, :], pick(gs.asrc, i * 2 + b)).then_inc(s_a[b], 16)
                    sp.dma_start(v[:, b], pick(gs.vsrc, i * 2 + b)).then_inc(s_v[b], 16)

        @block.scalar
        def _(act):
            with act.Fori(1, NG // 2) as i:
                for b in range(2):
                    act.wait_ge(s_h, i * (2 * E) + (b - 1) * E)
                    act.dma_start(w[:, b], pick(gs.wsrc, i * 2 + b)).then_inc(s_w[b], 16)

        @block.vector
        def _(dve):
            def hide(b, loaded):
                if loaded is not None:
                    dve.wait_ge(s_w[b], loaded)
                if b == 0 and loaded is not None:
                    dve.wait_ge(s_a[0], loaded)
                if b == 1:
                    dve.wait_ge(s_a[1], 16 if loaded is None else loaded + 16)
                for e in range(E):
                    nc.vector.tensor_tensor(H[b][:, e, :], H[b][:, e, :], w[:, b, e, :], ALU.mult).then_inc(s_h, 1)

            def add(m, made, before):
                dve.wait_ge(s_pv, made)
                if before is not None:
                    dve.wait_ge(s_ac, before)
                nc.vector.tensor_tensor(halves(x[:, m, :]), pv[:, m % 4, :, 0:HALF], halves(x[:, m, :]),
                                        ALU.add).then_inc(s_ac, 1)

            dve.wait_ge(gs.s_first, 16 * 5)
            hide(0, None)
            hide(1, None)
            for m in range(DC):
                add(m, m + 1, None)
            with dve.Fori(1, NG // 2) as i:
                for b in range(2):
                    hide(b, i * 16)
                    for m in range(DC):
                        add(m, i * (2 * DC) + ((b - 1) * DC + m + 1), i * (2 * DC) + ((b - 2) * DC + m + 1))
            for m in range(DC):
                add(m, (NG - 1) * DC + m + 1, (NG - 2) * DC + m + 1)
            dve.wait_ge(s_ac, NG * DC)

        @block.tensor
        def _(pe):
            def group(b, loaded, hidden, free):
                if loaded is not None:
                    pe.wait_ge(s_v[b], loaded)
                pe.wait_ge(s_h, hidden)
                for m in range(DC):
                    f = free(m)
                    if f is not None:
                        pe.wait_ge(s_ac, f)
                    for j in range(2):
                        for e in range(E):
                            last = nc.tensor.matmul(pv[:, m % 4, j, 0:HALF], v[:, b, e, m * P:(m + 1) * P],
                                                    H[b][:, e, j * HALF:(j + 1) * HALF],
                                                    start=(e == 0), stop=(e == E - 1))
                    last.then_inc(s_pv, 1)

            pe.wait_ge(gs.s_first, 16 * 5)
            group(0, None, E, lambda m: m - 3 if m >= 4 else None)
            group(1, None, 2 * E, lambda m: DC + m - 3)
            with pe.Fori(1, NG // 2) as i:
                for b in range(2):
                    group(b, i * 16, i * (2 * E) + (b + 1) * E, lambda m: i * (2 * DC) + (b * DC + m - 3))


def per_layer_input(nc, I, c, xn, x):
    RING = 4
    PC = 2
    with ExitStack() as ctx:
        a = Alloc(nc, ctx)
        ring = a.sb("pl_ring", [P, RING, DC + PC, P])
        pT = a.sb("pl_p", [P, PC, N])
        sg = a.sb("pl_sig", [P, 2, N])
        gd = a.sb("pl_gated", [P, 2, N])
        pa = a.ps("pl_ps_a", [P, 2, 2, 512])
        pb = a.ps("pl_ps_b", [P, 2, 2, 512])
        norm = Norm(nc, c, 2, "g_ple", a.sb("pl_sq", [P, DC, N]), a.sb("pl_root", [P, N])[:, :], pa[:, 0, :, 0:HALF])
        s_i, s_p, s_s, s_g, s_x = (a.sem("pl_" + k) for k in ("p_loaded", "products", "sigmoid", "gated", "added"))
        block = ctx.enter_context(nc.Block())

        @block.sync
        def _(sp):
            sp.dma_start(pT[:, :, :], I["pT"]).then_inc(s_i, 16)
            for n in range(DC):
                if n >= RING:
                    sp.wait_ge(s_p, n - RING + 1)
                sp.dma_start(ring[:, n % RING], I["w_gp"][n]).then_inc(c.slots.sems[n % RING], 16)

        @block.tensor
        def _(pe):
            norm.sums(pe)
            pe.wait_ge(s_i, 16)
            for n in range(DC):
                pe.wait_ge(*c.slots.landed(n))
                if n >= 2:
                    pe.wait_ge(s_g, n - 1)
                for ps, src, k0, kn in ((pb, pT, DC, PC), (pa, xn, 0, DC)):
                    for k in range(kn):
                        if n == 0 and ps is pa:
                            pe.wait_ge(*norm.scaled(k))
                        for j in range(2):
                            last = nc.tensor.matmul(ps[:, n % 2, j, 0:HALF], ring[:, n % RING, k0 + k, :],
                                                    src[:, k, j * HALF:(j + 1) * HALF],
                                                    start=(k == 0), stop=(k == kn - 1))
                last.then_inc(s_p, 1)

        @block.scalar
        def _(act):
            norm.squares(act)
            for n in range(DC):
                act.wait_ge(s_p, n + 1)
                if n >= 2:
                    act.wait_ge(s_g, n - 1)
                nc.scalar.activation(halves(sg[:, n % 2, :]), pa[:, n % 2, :, 0:HALF], ACT.Sigmoid).then_inc(s_s, 1)

        @block.vector
        def _(dve):
            norm.scale(dve)
            for n in range(DC):
                dve.wait_ge(s_s, n + 1)
                if n >= 2:
                    dve.wait_ge(s_x, n - 1)
                nc.vector.tensor_tensor(halves(gd[:, n % 2, :]), pb[:, n % 2, :, 0:HALF], halves(sg[:, n % 2, :]),
                                        ALU.mult).then_inc(s_g, 1)
                dve.wait_ge(s_g, n + 1)
                nc.vector.tensor_tensor(x[:, n, :], x[:, n, :], gd[:, n % 2, :], ALU.add).then_inc(s_x, 1)
            dve.wait_ge(s_x, DC)


def final_norm(nc, c, dst):
    with ExitStack() as ctx:
        a = Alloc(nc, ctx)
        norm = Norm(nc, c, 3, "g_final", a.sb("fin_sq", [P, DC, N]), a.sb("fin_root", [P, N])[:, :],
                    a.ps("fin_sum", [P, 2, 512])[:, :, 0:HALF])
        s_o = a.sem("y_stored")
        block = ctx.enter_context(nc.Block())

        @block.scalar
        def _(act):
            norm.squares(act)

        @block.tensor
        def _(pe):
            norm.sums(pe)

        @block.vector
        def _(dve):
            norm.scale(dve)

        @block.sync
        def _(sp):
            for k in range(0, DC, 2):
                sp.wait_ge(*norm.scaled(k + 1))
                sp.dma_start(dst[:, k:k + 2, :], c.h[:, k:k + 2, :]).then_inc(s_o, 16)
            sp.wait_ge(s_o, 16 * DC // 2)


class Tiles:
    pass


def build(nc, I, O, scratch):
    with ExitStack() as ctx:
        a = Alloc(nc, ctx)
        c = Tiles()
        c.ones, c.ident, c.iota = (a.sb(k, [P, P]) for k in ("ones", "ident", "iota"))
        c.sel_b, c.sel_h = a.sb("sel_b", [TS, TS, NH]), a.sb("sel_h", [TS, TS, NH])
        c.selT = a.sb("selT", [TS * NH, TS])
        c.rb = a.sb("rb", [NB + 1, NH])
        c.eps = a.sb("eps", [P, 1])
        c.slots = Slots(a, 4)
        c.norm_sems = NormSems(a)
        c.x_loaded = a.sem("x_loaded")
        c.x = a.sb("x", [P, DC, N])
        c.small = {k: a.sb("c_" + k, s) for k, s in (("g_mix", [P, DC]), ("g_ffn", [P, DC]), ("g_ple", [P, DC]),
                                                     ("g_final", [P, DC]), ("g_hgrn", [P, 1]), ("lbl", [P, 2, HG]))}
        c.small["pages"] = a.sb("c_pages", [1, TS * NPG], I32)
        x = c.x
        h = c.h = a.sb("h", [P, DC, N])
        with ExitStack() as mid:
            b = Alloc(nc, mid)
            c.causal, c.tri = (b.sb(k, [P, P]) for k in ("causal", "tri"))
            c.reset = b.sb("reset", [P, TP])
            c.pick = b.sb("pick", [TS, TS, P])
            constants(nc, a, I, c)
            c.n_phys = I["kidxT"].shape[0]
            proj = b.sb("proj", [P, MT, N])
            vtok = b.sb("vtok", [P, NT + 1, P])
            hitok = b.sb("hitok", [P, NT + 1, 512])
            iwtok = b.sb("iwtok", [P, NT + 1, NH])
            ikT = b.sb("ikT", [P, N])
            attT, hgoT = b.sb("attT", [P, 4, N]), h[:, 4:8, :]
            work = b.sb("work", [P, HG * (2 * TP + N)])
            dec = Decays(nc, b, c, h, proj, work)
            with ExitStack() as att:
                d = Alloc(nc, att)
                rev = d.sb("rev", [NH, REV])
                maskS = d.sb("maskS", [TS, L])
                project_first(nc, I, O, c, h, proj, ikT, vtok, hitok, iwtok, rev, scratch["rev"], work)
                c.slots.stage_ends(HQ)
                with ExitStack() as pro:
                    maskp = Alloc(nc, pro).sb("maskp", [P, NT, TP])
                    index_keys(nc, I, c, h, proj, ikT, iwtok, maskp, maskS, work)
                    c.slots.stage_ends(ZA - HQ)
                    attend_prompt(nc, I, c, h, proj, vtok, maskp, maskS, scratch["rev"], attT, work)
                    c.slots.stage_ends(MT - ZA)
                sample_attention(nc, I, c, proj, vtok, rev, maskS, attT, hgoT, dec)
            hgrn(nc, I, O, c, dec, proj, hitok, hgoT)
            merge(nc, I, c, proj, attT, hgoT, dec, x)
            c.slots.stage_ends(DC)
        with ExitStack() as mid:
            stage = Alloc(nc, mid).sb("stage", [P, 2, P * P])
            S = stage[:, 1, 0:(NT + 1) * 2 * PH * P].rearrange("p (t g k) -> p t g k", t=NT + 1, g=2 * PH)
            queries(nc, I, c, h, S, stage[:, 0, :])
            c.slots.stage_ends(2 * PH)
            gs = Gather(a, I, stage, scratch["A"], scratch["W"])
            pick_and_expand(nc, I, c, h, stage, scratch["A"], scratch["W"], gs)
            gather_experts(nc, gs, x)
        per_layer_input(nc, I, c, h, x)
        final_norm(nc, c, O["yT"])


def bucket_onehot():
    dist = PAST - np.arange(REV)
    n = np.maximum(dist, 0)
    nf = np.maximum(n, 1).astype(np.float32)
    large = 16 + (np.log(nf / np.float32(16)) / np.float32(math.log(128 / 16)) * np.float32(16)).astype(np.int32)
    b = np.where(n < 16, n, np.minimum(large, NB - 1))
    b = np.where(dist < 0, NB, b)
    out = np.zeros((NB + 1, REV), np.float32)
    out[b, np.arange(REV)] = 1.0
    return out


def kernel(**inputs):
    import concourse.bacc as bacc
    from concourse.bass_utils import run_bass_kernel_spmd

    g = {k: np.asarray(v) for k, v in inputs.items()}

    def tiles(w):
        k, m = w.shape
        return np.ascontiguousarray(w.reshape(k // P, P, m // P, P).transpose(2, 1, 0, 3))

    def cols(v):
        return np.ascontiguousarray(v.reshape(-1, P).T)

    w_in = g["w_in"][0]
    o = np.cumsum([0, 512, 128, 128, 512, 64, 8, 512, 512, 512, 512, 1024, 1024]).tolist()
    aq, ak, av, iq, ik, iw, hq, hf, hi, hg, za, zb = (w_in[:, o[i]:o[i + 1]] for i in range(12))
    order = [x for m in range(4) for x in (m, m + 4)]
    aq = aq.reshape(D, NH, HD)[:, order].reshape(D, 512)
    w_a = g["w_branch_a"][0].reshape(NH, HD, D)[order].reshape(512, D)
    xT = np.concatenate([g["x_prompt"][0], g["x_sample"][:, 0]]).T
    pT = np.concatenate([g["p_prompt"][0, 0], g["p_sample"][0, :, 0]]).T
    arrays = {
        "xT": xT.reshape(DC, P, N).transpose(1, 0, 2),
        "pT": pT.reshape(2, P, N).transpose(1, 0, 2),
        "w_t": tiles(np.concatenate([aq, ak, iq, hq, hg, hf, za, zb], axis=1)),
        "w_ik": ik.reshape(DC, P, HD).transpose(1, 0, 2),
        "w_tok": np.concatenate([av, hi, iw], axis=1).reshape(DC, P, 648).transpose(1, 0, 2),
        "w_ab": np.concatenate([tiles(w_a), tiles(g["w_branch_b"][0])], axis=2),
        "w_out": tiles(g["w_out"][0]),
        "w_q": tiles(g["peer_wq"][0]),
        "w_gp": np.concatenate([tiles(g["w_ple_gate"][0]), tiles(g["w_ple_proj"][0])], axis=2),
        "subkeys": g["peer_subkeys"][0].transpose(2, 0, 1),
        "uT": tiles(g["peer_u"][0].T),
        "v": g["peer_v"][0],
        "g_mix": cols(g["g_mix"][0]), "g_ffn": cols(g["g_ffn"][0]), "g_ple": cols(g["g_ple"][0]),
        "g_final": cols(g["g_final"]), "g_hgrn": cols(g["g_hgrn"][0]),
        "lbl": g["lb_logits"].reshape(2, HG, P).transpose(2, 0, 1),
        "rel_bias": g["rel_bias"],
        "onehot": bucket_onehot(),
        "pages": g["page_table"].reshape(1, -1),
        "kidxT": g["cache_kidx"][0].transpose(0, 2, 1),
        "kT": g["cache_k"][0].reshape(-1, PG, P).transpose(0, 2, 1),
        "vC": g["cache_v"][0].reshape(-1, PG, P),
        "state": g["state_hgrn"][0].transpose(2, 0, 1, 3),
    }
    nc = bacc.Bacc("TRN2", target_bir_lowering=False, num_devices=1)
    I, sent = {}, {}
    for name, arr in arrays.items():
        arr = np.ascontiguousarray(arr)
        sent["in_" + name] = arr
        I[name] = nc.dram_tensor("in_" + name, arr.shape, mybir.dt.from_np(arr.dtype), kind="ExternalInput").ap()
    shapes = {"yT": [P, DC, N], "kT": [P, N], "v_p": [TP, P], "v_s": [TS, P], "ikT": [HD, N],
              "hg_p": [P, HG, P], "hg_s": [P, TS, HG, P]}
    O = {k: nc.dram_tensor("out_" + k, s, F32, kind="ExternalOutput").ap() for k, s in shapes.items()}
    scratch = {"rev": nc.dram_tensor("scratch_rev", [NH, P, SK], F32).ap(),
               "A": nc.dram_tensor("scratch_a", [E1, P, N], F32).ap(),
               "W": nc.dram_tensor("scratch_w", [E1, P, N], F32).ap()}
    build(nc, I, O, scratch)
    r = run_bass_kernel_spmd(nc, [sent], core_ids=[0]).results[0]
    got = {k: r["out_" + k] for k in shapes}
    y = got["yT"].transpose(2, 1, 0).reshape(N, D)
    k = got["kT"].T.reshape(N, 2, HD)
    kidx = got["ikT"].T
    return (y[None, :TP], y[TP:, None],
            k[None, None, :TP], got["v_p"].reshape(1, 1, TP, 2, HD), kidx[None, None, :TP],
            got["hg_p"].transpose(1, 0, 2)[None, None],
            k[TP:][None, :, None], got["v_s"].reshape(1, TS, 1, 2, HD), kidx[TP:][None, :, None],
            got["hg_s"].transpose(1, 2, 0, 3)[None])
```
